# Optimizing a Trainium2 kernel written in Bass

```python
import math
import jax
import jax.numpy as jnp
from jax import lax
import numpy as np

D_MODEL = 1024
BATCH = 1
SEQ = 256
DEPTH = 2
DEC_BATCH = 8
DEC_SEQ = 1
PAST_LEN = 1024
PAGE_SIZE = 128

N_EVEN = (DEPTH + 1) // 2
N_ODD = DEPTH // 2
H_A = 8
HD_A = 64
GDN_CONV = 4
GDN_CHUNK = 64
H_B = 8
DK_B = 64
DV_B = 64
HGRN_CHUNK = 32
H_C = 8
HD_C = 64
MOBA_BLOCK = 256
MOBA_TOPK = 3
MOBA_QBLOCK = 64
N_BUCKETS = 32
MAX_DISTANCE = 128
S5_GROUPS = 32
S5_GROUP_CH = 16
S5_STATE = 64
N_MEM = 256
MEM_H = 4
MEM_HD = 128
D_FF = 2816
FFN_CONV = 3
EPS = 1e-6
EV_IN = 4 * H_A * HD_A + 2 * H_A + H_B * (2 * DK_B + 2 * DV_B)
OD_IN = 3 * H_C * HD_C + S5_GROUPS * S5_GROUP_CH
EV_OUT = H_A * HD_A + H_B * DV_B
OD_OUT = H_C * HD_C + S5_GROUPS * S5_GROUP_CH

kernel_name = 'hybrid_gdn_hgrn2_moba_s5_decoder_step'

def _split(x, sizes):
    out, off = [], 0
    for s in sizes:
        out.append(x[..., off:off + s])
        off += s
    return out

def rmsnorm(x, g):
    xf = x.astype(jnp.float32)
    y = xf * lax.rsqrt(jnp.mean(xf * xf, axis=-1, keepdims=True) + EPS)
    return (y * g.astype(jnp.float32)).astype(x.dtype)

def l2norm(x):
    xf = x.astype(jnp.float32)
    return xf * lax.rsqrt(jnp.sum(xf * xf, axis=-1, keepdims=True) + EPS)

def causal_dwconv(x, buf, w):
    xp = jnp.concatenate([buf.astype(x.dtype), x], axis=1)
    y = lax.conv_general_dilated(xp, w[:, None, :].astype(x.dtype), window_strides=(1,), padding='VALID',
                                 dimension_numbers=('NWC', 'WIO', 'NWC'), feature_group_count=x.shape[-1])
    return y, xp[:, xp.shape[1] - (w.shape[0] - 1):]

def rel_bucket(dist):
    n = jnp.maximum(dist, 0)
    exact = N_BUCKETS // 2
    nf = jnp.maximum(n, exact).astype(jnp.float32)
    large = exact + (jnp.log(nf / exact) / math.log(MAX_DISTANCE / exact) * (N_BUCKETS - exact)).astype(jnp.int32)
    return jnp.where(n < exact, n, jnp.minimum(large, N_BUCKETS - 1))

def _pad_time(t, pad):
    return jnp.pad(t, [(0, 0), (0, pad)] + [(0, 0)] * (t.ndim - 2))

def _chunks(t, n, c):
    t = t.reshape(t.shape[0], n, c, *t.shape[2:])
    return jnp.moveaxis(t, (1, 2), (0, 3))

def _unchunk(o, L):
    n, B, H, c, d = o.shape
    return jnp.moveaxis(o, (0, 3), (1, 2)).reshape(B, n * c, H, d)[:, :L]

def gated_delta_rule(q, k, v, beta, g, S0):
    B, L, H, dk = q.shape
    dv = v.shape[-1]
    c = min(GDN_CHUNK, L)
    n = -(-L // c)
    pad = n * c - L
    q, k, v, beta, g = [_chunks(_pad_time(t.astype(jnp.float32), pad), n, c) for t in (q, k, v, beta, g)]
    G = jnp.cumsum(g, axis=-1)
    causal = jnp.tril(jnp.ones((c, c), bool))
    decay = jnp.exp(jnp.where(causal, G[..., :, None] - G[..., None, :], -jnp.inf))
    A = beta[..., :, None] * jnp.einsum('nbhid,nbhjd->nbhij', k, k) * decay
    A = jnp.where(jnp.tril(jnp.ones((c, c), bool), -1), A, 0.0)
    rhs = jnp.concatenate([beta[..., None] * v, (beta * jnp.exp(G))[..., None] * k], axis=-1)
    sol = lax.linalg.triangular_solve(A, rhs, left_side=True, lower=True, unit_diagonal=True)
    u_v, w = sol[..., :dv], sol[..., dv:]
    qk = jnp.einsum('nbhid,nbhjd->nbhij', q, k) * decay
    q_in = q * jnp.exp(G)[..., None]
    k_out = k * jnp.exp(G[..., -1:] - G)[..., None]
    g_last = jnp.exp(G[..., -1])

    def step(S, xs):
        u_v_c, w_c, qk_c, q_c, k_c, gl = xs
        u = u_v_c - jnp.einsum('bhck,bhkv->bhcv', w_c, S)
        o = jnp.einsum('bhck,bhkv->bhcv', q_c, S) + jnp.einsum('bhij,bhjv->bhiv', qk_c, u)
        S = S * gl[..., None, None] + jnp.einsum('bhck,bhcv->bhkv', k_c, u)
        return S, o

    S, o = lax.scan(step, S0.astype(jnp.float32), (u_v, w, qk, q_in, k_out, g_last))
    return _unchunk(o, L), S

def hgrn2_recurrence(q, k, logf, v, S0):
    B, L, H, dk = q.shape
    c = min(HGRN_CHUNK, L)
    n = -(-L // c)
    pad = n * c - L
    q, k, logf, v = [_chunks(_pad_time(t.astype(jnp.float32), pad), n, c) for t in (q, k, logf, v)]
    Bc = jnp.cumsum(logf, axis=-2)
    r = (c - 1) // 2
    ref = Bc[..., r:r + 1, :]
    att = jnp.einsum('nbhid,nbhjd->nbhij', q * jnp.exp(Bc - ref), k * jnp.exp(ref - Bc))
    att = jnp.where(jnp.tril(jnp.ones((c, c), bool)), att, 0.0)
    o_intra = jnp.einsum('nbhij,nbhjv->nbhiv', att, v)
    q_in = q * jnp.exp(Bc)
    k_out = k * jnp.exp(Bc[..., -1:, :] - Bc)
    f_last = jnp.exp(Bc[..., -1, :])

    def step(S, xs):
        q_c, k_c, v_c, fl, oi = xs
        o = oi + jnp.einsum('bhck,bhkv->bhcv', q_c, S)
        S = S * fl[..., None] + jnp.einsum('bhck,bhcv->bhkv', k_c, v_c)
        return S, o

    S, o = lax.scan(step, S0.astype(jnp.float32), (q_in, k_out, v, f_last, o_intra))
    return _unchunk(o, L), S

def _cplx_combine(e1, e2):
    a1r, a1i, b1r, b1i = e1
    a2r, a2i, b2r, b2i = e2
    return (a2r * a1r - a2i * a1i, a2r * a1i + a2i * a1r,
            a2r * b1r - a2i * b1i + b2r, a2r * b1i + a2i * b1r + b2i)

def s5_scan(u, h0_re, h0_im, A_re, A_im, log_dt, B_re, B_im, C_re, C_im, D):
    dt = jnp.exp(log_dt.astype(jnp.float32))[:, None]
    lr, li = A_re.astype(jnp.float32), A_im.astype(jnp.float32)
    mag = jnp.exp(lr * dt)
    ar, ai = mag * jnp.cos(li * dt), mag * jnp.sin(li * dt)
    den = lr * lr + li * li
    nr = ar - 1.0
    cr, ci = (nr * lr + ai * li) / den, (ai * lr - nr * li) / den
    Br, Bi = B_re.astype(jnp.float32), B_im.astype(jnp.float32)
    bbr = cr[..., None] * Br - ci[..., None] * Bi
    bbi = cr[..., None] * Bi + ci[..., None] * Br
    xr = jnp.einsum('blgn,gpn->blgp', u, bbr)
    xi = jnp.einsum('blgn,gpn->blgp', u, bbi)
    h0r, h0i = h0_re.astype(jnp.float32), h0_im.astype(jnp.float32)
    xr = xr.at[:, 0].add(ar * h0r - ai * h0i)
    xi = xi.at[:, 0].add(ar * h0i + ai * h0r)
    _, _, hr, hi = lax.associative_scan(_cplx_combine, (jnp.broadcast_to(ar, xr.shape), jnp.broadcast_to(ai, xr.shape), xr, xi), axis=1)
    y = (jnp.einsum('blgp,gnp->blgn', hr, C_re.astype(jnp.float32))
         - jnp.einsum('blgp,gnp->blgn', hi, C_im.astype(jnp.float32)) + D.astype(jnp.float32) * u)
    return y, hr[:, -1], hi[:, -1]

def moba_attend(q, k_all, v_all, pos0, rel_bias):
    B, L, H, hd = q.shape
    T = k_all.shape[1]
    nb = -(-T // MOBA_BLOCK)
    padT = nb * MOBA_BLOCK - T

    def blocks(t):
        return jnp.pad(t, ((0, 0), (0, padT), (0, 0), (0, 0))).reshape(B, nb, MOBA_BLOCK, H, hd).transpose(0, 3, 1, 2, 4)

    kb, vb = blocks(k_all), blocks(v_all)
    kmean = jnp.mean(kb.astype(jnp.float32), axis=3)
    qpos = pos0 + jnp.arange(L, dtype=jnp.int32)
    qblk = qpos // MOBA_BLOCK
    gate = jnp.einsum('blhd,bhnd->bhln', q.astype(jnp.float32), kmean)
    gate = jnp.where(jnp.arange(nb)[None, :] < qblk[:, None], gate, -jnp.inf)
    if nb < MOBA_TOPK:
        gate = jnp.pad(gate, ((0, 0), (0, 0), (0, 0), (0, MOBA_TOPK - nb)), constant_values=-jnp.inf)
    top_s, top_i = lax.top_k(gate, MOBA_TOPK)
    n_sel = MOBA_TOPK + 1
    idx = jnp.concatenate([jnp.minimum(top_i, nb - 1), jnp.broadcast_to(qblk[None, None, :, None], (B, H, L, 1))], axis=-1)
    ok = jnp.concatenate([jnp.isfinite(top_s), jnp.ones((B, H, L, 1), bool)], axis=-1)

    qb = MOBA_QBLOCK if L % MOBA_QBLOCK == 0 else L
    nq = L // qb
    q_x = q.reshape(B, nq, qb, H, hd).transpose(0, 1, 3, 2, 4).reshape(B * nq, H, qb, hd)
    idx_x = idx.reshape(B, H, nq, qb, n_sel).transpose(0, 2, 1, 3, 4).reshape(B * nq, H, qb, n_sel)
    ok_x = ok.reshape(B, H, nq, qb, n_sel).transpose(0, 2, 1, 3, 4).reshape(B * nq, H, qb, n_sel)
    pos_x = jnp.broadcast_to(qpos.reshape(1, nq, qb), (B, nq, qb)).reshape(B * nq, qb)
    b_x = jnp.repeat(jnp.arange(B, dtype=jnp.int32), nq)
    bias_t = rel_bias.T
    hix = jnp.arange(H)[:, None, None]
    scale = HD_C ** -0.5

    def attend_block(args):
        b, qq, ii, oo, pp = args
        ksel = kb[b][hix, ii]
        vsel = vb[b][hix, ii]
        kpos = ii[..., None] * MOBA_BLOCK + jnp.arange(MOBA_BLOCK, dtype=jnp.int32)
        rel = pp[None, :, None, None] - kpos
        s = jnp.einsum('hqd,hqnkd->hqnk', qq, ksel).astype(jnp.float32) * scale
        s = s + bias_t[hix[..., None], rel_bucket(rel)].astype(jnp.float32)
        s = jnp.where(oo[..., None] & (rel >= 0), s, -jnp.inf)
        p = jax.nn.softmax(s.reshape(H, qb, -1), axis=-1).reshape(s.shape)
        return jnp.einsum('hqnk,hqnkd->hqd', p.astype(vsel.dtype), vsel)

    o = lax.map(attend_block, (b_x, q_x, idx_x, ok_x, pos_x))
    return o.reshape(B, nq, H, qb, hd).transpose(0, 1, 3, 2, 4).reshape(B, L, H * hd)

def even_mixer(h, conv_buf, S_gdn, S_hg, lb, P, e):
    B, L, _ = h.shape
    dA, dB = H_A * HD_A, H_B * DK_B
    z = h @ P['ev_w_in'][e]
    qkv, zg, b_raw, a_raw, hq, hf, hi, hg = _split(z, [3 * dA, dA, H_A, H_A, dB, dB, H_B * DV_B, H_B * DV_B])
    qkv, conv_new = causal_dwconv(qkv, conv_buf, P['gdn_conv_w'][e])
    q, k, v = _split(jax.nn.silu(qkv), [dA, dA, dA])
    q = l2norm(q.reshape(B, L, H_A, HD_A)) * HD_A ** -0.5
    k = l2norm(k.reshape(B, L, H_A, HD_A))
    v = v.reshape(B, L, H_A, HD_A)
    beta = jax.nn.sigmoid(b_raw.astype(jnp.float32))
    g = -jnp.exp(P['gdn_A_log'][e].astype(jnp.float32)) * jax.nn.softplus(a_raw.astype(jnp.float32) + P['gdn_dt_bias'][e].astype(jnp.float32))
    o_a, S_gdn_new = gated_delta_rule(q, k, v, beta, g, S_gdn)
    o_a = rmsnorm(o_a, P['gdn_norm'][e]) * jax.nn.silu(zg.reshape(B, L, H_A, HD_A).astype(jnp.float32))
    f = lb + (1.0 - lb) * jax.nn.sigmoid(hf.astype(jnp.float32))
    qh = jax.nn.silu(hq.astype(jnp.float32)).reshape(B, L, H_B, DK_B)
    o_b, S_hg_new = hgrn2_recurrence(qh, (1.0 - f).reshape(B, L, H_B, DK_B), jnp.log(f).reshape(B, L, H_B, DK_B),
                                     hi.reshape(B, L, H_B, DV_B), S_hg)
    o_b = rmsnorm(o_b, P['hgrn_norm'][e]) * jax.nn.silu(hg.reshape(B, L, H_B, DV_B).astype(jnp.float32))
    mixed = jnp.concatenate([o_a.reshape(B, L, -1), o_b.reshape(B, L, -1)], axis=-1).astype(h.dtype)
    return mixed @ P['ev_w_out'][e], conv_new, S_gdn_new.astype(S_gdn.dtype), S_hg_new.astype(S_hg.dtype)

def odd_mixer(h, pos0, k_past, v_past, s_re, s_im, P, o):
    B, L, _ = h.shape
    dC, dD = H_C * HD_C, S5_GROUPS * S5_GROUP_CH
    z = h @ P['od_w_in'][o]
    q, k, v, u = _split(z, [dC, dC, dC, dD])
    q = rmsnorm(q.reshape(B, L, H_C, HD_C), P['moba_gq'][o])
    k = rmsnorm(k.reshape(B, L, H_C, HD_C), P['moba_gk'][o])
    v = v.reshape(B, L, H_C, HD_C)
    k_all = jnp.concatenate([k_past.astype(k.dtype), k], axis=1)
    v_all = jnp.concatenate([v_past.astype(v.dtype), v], axis=1)
    o_c = moba_attend(q, k_all, v_all, pos0, P['rel_bias'])
    y, hr, hi = s5_scan(u.reshape(B, L, S5_GROUPS, S5_GROUP_CH).astype(jnp.float32), s_re, s_im,
                        P['s5_A_re'][o], P['s5_A_im'][o], P['s5_log_dt'][o], P['s5_B_re'][o], P['s5_B_im'][o],
                        P['s5_C_re'][o], P['s5_C_im'][o], P['s5_D'][o])
    y = jax.nn.gelu(y.reshape(B, L, dD))
    ga, gb = _split(y @ P['s5_glu_w'][o].astype(jnp.float32), [dD, dD])
    o_d = ga * jax.nn.sigmoid(gb)
    mixed = jnp.concatenate([o_c.astype(h.dtype), o_d.astype(h.dtype)], axis=-1)
    return mixed @ P['od_w_out'][o], k, v, hr.astype(s_re.dtype), hi.astype(s_im.dtype)

def mem_kv(mem, g_norm, w_kv, g_k):
    B, M, _ = mem.shape
    kv = rmsnorm(mem, g_norm) @ w_kv
    k, v = _split(kv, [MEM_H * MEM_HD, MEM_H * MEM_HD])
    return rmsnorm(k.reshape(B, M, MEM_H, MEM_HD), g_k), v.reshape(B, M, MEM_H, MEM_HD)

def mem_attend(h, mk, mv, w_q, g_q, w_o):
    B, L, _ = h.shape
    q = rmsnorm((h @ w_q).reshape(B, L, MEM_H, MEM_HD), g_q)
    s = jnp.einsum('blhd,bmhd->bhlm', q, mk.astype(q.dtype)).astype(jnp.float32) * MEM_HD ** -0.5
    p = jax.nn.softmax(s, axis=-1).astype(h.dtype)
    o = jnp.einsum('bhlm,bmhd->blhd', p, mv.astype(h.dtype)).reshape(B, L, MEM_H * MEM_HD)
    return o @ w_o

def conv_ffn(h, buf, w_gu, conv_w, conv_b, w_down):
    gt, up = _split(h @ w_gu, [D_FF, D_FF])
    gt, buf_new = causal_dwconv(gt, buf, conv_w)
    return (jax.nn.silu(gt + conv_b) * up) @ w_down, buf_new

def trunk(x, pos0, gdn_conv0, gdn0, hgrn0, k_past, v_past, s5re0, s5im0, mem_k, mem_v, ffn0, P):
    lb_all = jnp.cumsum(jax.nn.softmax(P['hgrn_lb_raw'].astype(jnp.float32), axis=0), axis=0)
    conv_s, gdn_s, hgrn_s, k_s, v_s, re_s, im_s, ffn_s = [], [], [], [], [], [], [], []
    for l in range(DEPTH):
        h = rmsnorm(x, P['norm_mix'][l])
        if l % 2 == 0:
            e = l // 2
            out, c, sg, sh = even_mixer(h, gdn_conv0[e], gdn0[e], hgrn0[e], lb_all[l], P, e)
            conv_s.append(c)
            gdn_s.append(sg)
            hgrn_s.append(sh)
        else:
            o = l // 2
            out, kn, vn, sr, si = odd_mixer(h, pos0, k_past[o], v_past[o], s5re0[o], s5im0[o], P, o)
            k_s.append(kn)
            v_s.append(vn)
            re_s.append(sr)
            im_s.append(si)
        x = x + out.astype(x.dtype)
        x = x + mem_attend(rmsnorm(x, P['norm_mem'][l]), mem_k[l], mem_v[l], P['mem_wq'][l], P['mem_gq'][l], P['mem_wo'][l]).astype(x.dtype)
        f, fs = conv_ffn(rmsnorm(x, P['norm_ffn'][l]), ffn0[l], P['ffn_w_gu'][l], P['ffn_conv_w'][l], P['ffn_conv_b'][l], P['ffn_w_down'][l])
        x = x + f.astype(x.dtype)
        ffn_s.append(fs)
    return (x, jnp.stack(conv_s), jnp.stack(gdn_s), jnp.stack(hgrn_s), jnp.stack(k_s), jnp.stack(v_s),
            jnp.stack(re_s), jnp.stack(im_s), jnp.stack(ffn_s))

def setup_inputs(seed: int = 0) -> dict:
    key = jax.random.key(seed)
    cnt = [0]

    def nk():
        cnt[0] += 1
        return jax.random.fold_in(key, cnt[0])

    def nrm(shape, scale=1.0):
        return scale * jax.random.normal(nk(), shape, jnp.float32)

    def gain(shape):
        return 1.0 + nrm(shape, 0.05)

    def unif(shape, lo, hi):
        return jax.random.uniform(nk(), shape, jnp.float32, lo, hi)

    n_pages = PAST_LEN // PAGE_SIZE
    n_pool = (DEC_BATCH * n_pages * 5) // 4
    page_table = jax.random.permutation(nk(), n_pool)[: DEC_BATCH * n_pages].reshape(DEC_BATCH, n_pages).astype(jnp.int32)
    dt_gdn = jnp.exp(unif((N_EVEN, H_A), math.log(1e-3), math.log(1e-1)))
    a_im0 = jnp.pi * jnp.arange(S5_STATE, dtype=jnp.float32)
    dA3 = 3 * H_A * HD_A
    return {
        'x_prompt': nrm((BATCH, SEQ, D_MODEL)),
        'x_sample': nrm((DEC_BATCH, DEC_SEQ, D_MODEL)),
        'state_gdn_conv': nrm((N_EVEN, DEC_BATCH, GDN_CONV - 1, dA3)),
        'state_gdn': nrm((N_EVEN, DEC_BATCH, H_A, HD_A, HD_A), 0.1),
        'state_hgrn': nrm((N_EVEN, DEC_BATCH, H_B, DK_B, DV_B), 0.5),
        'cache_moba_k': nrm((N_ODD, n_pool, PAGE_SIZE, H_C, HD_C)),
        'cache_moba_v': nrm((N_ODD, n_pool, PAGE_SIZE, H_C, HD_C)),
        'state_s5_re': nrm((N_ODD, DEC_BATCH, S5_GROUPS, S5_STATE), 0.3),
        'state_s5_im': nrm((N_ODD, DEC_BATCH, S5_GROUPS, S5_STATE), 0.3),
        'cache_mem_k': nrm((DEPTH, DEC_BATCH, N_MEM, MEM_H, MEM_HD)),
        'cache_mem_v': nrm((DEPTH, DEC_BATCH, N_MEM, MEM_H, MEM_HD)),
        'state_ffn_conv': nrm((DEPTH, DEC_BATCH, FFN_CONV - 1, D_FF)),
        'page_table': page_table,
        'mem_prompt': nrm((BATCH, N_MEM, D_MODEL)),
        'rel_bias': nrm((N_BUCKETS, H_C), 0.5),
        'hgrn_lb_raw': nrm((DEPTH + 1, H_B * DK_B), 0.1),
        'norm_mix': gain((DEPTH, D_MODEL)),
        'norm_mem': gain((DEPTH, D_MODEL)),
        'norm_memkv': gain((DEPTH, D_MODEL)),
        'norm_ffn': gain((DEPTH, D_MODEL)),
        'mem_wq': nrm((DEPTH, D_MODEL, MEM_H * MEM_HD), D_MODEL ** -0.5),
        'mem_wkv': nrm((DEPTH, D_MODEL, 2 * MEM_H * MEM_HD), D_MODEL ** -0.5),
        'mem_gq': gain((DEPTH, MEM_HD)),
        'mem_gk': gain((DEPTH, MEM_HD)),
        'mem_wo': nrm((DEPTH, MEM_H * MEM_HD, D_MODEL), 0.5 * (MEM_H * MEM_HD) ** -0.5),
        'ffn_w_gu': nrm((DEPTH, D_MODEL, 2 * D_FF), D_MODEL ** -0.5),
        'ffn_conv_w': nrm((DEPTH, FFN_CONV, D_FF), FFN_CONV ** -0.5),
        'ffn_conv_b': nrm((DEPTH, D_FF), 0.02),
        'ffn_w_down': nrm((DEPTH, D_FF, D_MODEL), 0.5 * D_FF ** -0.5),
        'ev_w_in': nrm((N_EVEN, D_MODEL, EV_IN), D_MODEL ** -0.5),
        'ev_w_out': nrm((N_EVEN, EV_OUT, D_MODEL), 0.5 * EV_OUT ** -0.5),
        'gdn_conv_w': nrm((N_EVEN, GDN_CONV, dA3), GDN_CONV ** -0.5),
        'gdn_A_log': jnp.log(unif((N_EVEN, H_A), 1.0, 16.0)),
        'gdn_dt_bias': dt_gdn + jnp.log(-jnp.expm1(-dt_gdn)),
        'gdn_norm': gain((N_EVEN, HD_A)),
        'hgrn_norm': gain((N_EVEN, DV_B)),
        'od_w_in': nrm((N_ODD, D_MODEL, OD_IN), D_MODEL ** -0.5),
        'od_w_out': nrm((N_ODD, OD_OUT, D_MODEL), 0.5 * OD_OUT ** -0.5),
        'moba_gq': gain((N_ODD, HD_C)),
        'moba_gk': gain((N_ODD, HD_C)),
        's5_A_re': -0.5 + nrm((N_ODD, S5_GROUPS, S5_STATE), 0.01),
        's5_A_im': a_im0 + nrm((N_ODD, S5_GROUPS, S5_STATE), 0.01),
        's5_log_dt': unif((N_ODD, S5_GROUPS), math.log(1e-3), math.log(1e-1)),
        's5_B_re': nrm((N_ODD, S5_GROUPS, S5_STATE, S5_GROUP_CH), (2 * S5_GROUP_CH) ** -0.5),
        's5_B_im': nrm((N_ODD, S5_GROUPS, S5_STATE, S5_GROUP_CH), (2 * S5_GROUP_CH) ** -0.5),
        's5_C_re': nrm((N_ODD, S5_GROUPS, S5_GROUP_CH, S5_STATE), (2 * S5_STATE) ** -0.5),
        's5_C_im': nrm((N_ODD, S5_GROUPS, S5_GROUP_CH, S5_STATE), (2 * S5_STATE) ** -0.5),
        's5_D': nrm((N_ODD, S5_GROUPS, S5_GROUP_CH), 0.5),
        's5_glu_w': nrm((N_ODD, S5_GROUPS * S5_GROUP_CH, 2 * S5_GROUPS * S5_GROUP_CH), (S5_GROUPS * S5_GROUP_CH) ** -0.5),
    }

def reference(x_prompt, x_sample, state_gdn_conv, state_gdn, state_hgrn, cache_moba_k, cache_moba_v,
              state_s5_re, state_s5_im, cache_mem_k, cache_mem_v, state_ffn_conv, page_table, mem_prompt,
              rel_bias, hgrn_lb_raw, norm_mix, norm_mem, norm_memkv, norm_ffn, mem_wq, mem_wkv, mem_gq, mem_gk,
              mem_wo, ffn_w_gu, ffn_conv_w, ffn_conv_b, ffn_w_down, ev_w_in, ev_w_out, gdn_conv_w, gdn_A_log,
              gdn_dt_bias, gdn_norm, hgrn_norm, od_w_in, od_w_out, moba_gq, moba_gk, s5_A_re, s5_A_im, s5_log_dt,
              s5_B_re, s5_B_im, s5_C_re, s5_C_im, s5_D, s5_glu_w):
    P = dict(rel_bias=rel_bias, hgrn_lb_raw=hgrn_lb_raw, norm_mix=norm_mix, norm_mem=norm_mem, norm_ffn=norm_ffn,
             mem_wq=mem_wq, mem_gq=mem_gq, mem_wo=mem_wo, ffn_w_gu=ffn_w_gu, ffn_conv_w=ffn_conv_w,
             ffn_conv_b=ffn_conv_b, ffn_w_down=ffn_w_down, ev_w_in=ev_w_in, ev_w_out=ev_w_out,
             gdn_conv_w=gdn_conv_w, gdn_A_log=gdn_A_log, gdn_dt_bias=gdn_dt_bias, gdn_norm=gdn_norm,
             hgrn_norm=hgrn_norm, od_w_in=od_w_in, od_w_out=od_w_out, moba_gq=moba_gq, moba_gk=moba_gk,
             s5_A_re=s5_A_re, s5_A_im=s5_A_im, s5_log_dt=s5_log_dt, s5_B_re=s5_B_re, s5_B_im=s5_B_im,
             s5_C_re=s5_C_re, s5_C_im=s5_C_im, s5_D=s5_D, s5_glu_w=s5_glu_w)

    Bp = x_prompt.shape[0]
    dt = x_prompt.dtype
    mk_l, mv_l = [], []
    for l in range(DEPTH):
        mk, mv = mem_kv(mem_prompt, norm_memkv[l], mem_wkv[l], mem_gk[l])
        mk_l.append(mk)
        mv_l.append(mv)
    p_mem_k = jnp.stack(mk_l)
    p_mem_v = jnp.stack(mv_l)
    (y_prompt, p_gdn_conv, p_gdn, p_hgrn, p_moba_k, p_moba_v, p_s5_re, p_s5_im, p_ffn_conv) = trunk(
        x_prompt, 0,
        jnp.zeros((N_EVEN, Bp, GDN_CONV - 1, 3 * H_A * HD_A), dt),
        jnp.zeros((N_EVEN, Bp, H_A, HD_A, HD_A), dt),
        jnp.zeros((N_EVEN, Bp, H_B, DK_B, DV_B), dt),
        jnp.zeros((N_ODD, Bp, 0, H_C, HD_C), dt), jnp.zeros((N_ODD, Bp, 0, H_C, HD_C), dt),
        jnp.zeros((N_ODD, Bp, S5_GROUPS, S5_STATE), dt), jnp.zeros((N_ODD, Bp, S5_GROUPS, S5_STATE), dt),
        p_mem_k, p_mem_v, jnp.zeros((DEPTH, Bp, FFN_CONV - 1, D_FF), dt), P)

    Bs = x_sample.shape[0]
    n_pages = page_table.shape[1]
    past = n_pages * PAGE_SIZE
    k_past = cache_moba_k[:, page_table].reshape(N_ODD, Bs, past, H_C, HD_C)
    v_past = cache_moba_v[:, page_table].reshape(N_ODD, Bs, past, H_C, HD_C)
    (y_sample, s_gdn_conv, s_gdn, s_hgrn, s_moba_k, s_moba_v, s_s5_re, s_s5_im, s_ffn_conv) = trunk(
        x_sample, past, state_gdn_conv, state_gdn, state_hgrn, k_past, v_past, state_s5_re, state_s5_im,
        cache_mem_k, cache_mem_v, state_ffn_conv, P)

    return (y_prompt, y_sample, p_gdn_conv, p_gdn, p_hgrn, p_moba_k, p_moba_v, p_s5_re, p_s5_im, p_mem_k, p_mem_v,
            p_ffn_conv, s_gdn_conv, s_gdn, s_hgrn, s_moba_k, s_moba_v, s_s5_re, s_s5_im, s_ffn_conv)


_drawn_inputs = setup_inputs


def setup_inputs(seed=0):
    import zlib

    import numpy as np

    out = dict(_drawn_inputs(seed))
    spreads = {}
    factors = {'cache_moba_k': 3.319,
     'cache_moba_v': 2.8,
     'norm_mem': 8.0,
     'mem_gq': 8.0,
     'ffn_conv_b': 7.212,
     'gdn_norm': 5.007,
     'hgrn_norm': 5.027,
     'moba_gq': 8.0,
     's5_A_re': 4.567,
     's5_C_re': 2.835,
     's5_C_im': 2.778}
    for name, (base, spread) in spreads.items():
        noise = np.random.default_rng([zlib.crc32(name.encode()), seed]).standard_normal(out[name].shape)
        drawn = base * np.exp(spread * noise) if base else spread * noise
        out[name] = jnp.asarray(drawn.astype(out[name].dtype))
    for name, factor in factors.items():
        out[name] = (out[name] * factor).astype(out[name].dtype)
    return out
```

```python
import math
from contextlib import ExitStack

import numpy as np
import concourse.bass as bass
from concourse import mybir

F32 = mybir.dt.float32
I32 = mybir.dt.int32
ALU = mybir.AluOpType
ACT = mybir.ActivationFunctionType
AX = mybir.AxisListType.X

D = 1024
KC = D // 128
L = 256
NS = 8
T = L + NS
H = 8
HC = 4
HD = 64
CHK = 128
NCH = L // CHK
HCK = 32
MH = 4
NM = 256
DFF = 2816
FT = DFF // 128
PAGES = 8
POOL_PAGES = 80
NT = 16
EPS = 1e-6
BIG = -1.0e30
LEV = 7
SLOTS = 4
SLOTW = FT * 128
NBANK = 8
TWO_PI = 2.0 * math.pi
MAGIC = 12582912.0

VEC = {}
_off = 0
for _name, _w in [("norm_mix", 16), ("norm_mem", 16), ("norm_memkv", 16), ("norm_ffn", 16), ("mem_gq", 2),
                  ("mem_gk", 2), ("ffn_w", 2 * 3 * FT), ("ffn_b", 2 * FT), ("conv_w", 48), ("gdn_norm", 1),
                  ("hgrn_norm", 1), ("moba_gq", 1), ("moba_gk", 1), ("lb", 12), ("s5_re", NT), ("s5_im", NT),
                  ("s5_dt", NT), ("s5_d", 4), ("small", 2), ("relb", H), ("relb0", H), ("w_ab", KC * 40)]:
    VEC[_name] = _off
    _off += _w
VECW = _off
CON = {}
_off = 0
for _name, _w in [("ident", 128), ("ones", 128), ("bd", 128), ("neg", 128), ("i2", 64), ("lev", LEV * 128),
                  ("selh", H * 128), ("nselh", H * 128), ("selc", HC * 128), ("hotx", 512), ("hots", 1024),
                  ("cmask", 128)]:
    CON[_name] = _off
    _off += _w
CONW = _off


def constants():
    c = np.zeros((128, CONW), np.float32)
    p = np.arange(128)

    def put(name, a):
        c[:a.shape[0], CON[name]:CON[name] + a.shape[1]] = a

    put("ident", np.eye(128))
    put("ones", np.ones((128, 128)))
    put("bd", (p[:, None] // 64 == p[None] // 64) * 1.0)
    put("neg", np.where(p[None] >= p[:, None], 0.0, BIG))
    put("i2", (p[:, None] % 64 == np.arange(64)[None]) * 1.0)
    for l in range(LEV):
        b = 1 << l
        m = (p[None] // (2 * b) == p[:, None] // (2 * b)) & (p[None] // b % 2 == 1) & (p[:, None] // b % 2 == 0)
        c[:, CON["lev"] + 128 * l:CON["lev"] + 128 * (l + 1)] = m
    for h in range(H):
        c[h, CON["selh"] + 128 * h:CON["selh"] + 128 * (h + 1)] = 1.0
        c[h, CON["nselh"] + 128 * h:CON["nselh"] + 128 * (h + 1)] = -1.0
        at = CON["selc"] + 64 * h
        c[h, at:at + 64] = 1.0

    def bucket(n):
        if n < 16:
            return n
        return min(16 + int(math.log(n / 16) / math.log(8.0) * 16 + 1e-9), 31)
    for j in range(512):
        dist = j - 255
        c[32 if dist < 0 else bucket(dist), CON["hotx"] + j] = 1.0
    for k in range(1024):
        c[bucket(1024 - k), CON["hots"] + k] = 1.0
    put("cmask", ((p[:, None] // HCK == p[None] // HCK) & (p[None] >= p[:, None])) * 1.0)
    return c


def make_plan():
    order, slots, slot_of = [], [], {}

    def lin(name, tiles, per_slot, cols):
        for m in range(tiles):
            if m % per_slot == 0:
                slots.append(("w", name, m // per_slot, cols, None))
            slot_of[(name, m)] = len(slots) - 1
            order.append(("lin", name, m))
            slots[-1] = slots[-1][:4] + (("lin", name, m),)

    def stream(name, i, cols, last):
        slots.append(("w" if name[0] == "c" else "page", name, i, cols, last))
        slot_of[(name, i)] = len(slots) - 1

    def memory(l):
        order.append(("ss", "memkv", l))
        lin(f"memk{l}", MH, 2, 2048)
        for h in range(MH):
            order.append(("hn", f"memk{l}", h))
        lin(f"memv{l}", MH, 2, 2048)
        order.extend([("mvt", l, 0), ("mvt", l, 1)])
        order.append(("ss", "mem", l))
        lin(f"wq{l}", MH, 2, 2048)
        for h in range(MH):
            order.append(("hn", f"memq{l}", h))
        attend(f"mem{l}", MH)
        for i in range(4):
            stream(f"ck{l}", i, 2048, ("sc", f"mem{l}", 0))
        order.append(("sc", f"mem{l}", 0))
        order.extend([("mxt", f"mem{l}", 0), ("mxb", f"mem{l}", 0), ("sum", f"mem{l}", 0)])
        for i in range(4):
            stream(f"cv{l}", i, 2048, ("so", f"mem{l}", 0))
        order.append(("so", f"mem{l}", 0))
        lin(f"wo{l}", KC, 4, 2048)

    def attend(name, n):
        for i in range(n + 2):
            if i < n:
                order.append(("S", name, i))
            if 0 <= i - 1 < n:
                order.append(("PT", name, i - 1))
            if 0 <= i - 2 < n:
                order.append(("O", name, i - 2))

    def ffn(l):
        order.append(("ss", "ffn", l))
        lin(f"gu{l}", 2 * FT, 2, 2048)
        lin(f"down{l}", KC, 1, SLOTW)

    order.append(("ss", "mix", 0))
    order.append(("ab",))
    lin("ev_in_a", 16, 2, 2048)
    for i in range(8):
        order.append(("hn", "l2", i))
    for c in range(HC):
        order.extend([("bcB", c), ("bcG", c), ("bcL", c)])
    for t in range(NCH):
        order.extend([("trk", t), ("trv", t)])
    G4 = [(t, par) for t in range(NCH) for par in range(2)]
    for g in G4:
        order.extend([("DT", g), ("QK", g), ("KK", g)])
    for g in G4:
        order.append(("X1", g))
    for l in range(1, LEV):
        for g in G4:
            order.append(("T1", l, g))
        for g in G4:
            order.append(("ZT", l, g))
            if l < LEV - 1:
                order.append(("Z", l, g))
    for t in range(NCH):
        if t:
            order.extend([("ks", 0), ("ks", 1)])
        order.extend([("u", t), ("o", t, 0), ("o", t, 1), ("S", "gdn", t)])
    for i in range(HC):
        order.append(("su", "gdn", i))
    order.extend([("sO", "gdn", 0), ("sO", "gdn", 1)])
    for c in range(HC):
        order.append(("hn", "gdn", c))
    lin("ev_in_b", 16, 2, 2048)
    for t in range(NCH):
        order.extend([("htk", t), ("htv", t)])
    for g in G4:
        order.append(("att", g))
    for k in range(L // HCK):
        order.append(("kv", k))
    for g in G4:
        order.append(("ho", g))
    for i in range(HC):
        order.append(("su", "hgrn", i))
    order.extend([("sO", "hgrn", 0), ("sO", "hgrn", 1)])
    for c in range(HC):
        order.append(("hn", "hgrn", c))
    lin("ev_out", KC, 2, 2048)
    memory(0)
    ffn(0)
    order.append(("ss", "mix", 1))
    lin("od_in", 16, 2, 2048)
    for i in range(8):
        order.append(("hn", "moba", i))
    order.extend([("vt", 0), ("vt", 1), ("bx",), ("bs",)])
    attend("moba", H)
    for i in range(16):
        stream("pk", i, 2048, ("used", i + 1) if i < 15 else ("sc", "moba", 0))
    order.append(("sc", "moba", 0))
    order.extend([("self",), ("gate",), ("mxt", "moba", 0), ("mxb", "moba", 0), ("sum", "moba", 0)])
    for i in range(16):
        stream("pv", i, 2048, ("used", 15 + i // 2 + 1) if i < 14 else ("so", "moba", 0))
    order.append(("so", "moba", 0))
    for j in range(4):
        order.append(("s5s", j))
    for n in range(NT):
        order.append(("s5x", n))
        if n >= 4 and n % 4 == 0:
            order.append(("s5y", n // 4 - 1))
    order.append(("s5y", 3))
    lin("glu", 8, 4, 2048)
    lin("od_out", KC, 2, 2048)
    memory(1)
    ffn(1)
    return order, slots, slot_of


def build(nc, A):
    order, slots, slot_of = make_plan()
    no = {k: i for i, k in enumerate(order)}
    assert len(no) == len(order)
    hn_no = {}
    at_no = {}
    for k in order:
        if k[0] == "hn":
            hn_no[k[1:]] = len(hn_no)
        if k[0] == "PT":
            at_no[k[1:]] = len(at_no)

    slot_value, seen = [], [0] * SLOTS
    for s, (kind, _, _, _, _) in enumerate(slots):
        seen[s % SLOTS] += 16 * (4 if kind == "page" else 1)
        slot_value.append(seen[s % SLOTS])

    with ExitStack() as ctx:
        def sb(name, shape, dt=F32):
            return ctx.enter_context(nc.sbuf_tensor(name, shape, dt))

        def sem(name):
            return ctx.enter_context(nc.semaphore(name))

        banks = [ctx.enter_context(nc.psum_tensor(f"bank{i}", [128, 512], F32)) for i in range(NBANK)]

        def bank(key):
            return banks[no[key] % NBANK]

        def blocks(key, n=4, p0=0, p1=128):
            return bank(key)[p0:p1, 0:n * 128].rearrange("p (n k) -> p n k", n=n)

        con = sb("con", [128, CONW])
        vec = sb("vec", [128, VECW])
        pages = sb("pages_sb", [1, NS * PAGES], I32)
        ring = sb("ring", [128, SLOTS, SLOTW])
        x = sb("x", [128, KC, T])
        h = sb("h", [128, KC, T])
        sq = sb("sq", [128, KC, T])
        mix = sb("mix", [128, KC, T])
        oT = sb("oT", [128, HC, T])
        tmp = sb("tmp", [128, 2, T])
        lnb = sb("lnb", [128, T])
        rs = sb("rs", [128, T])
        hsq = sb("hsq", [128, 2, T])
        hr = sb("hr", [128, 2, T])
        rmask = sb("rmask", [128, L])
        cvo = sb("cvo", [128, 12, 27])
        egc = sb("egc", [128, HC, 9])
        ch = sb("ch", [128, 12, 24])
        sg = sb("sg", [128, HC, HD])
        lbt = sb("lbt", [128, 8, HC])
        par = sb("s5par", [128, 24, NT])
        relb = sb("relb", [64, H])
        aexp = sb("aexp", [8, 1])
        epst = sb("epst", [128, 1])
        onec = sb("onec", [128, 1])
        WORK = 21700
        work = sb("work", [128, WORK])

        def place(at, *dims):
            n = int(np.prod(dims))
            assert at + n <= WORK, (at, n)
            v = work[:, at:at + n]
            if len(dims) == 2:
                v = v.rearrange("p (a b) -> p a b", a=dims[0])
            if len(dims) == 3:
                v = v.rearrange("p (a b c) -> p a b c", a=dims[0], b=dims[1])
            return v, at + n

        def cst(name, w=128, i=0, p=128):
            return con[0:p, CON[name] + i * w:CON[name] + (i + 1) * w]

        def col(name, i=0, p0=0, p1=128):
            return vec[p0:p1, VEC[name] + i:VEC[name] + i + 1]

        def cols(name, n, i=0, p0=0, p1=128):
            return vec[p0:p1, VEC[name] + i:VEC[name] + i + n]

        ident, ones, bd = cst("ident"), cst("ones"), cst("bd")

        def four(ap):
            return ap.unsqueeze(1).broadcast_to([128, 4, 128])

        psum_full = sem("psum_full")
        psum_free = [sem(f"psum_free{i}") for i in range(NBANK)]
        ring_full = [sem(f"ring_full{i}") for i in range(SLOTS)]
        (con_in, vec_in, x_in, pages_in, hist_in, memx_in, sgs_in, shs_in, fh_in, s5_in, bias_in) = [
            sem(n) for n in ("con_in", "vec_in", "x_in", "pages_in", "hist_in", "memx_in", "sgs_in", "shs_in",
                             "fh_in", "s5_in", "bias_in")]
        act_step, dve_step, pool_step = sem("act_step"), sem("dve_step"), sem("pool_step")
        msq_ready, pages_used = sem("msq_ready"), sem("pages_used")
        sq_ready, r_ready, h_ready = sem("sq_ready"), sem("r_ready"), sem("h_ready")
        hsq_ready, hr_ready, hn_done = sem("hsq_ready"), sem("hr_ready"), sem("hn_done")
        mix_ready, stored, sgs_out = sem("mix_ready"), sem("stored"), sem("sgs_out")
        pads_ready, lb_step, gate_rows, conv_done, silu_done = [
            sem(n) for n in ("pads_ready", "lb_step", "gate_rows", "conv_done", "silu_done")]
        cvo_ready, scaled_ready, xt_ready, ml_ready = [
            sem(n) for n in ("cvo_ready", "scaled_ready", "xt_ready", "ml_ready")]
        w_ready, sdec_ready, sst_ready = sem("w_ready"), sem("sdec_ready"), sem("sst_ready")
        fk_ready, lf_ready, dec_ready, exp_ready, hg_dve, hg_pool, att_zero, sh_ready = [
            sem(n) for n in ("fk_ready", "lf_ready", "dec_ready", "exp_ready", "hg_dve", "hg_pool", "att_zero",
                             "sh_ready")]
        smax_ready, p_exp, p_ready = [sem(n) for n in ("smax_ready", "p_exp", "p_ready")]
        mx_ready, dg_ready, pp_ready = [sem(n) for n in ("mx_ready", "dg_ready", "pp_ready")]
        fpads, fconv_done, fsilu_done, act_ready, fcopy_done = [
            sem(n) for n in ("fpads", "fconv_done", "fsilu_done", "act_ready", "fcopy_done")]
        bx_stored, qbd_ready, qk_ready, samp_o = [
            sem(n) for n in ("bx_stored", "qbd_ready", "qk_ready", "samp_o")]
        s5_par, s5_hr, s5_g, s5_hi, s5_y, s5_gelu, s5_hs = [
            sem(n) for n in ("s5_par", "s5_hr", "s5_g", "s5_hi", "s5_y", "s5_gelu", "s5_hs")]
        ssub_ready, eps_ready, relb_ready, s5_gl2 = [
            sem(n) for n in ("ssub_ready", "eps_ready", "relb_ready", "s5_gl2")]
        hg_stored, mem_stored, ffn_stored, kv_stored = [
            sem(n) for n in ("hg_stored", "mem_stored", "ffn_stored", "kv_stored")]

        def full(eng, key):
            eng.wait_ge(psum_full, no[key] + 1)

        def drained(eng, key):
            eng.wait_ge(psum_free[no[key] % NBANK], no[key] // NBANK + 1)

        def drain(ins, key):
            return ins.then_inc(psum_free[no[key] % NBANK], 1)

        class Steps:
            def __init__(self, eng, s):
                self.eng, self.s, self.n = eng, s, 0

            def __call__(self, ins):
                self.n += 1
                ins.then_inc(self.s, 1)
                self.eng.wait_ge(self.s, self.n)

        norms = [k[1:] for k in order if k[0] == "ss"]
        xnorms = [n for n in norms if n[0] != "memkv"]
        NORM_G = {"mix": "norm_mix", "memkv": "norm_memkv", "mem": "norm_mem", "ffn": "norm_ffn"}
        G4 = [(t, p) for t in range(NCH) for p in range(2)]

        zqkv, e = place(0, 12, 3 + T)
        qkv, e = place(e, 12, T)
        kb, e = place(e, HC, T)
        bk, e = place(e, HC, T)
        qe, e = place(e, HC, T)
        vb, e = place(e, HC, T)
        ke, e = place(e, HC, L)
        ketok, e = place(e, NCH, 512)
        vbtok, e = place(e, NCH, 512)
        qkd, e = place(e, 4, 512)
        ws1, _ = place(e - 2048, HC, NS, HD)
        gs, _ = place(e, 5, T)
        xx, e = place(e, 4, 512)
        ws2, _ = place(e - 2048, HC, NS, HD)
        dt_, e = place(e, 2, 512)
        rhst, e = place(e, 512)
        utok, e = place(e, 512)
        assert e <= WORK - HC * T
        zg, _ = place(WORK - HC * T, HC, T)
        mt, _ = place(0, 4, 512)
        ml, _ = place(2048, 2, 512)
        sgs, _ = place(0, HC, NS, HD)
        flat = "p a b -> p (a b)"
        xt = sq[:, :, :].rearrange(flat)[:, 0:2048].rearrange("p (g n) -> p g n", g=4)
        t1 = mix[:, :, :].rearrange(flat)[:, 0:2048].rearrange("p (g n) -> p g n", g=4)
        zq, e = place(2816, HC, T)
        zf, e = place(e, HC, T)
        zk, e = place(e, HC, T)
        zi, e = place(e, HC, T)
        zh, e = place(e, HC, T)
        hkt, _ = place(e, NCH, 512)
        hvt, _ = place(e + 1024, NCH, 512)
        lf, e = place(e, HC, L)
        bcs, e = place(e, HC, L)
        hws1, _ = place(e, HC, NS, HD)
        d1, e = place(e, HC, L)
        d2, e = place(e, HC, L)
        hws2, _ = place(e, HC, NS, HD)
        qx, e = place(e, HC, L)
        kx, e = place(e, HC, L)
        qin, e = place(e, HC, L)
        ko, e = place(e, HC, L)
        fl, e = place(e, HC, L // HCK)
        attb, e = place(e, 4, 512)
        sh0 = e
        SH = [place(sh0 + 256 * (k % 8), HC, HD)[0] for k in range(8)]
        e = sh0 + 2048
        assert e <= WORK - HC * T, e
        shs, _ = place(0, HC, NS, HD)
        mh, e = place(0, KC, NM)
        mk, e = place(e, MH, NM)
        mv, e = place(e, MH, NM)
        mvt, e = place(e, 2, 512)
        mq, e = place(e, MH, T)
        msb, e = place(e, 2, 512)
        mpt, e = place(e, 2, 512)
        msml, e = place(e, 12, 64)
        att_buf = {"mem0": (msb, mpt), "mem1": (msb, mpt)}
        act_, e = place(e, FT, T)
        gb, e = place(e, 3, 2 + T)
        cacc, e = place(e, 2, T)
        csil, e = place(e, 2, T)
        fo, e = place(e, FT, 18)
        fh, e = place(e, FT, 16)
        zo, e = place(0, 16, T)
        hank, e = place(e, H, 384)
        ovt, e = place(e, 2, 512)
        osb, e = place(e, 2, 512)
        opt, e = place(e, 2, 512)
        att_buf["moba"] = (osb, opt)
        bsp, e = place(e, 64)
        qbd, e = place(e, HC, NS, 2)
        qkp, e = place(e, HC, NS, 2)
        WTMP = e
        sraw, e = place(e, 512)
        ssc, e = place(e, 512)
        spp, e = place(e, 512)
        gt, e = place(e, 512)
        gsm, e = place(e, 12, 64)
        cosT, e = place(e, NT, L)
        sinT, e = place(e, NT, L)
        ygl = zo[:, 8:12, :]
        s0 = 16 * T
        TABTMP = s0
        NHB = 8
        tmpy = zo[:, 0:4, :]
        ta, e2 = place(s0, 2, 2, L)
        tb, e2 = place(e2, 2, 2, L)
        gg, e2 = place(e2, 2, 2, L)
        pt_, e2 = place(e2, 2, 2, L)
        hh, e2 = place(e2, NHB, 2, L)
        hsS, e2 = place(e2, 2, NT, NS)
        w3, e2 = place(e2, NT, NS)
        w4, e2 = place(e2, NT, NS)
        assert e2 <= e - 2 * NT * L, (e2, e)
        sqf, hf_ = sq[:, :, :].rearrange(flat), h[:, :, :].rearrange(flat)
        s5b = sqf[:, 0:1024].rearrange("p (q c n) -> p q c n", q=2, c=4)
        s5c = sqf[:, 1024:2048].rearrange("p (q n k) -> p q n k", q=2, n=NT)
        s5cp = hf_[:, 0:1536].rearrange("p (q n k) -> p q n k", q=3, n=NT)
        s5h = hf_[:, 1536:1792].rearrange("p (q n s) -> p q n s", q=2, n=NT)
        s5o = sb("s5o", [128, 2, NT, 9])
        hl = sb("hl", [128, 2, NT])
        t16 = sb("t16", [128, 4, NT])
        bxs = hsq[0:8, :, :].rearrange(flat)[:, 0:512]
        smx = sb("smx", [128, 2, 4, 2])

        s_slots = list(enumerate(slots))

        block = ctx.enter_context(nc.Block())

        @block.sync
        def _(sp):
            sp.dma_start(con[:, :], A["con"]).then_inc(con_in, 16)
            sp.dma_start(x[:, :, :], A["x"]).then_inc(x_in, 16)
            sp.dma_start(vec[:, :], A["vec"]).then_inc(vec_in, 16)
            sp.dma_start(pages[:, :], A["pages"]).then_inc(pages_in, 16)
            sp.wait_ge(pages_in, 16)
            for s, (kind, name, i, w, _) in s_slots:
                if s >= SLOTS:
                    last = slots[s - SLOTS][4]
                    if last[0] == "used":
                        sp.wait_ge(pages_used, last[1])
                    else:
                        full(sp, last)
                dst = ring[:, s % SLOTS, 0:w]
                if kind == "w":
                    sp.dma_start(dst, A[name][i]).then_inc(ring_full[s % SLOTS], 16)
                    continue
                pool = A["pool_k"] if name == "pk" else A["pool_v"]
                for j in range(4):
                    at = 4 * i + j
                    page = sp.value_load(pages[0:1, at:at + 1], min_val=0, max_val=POOL_PAGES - 1)
                    sp.dma_start(dst[:, 512 * j:512 * (j + 1)].unsqueeze(1),
                                 pool[bass.ds(page, 1)].rearrange("a p n -> p a n")).then_inc(ring_full[s % SLOTS], 16)

        @block.gpsimd
        def _(pool):
            step = Steps(pool, pool_step)
            stores = [0]

            def store(dst, src, done=None):
                pool.dma_start(dst, src).then_inc(done or stored, 16)
                if not done:
                    stores[0] += 1

            step(nc.gpsimd.memset(rmask[:, :], 1.0))
            nc.gpsimd.memset(rmask[:, :].rearrange("p (k c) -> p k c", c=HCK)[:, :, 0:1], 0.0).then_inc(pads_ready, 1)
            nc.gpsimd.memset(zqkv[:, :, 0:3], 0.0).then_inc(pads_ready, 1)
            pool.dma_start(ch[:, :, :], A["gconv"]).then_inc(hist_in, 16)

            pool.wait_ge(hist_in, 16)
            drained(pool, ("lin", "ev_in_a", 11))
            nc.gpsimd.tensor_copy(cvo[:, :, 0:3], zqkv[:, :, 256:259])
            nc.gpsimd.tensor_copy(cvo[:, :, 3:19], ch[:, :, 8:24])
            nc.gpsimd.tensor_copy(cvo[:, :, 19:27], zqkv[:, :, 259:267]).then_inc(cvo_ready, 1)
            pool.wait_ge(cvo_ready, 1)
            store(A["o_gconv"], cvo[:, :, :])
            pool.wait_ge(xt_ready, 4)
            for l in range(1, LEV):
                for gi, g in enumerate(G4):
                    n = (l - 1) * 4 + gi
                    if n >= 2:
                        pn = n - 2
                        full(pool, ("T1", pn // 4 + 1, G4[pn % 4]))
                    nc.gpsimd.tensor_tensor(ml[:, n % 2, :].rearrange("p (n k) -> p n k", n=4),
                                            mt[:, gi, :].rearrange("p (n k) -> p n k", n=4),
                                            four(cst("lev", i=l)), ALU.mult).then_inc(ml_ready, 1)
            full(pool, ("T1", LEV - 1, G4[3]))
            pool.dma_start(sgs, A["sgs"]).then_inc(sgs_in, 16)
            drained(pool, ("S", "gdn", NCH - 1))
            store(A["o_gdn"], sg[:, :, :])
            pool.wait_ge(sgs_in, 16)
            pool.wait_ge(w_ready, 1)
            nc.gpsimd.tensor_tensor(sgs, sgs, egc[:, :, 1:9].unsqueeze(3).broadcast_to([128, HC, NS, HD]),
                                    ALU.mult).then_inc(sdec_ready, 1)
            pool.wait_ge(sst_ready, 4)
            pool.dma_start(A["o_sgs"], sgs).then_inc(sgs_out, 16)
            pool.wait_ge(sgs_out, 16)
            full(pool, ("sO", "gdn", 1))
            pool.dma_start(shs, A["shs"]).then_inc(shs_in, 16)
            nc.gpsimd.memset(attb, 0.0).then_inc(att_zero, 1)
            for m in range(4):
                drained(pool, ("lin", "ev_in_b", m))
            pool.wait_ge(exp_ready, 4)
            pool.wait_ge(fk_ready, HC)
            nc.gpsimd.tensor_copy(fl, qin[:, :, HCK - 1::HCK]).then_inc(hg_pool, 1)
            pool.wait_ge(hg_pool, 1)
            nc.gpsimd.tensor_tensor(ko, ko, zk[:, :, 0:L], ALU.mult).then_inc(hg_pool, 1)
            nc.gpsimd.tensor_tensor(qin, qin, zq[:, :, 0:L], ALU.mult).then_inc(hg_pool, 1)
            full(pool, ("ho", G4[3]))
            drained(pool, ("lin", "ev_in_b", 11))
            nc.gpsimd.tensor_tensor(hws2, cst("i2", 64).unsqueeze(1).unsqueeze(1).broadcast_to([128, HC, NS, HD]),
                                    zi[:, :, L:T].unsqueeze(3).broadcast_to([128, HC, NS, HD]),
                                    ALU.mult).then_inc(w_ready, 1)
            pool.wait_ge(shs_in, 16)
            nc.gpsimd.tensor_tensor(shs, shs, zf[:, :, L:T].unsqueeze(3).broadcast_to([128, HC, NS, HD]),
                                    ALU.mult).then_inc(sdec_ready, 1)
            drained(pool, ("kv", 7))
            store(A["o_hgrn"], SH[0], hg_stored)
            pool.wait_ge(sst_ready, 8)
            store(A["o_shs"], shs, hg_stored)

            def memory_io(l):
                full(pool, ("lin", "ev_out" if l == 0 else "od_out", KC - 1))
                pool.dma_start(h[:, :, 0:NM], A["memx"]).then_inc(memx_in, 16)
                pool.wait_ge(hn_done, hn_no[(f"memk{l}", MH - 1)] + 1)
                store(A["o_memk"][l], mk, mem_stored)
                drained(pool, ("lin", f"memv{l}", MH - 1))
                store(A["o_memv"][l], mv, mem_stored)

            def ffn_rows(l):
                full(pool, ("ss", "ffn", l))
                nc.gpsimd.memset(gb[:, :, 0:2], 0.0).then_inc(fpads, 1)
                pool.dma_start(fh, A["fh"][l]).then_inc(fh_in, 16)
                pool.wait_ge(fh_in, 16 * (l + 1))
                for i in range(FT):
                    drained(pool, ("lin", f"gu{l}", 2 * i))
                    nc.gpsimd.tensor_copy(fo[:, i, 0:2], gb[:, i % 3, 2 + L - 2:2 + L])
                    nc.gpsimd.tensor_copy(fo[:, i, 10:18], gb[:, i % 3, 2 + L:2 + T]).then_inc(fcopy_done, 1)
                nc.gpsimd.tensor_copy(fo[:, :, 2:10], fh[:, :, 8:16]).then_inc(fcopy_done, 1)
                pool.wait_ge(fcopy_done, (FT + 1) * (l + 1))
                store(A["o_ffn"][l], fo, ffn_stored)

            memory_io(0)
            ffn_rows(0)
            full(pool, ("ss", "mix", 1))
            pool.dma_start(s5b, A["s5b"]).then_inc(s5_in, 16)
            pool.dma_start(s5c, A["s5c"]).then_inc(s5_in, 16)
            full(pool, ("lin", "od_in", 15))
            pool.dma_start(s5h, A["s5h"]).then_inc(s5_in, 16)
            pool.wait_ge(hn_done, hn_no[("moba", 7)] + 1)
            store(A["o_k"], zo[:, 4:8, :], kv_stored)
            drained(pool, ("lin", "od_in", 11))
            store(A["o_v"], zo[:, 8:12, :], kv_stored)
            drained(pool, ("bx",))
            pool.dma_start(A["bias_x"], bxs).then_inc(bx_stored, 16)
            pool.wait_ge(bx_stored, 16)
            bx = A["bias_x"]
            pool.dma_start(hank, bass.AP(tensor=bx.tensor, offset=bx.offset,
                                         ap=[[1, 128], [512, H], [1, 384]])).then_inc(bias_in, 16)
            for n in range(NT):
                pool.wait_ge(s5_g, 2 * (n + 1))
                b = n % 2
                step(nc.gpsimd.tensor_tensor(pt_[:, b, 0, :], gg[:, b, 0, :], sinT[:, n, :], ALU.mult))
                step(nc.gpsimd.tensor_tensor(pt_[:, b, 1, :], gg[:, b, 1, :], cosT[:, n, :], ALU.mult))
                if n >= NHB:
                    full(pool, ("s5y", (n - NHB) // 4))
                nc.gpsimd.tensor_tensor(hh[:, n % NHB, 1, :], pt_[:, b, 0, :], pt_[:, b, 1, :],
                                        ALU.add).then_inc(s5_hi, 1)
                pool.wait_ge(s5_hi, 2 * n + 1)
                nc.gpsimd.tensor_copy(hl[:, 1, n:n + 1], hh[:, n % NHB, 1, L - 1:L]).then_inc(s5_hi, 1)
            pool.wait_ge(s5_hs, 3)
            store(A["o_s5"], s5o[:, :, :, :])
            memory_io(1)
            ffn_rows(1)
            drained(pool, ("lin", "down1", KC - 1))
            store(A["y"], x[:, :, :])
            for s_, n in ((stored, stores[0]), (hg_stored, 2), (mem_stored, 4), (ffn_stored, 2), (kv_stored, 2)):
                pool.wait_ge(s_, 16 * n)

        @block.scalar
        def _(act):
            step = Steps(act, act_step)

            def f(out, in_, func, **k):
                return nc.scalar.activation(out, in_, func, **k)

            def norm(i):
                kind, l = norms[i]
                w = NM if kind == "memkv" else T
                key = ("ss", kind, l)
                full(act, key)
                if seen["hn"]:
                    act.wait_ge(hr_ready, seen["hn"])
                seen["norm"] += 1
                f(lnb[:, 0:w], bank(key)[:, 0:w], ACT.Ln, scale=1.0 / D, bias=epsc).then_inc(
                    psum_free[no[key] % NBANK], 1)
                drained(act, key)
                f(rs[:, 0:w], lnb[:, 0:w], ACT.Exp, scale=-0.5).then_inc(r_ready, 1)

            seen = {"hn": 0, "norm": 0}

            def squares(name):
                for m in range(KC):
                    drained(act, ("lin", name, m))
                    f(sq[:, m, :], x[:, m, :], ACT.Square).then_inc(sq_ready, 1)

            def headnorm(name, n, w, mean, src, ready):
                base = hn_no[(name, 0)]
                for i in range(n + 1):
                    if i < n:
                        ready(i)
                        f(hsq[:, (base + i) % 2, 0:w], src(i), ACT.Square).then_inc(hsq_ready, 1)
                    if i >= 1:
                        j = base + i - 1
                        key = ("hn", name, i - 1)
                        full(act, key)
                        act.wait_ge(r_ready, seen["norm"])
                        if j:
                            act.wait_ge(hr_ready, j)
                        seen["hn"] = j + 1
                        drain(f(lnb[:, 0:w], bank(key)[:, 0:w], ACT.Ln, scale=mean, bias=epsc), key)
                        drained(act, key)
                        if j >= 2:
                            act.wait_ge(hn_done, j - 1)
                        f(hr[:, j % 2, 0:w], lnb[:, 0:w], ACT.Exp, scale=-0.5).then_inc(hr_ready, 1)

            def copy_out(key, dst, src):
                full(act, key)
                drain(f(dst, src, ACT.Copy), key)

            def attend(name, n, hd):
                pbuf, ptb = att_buf[name]
                for i in range(n + 2):
                    if i < n:
                        j = at_no[(name, i)]
                        act.wait_ge(smax_ready, j + 1)
                        b = j % 2
                        for qt in range(2):
                            v = pbuf[:, i % 2, qt * L:(qt + 1) * L]
                            ins = f(v, v, ACT.Exp, bias=smx[:, b, 0, qt:qt + 1], scale=1.0,
                                    accum_out=smx[:, b, 1, qt:qt + 1])
                        ins.then_inc(p_exp, 1)
                    if 0 <= i - 1 < n:
                        key = ("PT", name, i - 1)
                        full(act, key)
                        drain(f(ptb[:, (i - 1) % 2, :], bank(key)[:, :], ACT.Copy), key)
                    if 0 <= i - 2 < n:
                        k = i - 2
                        key = ("O", name, k)
                        p0 = 0 if hd == 128 else 64 * (k % 2)
                        c = k if hd == 128 else k // 2
                        copy_out(key, mix[p0:p0 + hd, c, 0:L], bank(key)[p0:p0 + hd, 0:L])

            epsc = epst[:, 0:1]
            act.wait_ge(eps_ready, 1)
            act.wait_ge(x_in, 16)
            for m in range(KC):
                f(sq[:, m, :], x[:, m, :], ACT.Square).then_inc(sq_ready, 1)
            act.wait_ge(vec_in, 16)
            act.wait_ge(lb_step, 1)
            f(lbt[:, 0:3, :], lbt[:, 0:3, :], ACT.Exp).then_inc(lb_step, 1)
            f(par[:, 0, :], cols("s5_dt", NT), ACT.Exp).then_inc(s5_par, 1)
            norm(0)
            act.wait_ge(s5_par, 2)
            f(par[:, 1, :], par[:, 1, :], ACT.Exp)
            f(par[:, 4, :], par[:, 4, :], ACT.Sin)
            f(par[:, 5, :], par[:, 5, :], ACT.Sin).then_inc(s5_par, 1)
            full(act, ("ab",))
            f(gs[0:8, 0, :], bank(("ab",))[0:8, 0:T], ACT.Exp, scale=-1.0).then_inc(gate_rows, 1)
            f(aexp[0:8, :], col("small", 1, 0, 8), ACT.Exp).then_inc(gate_rows, 1)
            act.wait_ge(gate_rows, 3)
            step(f(gs[0:8, 4, :], gs[0:8, 4, :], ACT.Exp))
            f(gs[0:8, 4, :], gs[0:8, 4, :], ACT.Ln, bias=onec[0:8, 0:1]).then_inc(gate_rows, 1)
            act.wait_ge(gate_rows, 5)
            f(gs[0:8, 2, :], gs[0:8, 4, :], ACT.Exp)
            f(gs[0:8, 3, 0:L], gs[0:8, 3, 0:L], ACT.Exp).then_inc(gate_rows, 1)
            for m in range(16):
                key = ("lin", "ev_in_a", m)
                full(act, key)
                if m < 12:
                    drain(f(zqkv[:, m, 3:3 + T], bank(key)[:, 0:T], ACT.Copy), key)
                else:
                    drain(f(zg[:, m - 12, :], bank(key)[:, 0:T], ACT.Silu), key)
                if 2 <= m < 14:
                    act.wait_ge(conv_done, m - 1)
                    f(qkv[:, m - 2, :], qkv[:, m - 2, :], ACT.Silu).then_inc(silu_done, 1)
            act.wait_ge(silu_done, 12)
            headnorm("l2", 8, T, 1.0, lambda i: qkv[:, i, :], lambda i: None)
            for t in range(NCH):
                copy_out(("trk", t), ketok[:, t, :], bank(("trk", t))[:, :])
                copy_out(("trv", t), vbtok[:, t, :], bank(("trv", t))[:, :])
            for gi, g in enumerate(G4):
                if gi >= 2:
                    drained(act, ("KK", G4[gi - 2]))
                full(act, ("DT", g))
                drain(f(dt_[:, gi % 2, :], bank(("DT", g))[:, :], ACT.Exp), ("DT", g))
            for gi, g in enumerate(G4):
                copy_out(("X1", g), xx[:, gi, :], bank(("X1", g))[:, :])
            for l in range(1, LEV):
                for gi, g in enumerate(G4):
                    copy_out(("T1", l, g), t1[:, gi, :], bank(("T1", l, g))[:, :])

            def o_copy(key, p, at, t):
                full(act, key)
                drain(f(oT[64 * p:64 * p + 64, :, t * 128:(t + 1) * 128],
                        blocks(key, 4, 64 * p, 64 * p + 64), ACT.Copy), key)

            def so_copy(name):
                for p in range(2):
                    key = ("sO", name, p)
                    full(act, key)
                    drain(f(oT[64 * p:64 * p + 64, :, L:T],
                            bank(key)[64 * p:64 * p + 64, 0:32].rearrange("p (c s) -> p c s", c=HC),
                            ACT.Copy), key)

            for t in range(NCH):
                copy_out(("u", t), utok, bank(("u", t))[:, :])
                for p in range(2):
                    o_copy(("o", t, p), p, 0, t)
            so_copy("gdn")

            def so_done(name):
                for p in range(2):
                    drained(act, ("sO", name, p))

            headnorm("gdn", HC, T, 1.0 / HD, lambda i: oT[:, i, :], lambda i: so_done("gdn") if i == 0 else None)
            for m in range(16):
                key = ("lin", "ev_in_b", m)
                b = bank(key)[:, 0:T]
                full(act, key)
                if m < 4:
                    drain(f(zq[:, m, :], b, ACT.Silu), key)
                elif m < 8:
                    f(zf[:, m - 4, :], b, ACT.Sigmoid)
                    drain(f(zk[:, m - 4, :], b, ACT.Sigmoid, scale=-1.0), key)
                elif m < 12:
                    drain(f(zi[:, m - 8, :], b, ACT.Copy), key)
                else:
                    drain(f(zh[:, m - 12, :], b, ACT.Silu), key)
            act.wait_ge(fk_ready, HC)
            f(lf, zf[:, :, 0:L], ACT.Ln).then_inc(lf_ready, 1)
            act.wait_ge(dec_ready, 2)
            f(qx, d1, ACT.Exp).then_inc(exp_ready, 1)
            f(kx, d1, ACT.Exp, scale=-1.0).then_inc(exp_ready, 1)
            f(qin, bcs, ACT.Exp).then_inc(exp_ready, 1)
            f(ko, d2, ACT.Exp).then_inc(exp_ready, 1)
            for t in range(NCH):
                copy_out(("htk", t), hkt[:, t, :], bank(("htk", t))[:, :])
                copy_out(("htv", t), hvt[:, t, :], bank(("htv", t))[:, :])
            act.wait_ge(mix_ready, HC)
            for t, p in G4:
                o_copy(("ho", (t, p)), p, 0, t)
            so_copy("hgrn")
            headnorm("hgrn", HC, T, 1.0 / HD, lambda i: oT[:, i, :], lambda i: so_done("hgrn") if i == 0 else None)
            squares("ev_out")

            def memory(l):
                act.wait_ge(memx_in, 16 * (l + 1))
                act.wait_ge(hg_stored if l == 0 else kv_stored, 32)
                full(act, ("lin", "ev_out" if l == 0 else "od_out", KC - 1))
                for m in range(KC):
                    f(mh[:, m, :], h[:, m, 0:NM], ACT.Square).then_inc(msq_ready, 1)
                norm(norms.index(("memkv", l)))
                for m in range(MH):
                    copy_out(("lin", f"memk{l}", m), mk[:, m, :], bank(("lin", f"memk{l}", m))[:, 0:NM])
                headnorm(f"memk{l}", MH, NM, 1.0 / 128, lambda i: mk[:, i, :],
                         lambda i: drained(act, ("lin", f"memk{l}", i)))
                for m in range(MH):
                    copy_out(("lin", f"memv{l}", m), mv[:, m, :], bank(("lin", f"memv{l}", m))[:, 0:NM])
                for t in range(2):
                    copy_out(("mvt", l, t), mvt[:, t, :], bank(("mvt", l, t))[:, :])
                norm(norms.index(("mem", l)))
                for m in range(MH):
                    copy_out(("lin", f"wq{l}", m), mq[:, m, :], bank(("lin", f"wq{l}", m))[:, 0:T])
                headnorm(f"memq{l}", MH, T, 1.0 / 128, lambda i: mq[:, i, :],
                         lambda i: drained(act, ("lin", f"wq{l}", i)))
                attend(f"mem{l}", MH, 128)
                drained(act, ("mxb", f"mem{l}", 0))
                f(msml[:, 1, :], msml[:, 0, :], ACT.Exp).then_inc(pp_ready, 1)
                squares(f"wo{l}")

            def ffn(l):
                norm(norms.index(("ffn", l)))
                act.wait_ge(fpads, l + 1)
                for i in range(FT + 1):
                    if i < FT:
                        key = ("lin", f"gu{l}", 2 * i)
                        full(act, key)
                        n = l * FT + i
                        if i >= 3:
                            act.wait_ge(fconv_done, n - 2)
                            act.wait_ge(fcopy_done, l * (FT + 1) + i - 2)
                        drain(f(gb[:, i % 3, 2:2 + T], bank(key)[:, 0:T], ACT.Copy), key)
                    if i >= 1:
                        n = l * FT + i - 1
                        act.wait_ge(fconv_done, n + 1)
                        if i >= 3:
                            drained(act, ("lin", f"gu{l}", 2 * (i - 3) + 1))
                        f(csil[:, (i - 1) % 2, :], cacc[:, (i - 1) % 2, :], ACT.Silu).then_inc(fsilu_done, 1)
                if l == 0:
                    squares("down0")

            memory(0)
            ffn(0)
            norm(norms.index(("mix", 1)))
            act.wait_ge(mem_stored, 32)
            for m in range(16):
                key = ("lin", "od_in", m)
                copy_out(key, zo[:, m, :], bank(key)[:, 0:T])
            headnorm("moba", 8, T, 1.0 / HD, lambda i: zo[:, i, :],
                     lambda i: drained(act, ("lin", "od_in", i)))
            for t in range(2):
                copy_out(("vt", t), ovt[:, t, :], bank(("vt", t))[:, :])
            copy_out(("bx",), bxs, bank(("bx",))[0:8, 0:512])
            copy_out(("bs",), bsp, bank(("bs",))[:, 0:64])
            attend("moba", H, 64)
            act.wait_ge(ssub_ready, 1)
            f(spp, ssc, ACT.Exp)
            f(gsm[:, 4, :], gsm[:, 3, :], ACT.Exp).then_inc(pp_ready, 1)
            act.wait_ge(kv_stored, 32)
            for c in range(HC):
                drained(act, ("s5y", c))
                f(ygl[:, c, :], tmpy[:, c, :], ACT.Gelu_apprx_tanh).then_inc(s5_gl2, 1)
            for c in range(HC):
                key = ("lin", "glu", 2 * c + 1)
                full(act, key)
                if c >= 2:
                    drained(act, ("lin", "glu", 2 * (c - 2)))
                drain(f(tmp[:, c % 2, :], bank(key)[:, 0:T], ACT.Sigmoid), key)
            squares("od_out")
            memory(1)
            ffn(1)

        @block.tensor
        def _(pe):
            at = [0]

            def begin(key):
                assert order[at[0]] == key, (order[at[0]], key)
                if at[0] >= NBANK:
                    pe.wait_ge(psum_free[at[0] % NBANK], at[0] // NBANK)
                return bank(key)

            def end(ins):
                ins.then_inc(psum_full, 1)
                at[0] += 1

            def mm(out, lhsT, rhs, start=True, stop=True):
                return nc.tensor.matmul(out, lhsT, rhs, start=start, stop=stop, skip_group_check=True)

            def tr(out, in_):
                return nc.tensor.transpose(out, in_, ident)

            def norm(i):
                kind, l = norms[i]
                w = NM if kind == "memkv" else T
                b = begin(("ss", kind, l))
                src = mh if kind == "memkv" else sq
                for k in range(KC):
                    if kind == "memkv":
                        pe.wait_ge(msq_ready, KC * l + k + 1)
                    else:
                        pe.wait_ge(sq_ready, KC * xnorms.index((kind, l)) + k + 1)
                    ins = mm(b[:, 0:w], ones, src[:, k, 0:w], k == 0, k == KC - 1)
                end(ins)

            def hready(i):
                return lambda k: pe.wait_ge(h_ready, KC * i + k + 1)

            def lin(name, m, kc, per_slot, src, w, ready=None):
                b = begin(("lin", name, m))
                s = slot_of[(name, m)]
                if m % per_slot == 0:
                    pe.wait_ge(ring_full[s % SLOTS], slot_value[s])
                for k in range(kc):
                    if ready and m == 0:
                        ready(k)
                    o = ((m % per_slot) * kc + k) * 128
                    ins = mm(b[:, 0:w], ring[:, s % SLOTS, o:o + 128], src[:, k, 0:w], k == 0, k == kc - 1)
                end(ins)

            def headnorm(name, n, w, lhsT):
                base = hn_no[(name, 0)]
                for i in range(n):
                    b = begin(("hn", name, i))
                    pe.wait_ge(hsq_ready, base + i + 1)
                    end(mm(b[:, 0:w], lhsT, hsq[:, (base + i) % 2, 0:w]))

            def transposes(key, srcs):
                b = begin(key)
                for j, v in enumerate(srcs):
                    ins = tr(b[:, 128 * j:128 * (j + 1)], v)
                end(ins)

            def attend(name, n, hd, q, k, vt):
                pbuf, ptb = att_buf[name]
                for i in range(n + 2):
                    if i < n:
                        b = begin(("S", name, i))
                        p0, c = (0, i) if hd == 128 else (64 * (i % 2), i // 2)
                        for qt in range(2):
                            ins = mm(b[:, qt * L:(qt + 1) * L], q[p0:p0 + hd, c, qt * 128:(qt + 1) * 128],
                                     k[p0:p0 + hd, c, 0:L])
                        end(ins)
                    if 0 <= i - 1 < n:
                        b = begin(("PT", name, i - 1))
                        pe.wait_ge(p_ready, at_no[(name, i - 1)] + 1)
                        for kt in range(2):
                            for qt in range(2):
                                ins = tr(b[:, kt * L + qt * 128:kt * L + (qt + 1) * 128],
                                         pbuf[:, (i - 1) % 2, qt * L + kt * 128:qt * L + (kt + 1) * 128])
                        end(ins)
                    if 0 <= i - 2 < n:
                        j = i - 2
                        b = begin(("O", name, j))
                        drained(pe, ("PT", name, j))
                        p0 = 0 if hd == 128 else 64 * (j % 2)
                        for kt in range(2):
                            ins = mm(b[p0:p0 + hd, 0:L], vt[:, kt, j * hd:(j + 1) * hd],
                                     ptb[:, j % 2, kt * L:(kt + 1) * L], kt == 0, kt == 1)
                        end(ins)

            def softmax_over_keys(name, mx, dg, n, pp, w):
                i = ["mem0", "moba", "mem1"].index(name)
                b = begin(("mxt", name, 0))
                pe.wait_ge(mx_ready, i + 1)
                end(tr(b[0:n, 0:128], mx))
                b = begin(("mxb", name, 0))
                pe.wait_ge(dg_ready, i + 1)
                end(mm(b[:, 0:n], cst("ones", p=n), dg))
                b = begin(("sum", name, 0))
                pe.wait_ge(pp_ready, i + 1)
                end(mm(b[:, 0:w], ones, pp))

            def state_update(name, w2, n):
                pe.wait_ge(w_ready, n)
                for c in range(HC):
                    b = begin(("su", name, c))
                    end(mm(b[:, :], bd, w2[:, c, :, :].rearrange("p s v -> p (s v)")))

            def state_out(name, st, q, n):
                pe.wait_ge(sst_ready, 4 * n)
                for p in range(2):
                    b = begin(("sO", name, p))
                    for c in range(HC):
                        for s in range(NS):
                            ins = mm(b[64 * p:64 * p + 64, c * NS + s:c * NS + s + 1],
                                     st[64 * p:64 * p + 64, c, s, :], q[64 * p:64 * p + 64, c, L + s:L + s + 1])
                    end(ins)

            pe.wait_ge(con_in, 16)
            norm(0)
            b = begin(("ab",))
            pe.wait_ge(vec_in, 16)
            for k in range(KC):
                hready(0)(k)
                ins = mm(b[0:40, 0:T], cols("w_ab", 40, 40 * k), h[:, k, :], k == 0, k == KC - 1)
            end(ins)
            for m in range(16):
                lin("ev_in_a", m, KC, 2, h, T)
            headnorm("l2", 8, T, bd)
            pe.wait_ge(gate_rows, 6)
            for c in range(HC):
                for name, r, w in (("bcB", 0, T), ("bcG", 2, T), ("bcL", 3, L)):
                    b = begin((name, c))
                    end(mm(b[:, 0:w], cst("selc", i=c, p=8), gs[0:8, r, 0:w]))
            for t in range(NCH):
                drained(pe, ("bcL", HC - 1))
                transposes(("trk", t), [ke[:, c, t * 128:(t + 1) * 128] for c in range(HC)])
                transposes(("trv", t), [vb[:, c, t * 128:(t + 1) * 128] for c in range(HC)])
            kn = qkv[:, 4:8, :]
            for gi, (t, p) in enumerate(G4):
                ts, ps = slice(t * 128, (t + 1) * 128), slice(64 * p, 64 * p + 64)
                b = begin(("DT", (t, p)))
                for c in range(HC):
                    hh_, o = 2 * c + p, b[:, c * 128:(c + 1) * 128]
                    mm(o, cst("selh", i=hh_, p=8), gs[0:8, 4, ts], True, False)
                    mm(o, gs[0:8, 4, ts], cst("nselh", i=hh_, p=8), False, False)
                    ins = mm(o, ident, cst("neg"), False, True)
                end(ins)
                b = begin(("QK", (t, p)))
                for c in range(HC):
                    ins = mm(b[:, c * 128:(c + 1) * 128], kn[ps, c, ts], qkv[ps, c, ts])
                end(ins)
                b = begin(("KK", (t, p)))
                for c in range(HC):
                    ins = mm(b[:, c * 128:(c + 1) * 128], kn[ps, c, ts], kb[ps, c, ts])
                end(ins)

            def blk(v, gi, c):
                return v[:, gi, c * 128:(c + 1) * 128]

            for gi, g in enumerate(G4):
                pe.wait_ge(xt_ready, gi + 1)
                transposes(("X1", g), [blk(xt, gi, c) for c in range(HC)])
            for l in range(1, LEV):
                for gi, g in enumerate(G4):
                    n = (l - 1) * 4 + gi
                    b = begin(("T1", l, g))
                    pe.wait_ge(ml_ready, n + 1)
                    drained(pe, ("X1", g) if l == 1 else ("Z", l - 1, g))
                    for c in range(HC):
                        ins = mm(b[:, c * 128:(c + 1) * 128], blk(ml, n % 2, c), blk(xx, gi, c))
                    end(ins)
                for gi, g in enumerate(G4):
                    b = begin(("ZT", l, g))
                    drained(pe, ("T1", l, g))
                    if l > 1:
                        drained(pe, ("ZT", l - 1, g))
                    for c in range(HC):
                        ins = mm(b[:, c * 128:(c + 1) * 128], blk(t1, gi, c), blk(xt, gi, c))
                    end(ins)
                    if l < LEV - 1:
                        b = begin(("Z", l, g))
                        for c in range(HC):
                            ins = mm(b[:, c * 128:(c + 1) * 128], blk(xt, gi, c), blk(t1, gi, c))
                        end(ins)
            for g in G4:
                drained(pe, ("ZT", LEV - 1, g))
            for t in range(NCH):
                ts = slice(t * 128, (t + 1) * 128)
                if t:
                    drained(pe, ("S", "gdn", t - 1))
                    for p in range(2):
                        ps = slice(64 * p, 64 * p + 64)
                        b = begin(("ks", p))
                        for c in range(HC):
                            ins = mm(b[:, c * 64:(c + 1) * 64], bk[ps, c, ts], sg[ps, c, :])
                        end(ins)
                    drained(pe, ("ks", 1))
                b = begin(("u", t))
                for hh_ in range(H):
                    cs = slice(hh_ * 64, (hh_ + 1) * 64)
                    ins = mm(b[:, cs], blk(xt, 2 * t + hh_ % 2, hh_ // 2), (rhst if t else vbtok[:, 0, :])[:, cs])
                end(ins)
                drained(pe, ("u", t))
                for p in range(2):
                    ps = slice(64 * p, 64 * p + 64)
                    b = begin(("o", t, p))
                    for c in range(HC):
                        hh_, o = 2 * c + p, b[ps, c * 128:(c + 1) * 128]
                        if t:
                            mm(o, sg[ps, c, :], qe[ps, c, ts], True, False)
                        ins = mm(o, utok[:, hh_ * 64:(hh_ + 1) * 64], blk(qkd, 2 * t + p, c), t == 0, True)
                    end(ins)
                b = begin(("S", "gdn", t))
                for hh_ in range(H):
                    ps, cs = slice(64 * (hh_ % 2), 64 * (hh_ % 2) + 64), slice(hh_ * 64, (hh_ + 1) * 64)
                    ins = mm(b[ps, (hh_ // 2) * 64:(hh_ // 2 + 1) * 64], ketok[:, t, cs], utok[:, cs])
                end(ins)
            state_update("gdn", ws2, 2)
            state_out("gdn", sgs, qkv, 1)
            headnorm("gdn", HC, T, bd)
            for m in range(16):
                lin("ev_in_b", m, KC, 2, h, T)
            pe.wait_ge(hg_dve, 2)
            pe.wait_ge(hg_pool, 3)
            for t in range(NCH):
                ts = slice(t * 128, (t + 1) * 128)
                transposes(("htk", t), [ko[:, c, ts] for c in range(HC)])
                drained(pe, ("lin", "ev_in_b", 11))
                transposes(("htv", t), [zi[:, c, ts] for c in range(HC)])
            for t, p in G4:
                ts, ps = slice(t * 128, (t + 1) * 128), slice(64 * p, 64 * p + 64)
                b = begin(("att", (t, p)))
                for c in range(HC):
                    ins = mm(b[:, c * 128:(c + 1) * 128], kx[ps, c, ts], qx[ps, c, ts])
                end(ins)
            for t in range(NCH):
                drained(pe, ("htk", t))
                drained(pe, ("htv", t))
            for k in range(L // HCK):
                t, r = k // 4, k % 4
                rs_ = slice(32 * r, 32 * r + 32)
                b = begin(("kv", k))
                for hh_ in range(H):
                    ps, cs = slice(64 * (hh_ % 2), 64 * (hh_ % 2) + 64), slice(hh_ * 64, (hh_ + 1) * 64)
                    ins = mm(b[ps, (hh_ // 2) * 64:(hh_ // 2 + 1) * 64], hkt[rs_, t, cs], hvt[rs_, t, cs])
                end(ins)
            drained(pe, ("kv", 7))
            for gi, (t, p) in enumerate(G4):
                ps = slice(64 * p, 64 * p + 64)
                b = begin(("ho", (t, p)))
                drained(pe, ("att", (t, p)))
                for c in range(HC):
                    hh_ = 2 * c + p
                    ins = mm(b[ps, c * 128:(c + 1) * 128], hvt[:, t, hh_ * 64:(hh_ + 1) * 64],
                             blk(attb, gi, c), True, False)
                    for r in range(4):
                        k = 4 * t + r
                        if k:
                            ins = mm(b[ps, c * 128 + 32 * r:c * 128 + 32 * r + 32], SH[k][ps, c, :],
                                     qin[ps, c, 32 * k:32 * k + 32], False, r == 3)
                end(ins)
            state_update("hgrn", hws2, 3)
            state_out("hgrn", shs, zq, 2)
            headnorm("hgrn", HC, T, bd)
            for m in range(KC):
                lin("ev_out", m, KC, 2, mix, T, lambda k: pe.wait_ge(mix_ready, k + 1))

            def memory(l):
                i = norms.index(("memkv", l))
                norm(i)
                for m in range(MH):
                    lin(f"memk{l}", m, KC, 2, mh, NM, hready(i))
                headnorm(f"memk{l}", MH, NM, ones)
                for m in range(MH):
                    lin(f"memv{l}", m, KC, 2, mh, NM)
                for t in range(2):
                    drained(pe, ("lin", f"memv{l}", MH - 1))
                    transposes(("mvt", l, t), [mv[:, hh_, t * 128:(t + 1) * 128] for hh_ in range(MH)])
                norm(i + 1)
                for m in range(MH):
                    lin(f"wq{l}", m, KC, 2, h, T, hready(i + 1))
                headnorm(f"memq{l}", MH, T, ones)
                pe.wait_ge(hn_done, hn_no[(f"memq{l}", MH - 1)] + 1)
                for t in range(2):
                    drained(pe, ("mvt", l, t))
                attend(f"mem{l}", MH, 128, mq, mk, mvt)
                b = begin(("sc", f"mem{l}", 0))
                for s in range(NS):
                    n = slot_of[(f"ck{l}", s // 2)]
                    if s % 2 == 0:
                        pe.wait_ge(ring_full[n % SLOTS], slot_value[n])
                    for hh_ in range(MH):
                        for t in range(2):
                            o = (s % 2) * 1024 + hh_ * 256 + t * 128
                            i_ = (s * MH + hh_) * 2 + t
                            ins = mm(b[:, i_:i_ + 1], ring[:, n % SLOTS, o:o + 128], mq[:, hh_, L + s:L + s + 1])
                end(ins)
                softmax_over_keys(f"mem{l}", msml[:, 2, 0:32], msml[0:32, 3, 0:32], 32, msml[:, 1, :], 64)
                b = begin(("so", f"mem{l}", 0))
                for s in range(NS):
                    n = slot_of[(f"cv{l}", s // 2)]
                    if s % 2 == 0:
                        pe.wait_ge(ring_full[n % SLOTS], slot_value[n])
                    for hh_ in range(MH):
                        for t in range(2):
                            o = (s % 2) * 1024 + hh_ * 256 + t * 128
                            i_ = (s * MH + hh_) * 2 + t
                            ins = mm(b[:, hh_ * NS + s:hh_ * NS + s + 1], ring[:, n % SLOTS, o:o + 128],
                                     msml[:, 1, i_:i_ + 1], t == 0, t == 1)
                end(ins)
                for hh_ in range(MH):
                    drained(pe, ("O", f"mem{l}", hh_))
                drained(pe, ("so", f"mem{l}", 0))
                for m in range(KC):
                    lin(f"wo{l}", m, MH, 4, mix, T)

            def ffn(l):
                i = norms.index(("ffn", l))
                norm(i)
                for m in range(2 * FT):
                    lin(f"gu{l}", m, KC, 2, h, T, hready(i))
                for m in range(KC):
                    lin(f"down{l}", m, FT, 1, act_, T, lambda k: drained(pe, ("lin", f"gu{l}", 2 * k + 1)))

            memory(0)
            ffn(0)
            norm(norms.index(("mix", 1)))
            for m in range(16):
                lin("od_in", m, KC, 2, h, T, hready(norms.index(("mix", 1))))
            headnorm("moba", 8, T, bd)
            for m in range(8, 12):
                drained(pe, ("lin", "od_in", m))
            for t in range(2):
                transposes(("vt", t), [zo[:, 8 + c, t * 128:(t + 1) * 128] for c in range(HC)])
            b = begin(("bx",))
            pe.wait_ge(relb_ready, 1)
            end(mm(b[0:8, :], relb[0:33, :], cst("hotx", 512, p=33)))
            b = begin(("bs",))
            for g in range(PAGES):
                ins = mm(b[:, 8 * g:8 * g + 8], con[0:32, CON["hots"] + 128 * g:CON["hots"] + 128 * (g + 1)],
                         relb[0:32, :])
            end(ins)
            pe.wait_ge(hn_done, hn_no[("moba", 7)] + 1)
            for t in range(2):
                drained(pe, ("vt", t))
            attend("moba", H, 64, zo[:, 0:4, :], zo[:, 4:8, :], ovt)
            b = begin(("sc", "moba", 0))
            pe.wait_ge(qbd_ready, 1)
            for s in range(NS):
                for g in range(PAGES):
                    n = slot_of[("pk", 2 * s + g // 4)]
                    if g % 4 == 0:
                        pe.wait_ge(ring_full[n % SLOTS], slot_value[n])
                    for c in range(HC):
                        o, i_ = (g % 4) * 512 + c * 128, (s * PAGES + g) * H + 2 * c
                        ins = mm(b[:, i_:i_ + 2], ring[:, n % SLOTS, o:o + 128], qbd[:, c, s, :])
                    if g % 4 == 3 and (s, g) != (NS - 1, PAGES - 1):
                        ins.then_inc(pages_used, 1)
            end(ins)
            b = begin(("self",))
            pe.wait_ge(qk_ready, 1)
            end(mm(b[:, 0:64], ones, qkp.rearrange("p c s t -> p (c s t)")))
            b = begin(("gate",))
            drained(pe, ("sc", "moba", 0))
            end(mm(b[:, :], ones, sraw))
            softmax_over_keys("moba", gsm[:, 5, :], gsm[0:64, 6, :], 64, spp, 512)
            b = begin(("so", "moba", 0))
            for s in range(NS):
                for half in range(2):
                    n = slot_of[("pv", 2 * s + half)]
                    pe.wait_ge(ring_full[n % SLOTS], slot_value[n])
                for c in range(HC):
                    for g in range(PAGES):
                        n = slot_of[("pv", 2 * s + g // 4)]
                        o, i_ = (g % 4) * 512 + c * 128, (s * PAGES + g) * H + 2 * c
                        j = (s * HC + c) * 2
                        ins = mm(b[:, j:j + 2], ring[:, n % SLOTS, o:o + 128], spp[:, i_:i_ + 2],
                                 g == 0, g == PAGES - 1)
                if s < NS - 1:
                    ins.then_inc(pages_used, 1)
            end(ins)
            pe.wait_ge(s5_in, 48)
            for c in range(HC):
                drained(pe, ("lin", "od_in", 12 + c))
            for j in range(4):
                b = begin(("s5s", j))
                js = slice(32 * j, 32 * j + 32)
                for c in range(HC):
                    for q in range(2):
                        i_ = (c * 2 + q) * NS
                        ins = mm(b[:, i_:i_ + NS], s5b[js, q, c, :], zo[js, 12 + c, L:T])
                end(ins)

            def y_tile(c):
                b = begin(("s5y", c))
                if c == 0:
                    pe.wait_ge(s5_hs, 2)
                for j in range(4):
                    n = 4 * c + j
                    o = b[32 * j:32 * j + 32, 0:L]
                    pe.wait_ge(s5_hr, n + 1)
                    pe.wait_ge(s5_hi, 2 * n + 1)
                    mm(o, s5cp[:, 0, n, :], hh[:, n % NHB, 0, :], True, False)
                    mm(o, s5cp[:, 1, n, :], hh[:, n % NHB, 1, :], False, True)
                    o = b[32 * j:32 * j + 32, L:T]
                    mm(o, s5c[:, 0, n, :], hsS[:, 0, n, :], True, False)
                    ins = mm(o, s5cp[:, 2, n, :], hsS[:, 1, n, :], False, True)
                end(ins)

            for n in range(NT):
                c, js = n // 4, slice(32 * (n % 4), 32 * (n % 4) + 32)
                b = begin(("s5x", n))
                for q in range(2):
                    ins = mm(b[:, q * L:(q + 1) * L], s5b[js, q, c, :], zo[js, 12 + c, 0:L])
                end(ins)
                if n >= 4 and n % 4 == 0:
                    y_tile(n // 4 - 1)
            y_tile(3)
            for m in range(8):
                lin("glu", m, HC, 4, ygl, T, lambda k: pe.wait_ge(s5_gl2, k + 1))
            for j in range(H):
                drained(pe, ("O", "moba", j))
            for c in range(HC):
                drained(pe, ("lin", "glu", 2 * c))
            pe.wait_ge(samp_o, 1)
            for m in range(KC):
                lin("od_out", m, KC, 2, mix, T)
            memory(1)
            ffn(1)
            assert at[0] == len(order)

        @block.vector
        def _(dve):
            step = Steps(dve, dve_step)
            V = nc.vector

            def tt(out, a, b, op):
                return V.tensor_tensor(out, a, b, op)

            def stt(out, a, s, b, op0, op1):
                return V.scalar_tensor_tensor(out, a, s, b, op0, op1)

            def norm(i):
                kind, l = norms[i]
                w = NM if kind == "memkv" else T
                dst = mh if kind == "memkv" else h
                src = h if kind == "memkv" else x
                dve.wait_ge(r_ready, i + 1)
                for k in range(KC):
                    stt(dst[:, k, 0:w], src[:, k, 0:w], col(NORM_G[kind], KC * l + k), rs[:, 0:w],
                        ALU.mult, ALU.mult).then_inc(h_ready, 1)

            def residual(name):
                for m in range(KC):
                    key = ("lin", name, m)
                    full(dve, key)
                    drain(tt(x[:, m, :], x[:, m, :], bank(key)[:, 0:T], ALU.add), key)

            def headnorm(name, n, w, src, gain, dst, after=None):
                base = hn_no[(name, 0)]
                for i in range(n):
                    dve.wait_ge(hr_ready, base + i + 1)
                    stt(dst(i), src(i), gain(i), hr[:, (base + i) % 2, 0:w], ALU.mult, ALU.mult).then_inc(hn_done, 1)
                    if after:
                        dve.wait_ge(hn_done, base + i + 1)
                        after(i)

            def attend(name, n, hd, scale):
                pbuf, _ = att_buf[name]

                def scores(i):
                    j = at_no[(name, i)]
                    key = ("S", name, i)
                    full(dve, key)
                    v = pbuf[:, i % 2, :].rearrange("p (q k) -> p q k", q=2)
                    sv = bank(key)[:, :].rearrange("p (q k) -> p q k", q=2)
                    if i >= 2:
                        full(dve, ("PT", name, i - 2))
                    if hd == 128:
                        drain(V.tensor_scalar(v, sv, scale, None, ALU.mult), key)
                    else:
                        bv = hank[:, i, 255:256]
                        bv = bass.AP(tensor=bv.tensor, offset=bv.offset, ap=[list(bv.ap[0]), [128, 2], [-1, L]])
                        drain(stt(v, sv, scale, bv, ALU.mult, ALU.add), key)
                    drained(dve, key)
                    step(V.tensor_reduce(smx[:, j % 2, 2, 0:2], v, AX, ALU.max))
                    V.tensor_scalar(smx[:, j % 2, 0, 0:2], smx[:, j % 2, 2, 0:2], -1.0, None,
                                    ALU.mult).then_inc(smax_ready, 1)

                def normalise(i):
                    j = at_no[(name, i)]
                    dve.wait_ge(p_exp, j + 1)
                    step(V.reciprocal(smx[:, j % 2, 3, 0:2], smx[:, j % 2, 1, 0:2]))
                    for qt in range(2):
                        v = pbuf[:, i % 2, qt * L:(qt + 1) * L]
                        ins = V.tensor_scalar(v, v, smx[:, j % 2, 3, qt:qt + 1], None, ALU.mult)
                    ins.then_inc(p_ready, 1)

                for i in range(n + 1):
                    if i < n:
                        scores(i)
                    if i >= 1:
                        normalise(i - 1)

            dve.wait_ge(vec_in, 16)
            V.memset(epst[:, :], EPS).then_inc(eps_ready, 1)
            step(V.memset(onec[:, :], 1.0))
            step(V.tensor_copy(relb[0:32, :], cols("relb", H, 0, 0, 32)))
            V.memset(relb[32:33, :], BIG).then_inc(relb_ready, 1)
            lb = lambda i: cols("lb", 4, 4 * i)
            step(tt(lbt[:, 5, :], lb(0), lb(1), ALU.max))
            step(tt(lbt[:, 6, :], lbt[:, 5, :], lb(2), ALU.max))
            for i in range(3):
                ins = tt(lbt[:, i, :], lb(i), lbt[:, 6, :], ALU.subtract)
            ins.then_inc(lb_step, 1)
            dve.wait_ge(lb_step, 2)
            step(tt(lbt[:, 5, :], lbt[:, 0, :], lbt[:, 1, :], ALU.add))
            step(tt(lbt[:, 6, :], lbt[:, 5, :], lbt[:, 2, :], ALU.add))
            step(V.reciprocal(lbt[:, 7, :], lbt[:, 6, :]))
            step(tt(lbt[:, 3, :], lbt[:, 0, :], lbt[:, 7, :], ALU.mult))
            step(V.tensor_scalar(lbt[:, 4, :], lbt[:, 3, :], -1.0, 1.0, ALU.mult, ALU.add))
            dt0, lrd, th, k0, r_s, r_c = [par[:, i, :] for i in range(6)]
            lr, li = cols("s5_re", NT), cols("s5_im", NT)
            dve.wait_ge(s5_par, 1)
            step(tt(lrd, lr, dt0, ALU.mult))
            step(tt(th, li, dt0, ALU.mult))
            hi_, mid_ = 6.28125, 0.0019350051879882812
            lo_ = TWO_PI - hi_ - mid_
            for add, r in ((0.0, r_s), (0.25, r_c)):
                step(V.tensor_scalar(k0, th, 1.0 / TWO_PI, add, ALU.mult, ALU.add))
                step(V.tensor_scalar(k0, k0, MAGIC, None, ALU.add))
                step(V.tensor_scalar(k0, k0, -MAGIC, None, ALU.add))
                step(stt(r, k0, -hi_, th, ALU.mult, ALU.add))
                step(stt(r, k0, -mid_, r, ALU.mult, ALU.add))
                step(stt(r, k0, -lo_, r, ALU.mult, ALU.add))
                step(V.tensor_scalar(r, r, add * TWO_PI, 3.1415925, ALU.add, ALU.min))
                ins = V.tensor_scalar(r, r, -3.1415925, None, ALU.max)
                if add == 0.0:
                    step(ins)
            ins.then_inc(s5_par, 1)
            norm(0)
            dve.wait_ge(s5_par, 3)
            mag, sn, cs_ = par[:, 1, :], par[:, 4, :], par[:, 5, :]
            ar, ai, den, nr, cr, ci, q1, q2, nci = [par[:, i, :] for i in range(6, 15)]
            step(tt(ar, mag, cs_, ALU.mult))
            step(tt(ai, mag, sn, ALU.mult))
            step(tt(q1, lr, lr, ALU.mult))
            step(tt(q2, li, li, ALU.mult))
            step(tt(q1, q1, q2, ALU.add))
            step(V.reciprocal(den, q1))
            step(V.tensor_scalar(nr, ar, -1.0, None, ALU.add))
            for out, a, b, c, d, op in ((cr, nr, lr, ai, li, ALU.add), (ci, ai, lr, nr, li, ALU.subtract)):
                step(tt(q1, a, b, ALU.mult))
                step(tt(q2, c, d, ALU.mult))
                step(tt(q1, q1, q2, op))
                step(tt(out, q1, den, ALU.mult))
            full(dve, ("ab",))
            dve.wait_ge(gate_rows, 2)
            step(V.tensor_scalar(gs[0:8, 1, :], bank(("ab",))[32:40, 0:T], col("small", 0, 32, 40), None, ALU.add))
            step(V.tensor_scalar(gs[0:8, 2, :], gs[0:8, 1, :], -1.0, None, ALU.mult))
            step(tt(gs[0:8, 4, :], gs[0:8, 1, :], gs[0:8, 2, :], ALU.min))
            drain(V.tensor_scalar(gs[0:8, 0, :], gs[0:8, 0, :], 1.0, None, ALU.add), ("ab",))
            drained(dve, ("ab",))
            V.reciprocal(gs[0:8, 0, :], gs[0:8, 0, :]).then_inc(gate_rows, 1)
            dve.wait_ge(gate_rows, 4)
            step(stt(gs[0:8, 1, :], gs[0:8, 1, :], 0.0, gs[0:8, 4, :], ALU.max, ALU.add))
            step(V.tensor_scalar(gs[0:8, 1, :], gs[0:8, 1, :], aexp[0:8, 0:1], -1.0, ALU.mult, ALU.mult))
            for t in range(NCH):
                ts = slice(t * 128, (t + 1) * 128)
                step(V.tensor_tensor_scan(gs[0:8, 4, ts], cst("ones", p=8), gs[0:8, 1, ts], 0.0, ALU.mult, ALU.add))
                step(V.tensor_scalar(gs[0:8, 3, ts], gs[0:8, 4, ts], -1.0,
                                     gs[0:8, 4, (t + 1) * 128 - 1:(t + 1) * 128], ALU.mult, ALU.add))
            V.tensor_copy(gs[0:8, 4, L:T], gs[0:8, 1, L:T]).then_inc(gate_rows, 1)
            dve.wait_ge(pads_ready, 2)
            dve.wait_ge(hist_in, 16)
            cw = lambda k, m: col("conv_w", 12 * k + m)
            for m in range(12):
                drained(dve, ("lin", "ev_in_a", m))
                o, os_ = qkv[:, m, 0:L], qkv[:, m, L:T]
                V.tensor_scalar(o, zqkv[:, m, 0:L], cw(0, m), None, ALU.mult)
                step(V.tensor_scalar(os_, ch[:, m, 0:8], cw(0, m), None, ALU.mult))
                for k in range(1, 4):
                    stt(o, zqkv[:, m, k:k + L], cw(k, m), o, ALU.mult, ALU.add)
                    v = ch[:, m, 8 * k:8 * k + 8] if k < 3 else zqkv[:, m, 3 + L:3 + T]
                    ins = stt(os_, v, cw(k, m), os_, ALU.mult, ALU.add)
                    if k < 3:
                        step(ins)
                ins.then_inc(conv_done, 1)
            headnorm("l2", 8, T, lambda i: qkv[:, i, :], lambda i: HD ** -0.5 if i < 4 else 1.0,
                     lambda i: qkv[:, i, :])
            dve.wait_ge(silu_done, 12)
            dve.wait_ge(hn_done, 8)
            for c in range(HC):
                full(dve, ("bcL", c))
                B, G, E_ = bank(("bcB", c))[:, 0:T], bank(("bcG", c))[:, 0:T], bank(("bcL", c))[:, 0:L]
                tt(vb[:, c, :], qkv[:, 8 + c, :], B, ALU.mult)
                drain(tt(kb[:, c, :], qkv[:, 4 + c, :], B, ALU.mult), ("bcB", c))
                drained(dve, ("bcB", c))
                tt(bk[:, c, :], kb[:, c, :], G, ALU.mult)
                tt(qe[:, c, :], qkv[:, c, :], G, ALU.mult)
                drain(V.tensor_copy(egc[:, c, :], G[:, L - 1:T]), ("bcG", c))
                drain(tt(ke[:, c, :], qkv[:, 4 + c, 0:L], E_, ALU.mult), ("bcL", c))
            dve.wait_ge(cvo_ready, 1)
            for gi, g in enumerate(G4):
                d = dt_[:, gi % 2, :]
                drained(dve, ("DT", g))
                full(dve, ("QK", g))
                drain(tt(qkd[:, gi, :], bank(("QK", g))[:, :], d, ALU.mult), ("QK", g))
                full(dve, ("KK", g))
                drain(tt(mt[:, gi, :], bank(("KK", g))[:, :], d, ALU.mult), ("KK", g))
                drained(dve, ("KK", g))
                m4 = mt[:, gi, :].rearrange("p (n k) -> p n k", n=4)
                x4 = xt[:, gi, :].rearrange("p (n k) -> p n k", n=4)
                step(stt(x4, m4, -1.0, four(cst("lev", i=0)), ALU.mult, ALU.mult))
                tt(x4, x4, four(ident), ALU.add).then_inc(xt_ready, 1)
            for l in range(1, LEV):
                for gi, g in enumerate(G4):
                    key = ("ZT", l, g)
                    last = l == LEV - 1
                    full(dve, key if last else ("Z", l, g))
                    drain(tt(xt[:, gi, :], xt[:, gi, :], bank(key)[:, :], ALU.subtract), key)
                    if not last:
                        key = ("Z", l, g)
                        drain(tt(xx[:, gi, :], xx[:, gi, :], bank(key)[:, :], ALU.subtract), key)
            full(dve, ("S", "gdn", 0))
            drain(V.tensor_copy(sg[:, :, :], bank(("S", "gdn", 0))[:, 0:256].rearrange("p (c v) -> p c v", c=HC)),
                  ("S", "gdn", 0))
            for p in range(2):
                full(dve, ("ks", p))
                ap = lambda v: v.rearrange("p (c b v) -> p c b v", c=HC, b=2)[:, :, p, :]
                drain(tt(ap(rhst), ap(vbtok[:, 1, :]), bank(("ks", p))[:, 0:256].rearrange("p (c v) -> p c v", c=HC),
                         ALU.subtract), ("ks", p))
            full(dve, ("S", "gdn", 1))
            for c in range(HC):
                ins = stt(sg[:, c, :], sg[:, c, :], egc[:, c, 0:1], bank(("S", "gdn", 1))[:, c * 64:(c + 1) * 64],
                          ALU.mult, ALU.add)
            drain(ins, ("S", "gdn", 1))

            bc4 = lambda v: v.unsqueeze(3).broadcast_to([128, HC, NS, HD])
            bc3 = lambda v: v.unsqueeze(2).broadcast_to([128, NS, HD])

            def state_update(name, w1, st, k, n):
                for c in range(HC):
                    key = ("su", name, c)
                    full(dve, key)
                    drain(tt(w1[:, c], bank(key)[:, :].rearrange("p (s v) -> p s v", s=NS), bc3(k[:, c, L:T]),
                             ALU.mult), key)
                dve.wait_ge(sdec_ready, n)
                for c in range(HC):
                    drained(dve, ("su", name, c))
                    tt(st[:, c], st[:, c], w1[:, c], ALU.add).then_inc(sst_ready, 1)

            dve.wait_ge(sgs_in, 16)
            tt(ws1, sgs, bc4(bk[:, :, L:T]), ALU.mult).then_inc(w_ready, 1)
            dve.wait_ge(w_ready, 1)
            step(tt(ws2, cst("i2", 64).unsqueeze(1).unsqueeze(1).broadcast_to([128, HC, NS, HD]),
                    bc4(vb[:, :, L:T]), ALU.mult))
            tt(ws2, ws2, ws1, ALU.subtract).then_inc(w_ready, 1)
            state_update("gdn", ws1, sgs, qkv[:, 4:8, :], 1)

            def gated(gate, at):
                def after(i):
                    tt(mix[:, at + i, :], tmp[:, i % 2, :], gate[:, i, :], ALU.mult).then_inc(mix_ready, 1)
                return after

            for m in range(12, 16):
                drained(dve, ("lin", "ev_in_a", m))
            headnorm("gdn", HC, T, lambda i: oT[:, i, :], lambda i: col("gdn_norm"), lambda i: tmp[:, i % 2, :],
                     gated(zg, 0))
            for c in range(HC):
                drained(dve, ("lin", "ev_in_b", 4 + c))
                V.tensor_scalar(zk[:, c, :], zk[:, c, :], lbt[:, 4, c:c + 1], None, ALU.mult)
                V.tensor_scalar(zf[:, c, :], zf[:, c, :], lbt[:, 4, c:c + 1], lbt[:, 3, c:c + 1],
                                ALU.mult, ALU.add).then_inc(fk_ready, 1)
            dve.wait_ge(lf_ready, 1)
            for c in range(HC):
                ins = V.tensor_tensor_scan(bcs[:, c, :], rmask[:, :], lf[:, c, :], 0.0, ALU.mult, ALU.add)
            step(ins)
            ch4 = lambda v: v.rearrange("p c (k i) -> p (c k) i", i=HCK)
            mid, end_ = (HCK - 1) // 2, HCK - 1
            b4 = ch4(bcs)
            tt(ch4(d1), b4, b4[:, :, mid:mid + 1].broadcast_to([128, 32, HCK]), ALU.subtract).then_inc(dec_ready, 1)
            tt(ch4(d2), b4[:, :, end_:end_ + 1].broadcast_to([128, 32, HCK]), b4, ALU.subtract).then_inc(dec_ready, 1)
            dve.wait_ge(exp_ready, 2)
            for m in range(HC):
                drained(dve, ("lin", "ev_in_b", m))
            tt(qx, qx, zq[:, :, 0:L], ALU.mult).then_inc(hg_dve, 1)
            dve.wait_ge(fk_ready, HC)
            tt(kx, kx, zk[:, :, 0:L], ALU.mult).then_inc(hg_dve, 1)
            dve.wait_ge(att_zero, 1)
            for gi, g in enumerate(G4):
                full(dve, ("att", g))
                drain(V.copy_predicated(attb[:, gi, :].rearrange("p (n k) -> p n k", n=4),
                                        four(cst("cmask").bitcast(I32)),
                                        blocks(("att", g))), ("att", g))
            dve.wait_ge(hg_pool, 1)
            for k in range(8):
                key = ("kv", k)
                full(dve, key)
                kv = bank(key)[:, 0:256].rearrange("p (c v) -> p c v", c=HC)
                nxt = SH[(k + 1) % 8]
                if k:
                    drained(dve, ("kv", k - 1))
                    step(tt(nxt, SH[k], fl[:, :, k:k + 1].broadcast_to([128, HC, HD]), ALU.mult))
                    drain(tt(nxt, nxt, kv, ALU.add), key)
                else:
                    drain(V.tensor_copy(nxt, kv), key)
            state_update("hgrn", hws1, shs, zk, 2)
            headnorm("hgrn", HC, T, lambda i: oT[:, i, :], lambda i: col("hgrn_norm"), lambda i: tmp[:, i % 2, :],
                     gated(zh, 4))
            residual("ev_out")

            def memory(l):
                norm(norms.index(("memkv", l)))
                headnorm(f"memk{l}", MH, NM, lambda i: mk[:, i, :], lambda i: col("mem_gk", l),
                         lambda i: mk[:, i, :])
                norm(norms.index(("mem", l)))
                headnorm(f"memq{l}", MH, T, lambda i: mq[:, i, :], lambda i: col("mem_gq", l),
                         lambda i: mq[:, i, :])
                attend(f"mem{l}", MH, 128, 128 ** -0.5)
                name = f"mem{l}"
                s_, mx = msml[:, 0, :], msml[:, 2, 0:32]
                full(dve, ("sc", name, 0))
                drain(V.tensor_scalar(s_, bank(("sc", name, 0))[:, 0:64], 128 ** -0.5, None, ALU.mult),
                      ("sc", name, 0))
                drained(dve, ("sc", name, 0))
                V.tensor_reduce(mx, s_.rearrange("p (a t) -> p a t", t=2), AX, ALU.max).then_inc(mx_ready, 1)
                full(dve, ("mxt", name, 0))
                drain(V.tensor_reduce(msml[0:32, 4, 0:1], bank(("mxt", name, 0))[0:32, 0:128], AX, ALU.max),
                      ("mxt", name, 0))
                drained(dve, ("mxt", name, 0))
                V.tensor_scalar(msml[0:32, 3, 0:32], ident[0:32, 0:32], msml[0:32, 4, 0:1], None,
                                ALU.mult).then_inc(dg_ready, 1)
                full(dve, ("mxb", name, 0))
                s3 = s_.rearrange("p (a t) -> p a t", t=2)
                drain(tt(s3, s3, bank(("mxb", name, 0))[:, 0:32].unsqueeze(2).broadcast_to([128, 32, 2]),
                         ALU.subtract), ("mxb", name, 0))
                full(dve, ("sum", name, 0))
                drain(V.tensor_reduce(msml[:, 5, 0:32],
                                      bank(("sum", name, 0))[:, 0:64].rearrange("p (a t) -> p a t", t=2), AX,
                                      ALU.add), ("sum", name, 0))
                drained(dve, ("sum", name, 0))
                step(V.reciprocal(msml[:, 6, 0:32], msml[:, 5, 0:32]))
                full(dve, ("so", name, 0))
                drain(tt(mix[:, 0:4, L:T], bank(("so", name, 0))[:, 0:32].rearrange("p (h s) -> p h s", h=MH),
                         msml[:, 6, 0:32].rearrange("p (s h) -> p h s", h=MH), ALU.mult), ("so", name, 0))
                residual(f"wo{l}")

            def ffn(l):
                norm(norms.index(("ffn", l)))
                dve.wait_ge(fh_in, 16 * (l + 1))
                fw = lambda k, i: col("ffn_w", (l * 3 + k) * FT + i)
                for i in range(FT + 1):
                    if i < FT:
                        g, c = gb[:, i % 3, :], cacc[:, i % 2, :]
                        drained(dve, ("lin", f"gu{l}", 2 * i))
                        if i >= 2:
                            dve.wait_ge(fsilu_done, l * FT + i - 1)
                        fb = col("ffn_b", l * FT + i)
                        V.tensor_scalar(c[:, 0:L], g[:, 0:L], fw(0, i), fb, ALU.mult, ALU.add)
                        step(V.tensor_scalar(c[:, L:T], fh[:, i, 0:8], fw(0, i), fb, ALU.mult, ALU.add))
                        stt(c[:, 0:L], g[:, 1:1 + L], fw(1, i), c[:, 0:L], ALU.mult, ALU.add)
                        step(stt(c[:, L:T], fh[:, i, 8:16], fw(1, i), c[:, L:T], ALU.mult, ALU.add))
                        stt(c[:, 0:L], g[:, 2:2 + L], fw(2, i), c[:, 0:L], ALU.mult, ALU.add)
                        stt(c[:, L:T], g[:, 2 + L:2 + T], fw(2, i), c[:, L:T], ALU.mult,
                            ALU.add).then_inc(fconv_done, 1)
                    if i >= 1:
                        j = i - 1
                        key = ("lin", f"gu{l}", 2 * j + 1)
                        full(dve, key)
                        dve.wait_ge(fsilu_done, l * FT + j + 1)
                        drain(tt(act_[:, j, :], csil[:, j % 2, :], bank(key)[:, 0:T], ALU.mult), key)
                residual(f"down{l}")

            memory(0)
            ffn(0)
            norm(norms.index(("mix", 1)))
            ms = lambda v, c_: V.memset(v, c_)
            dve.wait_ge(ffn_stored, 16)
            ms(cosT[:, :, 0:1], 1.0)
            step(ms(sinT[:, :, 0:1], 0.0))
            c0, s0_, c1, s1_ = [t16[:, i, :] for i in range(4)]
            step(V.tensor_copy(c0, cs_))
            step(V.tensor_copy(s0_, sn))
            wt = lambda i, n: place(TABTMP + i * 2048, NT, n)[0]
            n = 1
            while n < L:
                bb = lambda v: v.unsqueeze(2).broadcast_to([128, NT, n])
                wa, wb, wc, wd = [wt(i, n) for i in range(4)]
                C_, S_ = cosT[:, :, 0:n], sinT[:, :, 0:n]
                tt(wa, C_, bb(c0), ALU.mult)
                tt(wb, S_, bb(s0_), ALU.mult)
                tt(wc, C_, bb(s0_), ALU.mult)
                step(tt(wd, S_, bb(c0), ALU.mult))
                tt(cosT[:, :, n:2 * n], wa, wb, ALU.subtract)
                step(tt(sinT[:, :, n:2 * n], wc, wd, ALU.add))
                n *= 2
                if n < L:
                    step(tt(c1, c0, c0, ALU.mult))
                    step(tt(q1, s0_, s0_, ALU.mult))
                    step(tt(s1_, c0, s0_, ALU.mult))
                    step(tt(c0, c1, q1, ALU.subtract))
                    step(V.tensor_scalar(s0_, s1_, 2.0, None, ALU.mult))
            headnorm("moba", 8, T, lambda i: zo[:, i, :],
                     lambda i: col("moba_gq") if i < 4 else col("moba_gk"), lambda i: zo[:, i, :])
            dve.wait_ge(s5_in, 48)
            full(dve, ("lin", "od_in", 15))
            cb = lambda v: v.unsqueeze(2).broadcast_to([128, NT, 32])
            w1_, w2_ = place(WTMP, NT, 32)[0], place(WTMP + 512, NT, 32)[0]
            step(tt(w1_, s5c[:, 0], cb(cr), ALU.mult))
            step(tt(w2_, s5c[:, 1], cb(ci), ALU.mult))
            step(tt(s5cp[:, 0], w1_, w2_, ALU.subtract))
            step(tt(w1_, s5c[:, 0], cb(ci), ALU.mult))
            step(tt(w2_, s5c[:, 1], cb(cr), ALU.mult))
            step(stt(s5cp[:, 1].rearrange("p a b -> p (a b)"), w1_.rearrange("p a b -> p (a b)"), -1.0,
                     w2_.rearrange("p a b -> p (a b)"), ALU.mult, ALU.subtract))
            step(V.tensor_scalar(s5cp[:, 2].rearrange("p a b -> p (a b)"), s5c[:, 1].rearrange("p a b -> p (a b)"),
                                 -1.0, None, ALU.mult))
            step(ms(qbd, 0.0))
            dve.wait_ge(hn_done, hn_no[("moba", 7)] + 1)
            for p in range(2):
                ps = slice(64 * p, 64 * p + 64)
                ins = V.tensor_copy(qbd[ps, :, :, p], zo[ps, 0:4, L:T])
            ins.then_inc(qbd_ready, 1)
            dve.wait_ge(qbd_ready, 1)
            tt(qkp, qbd, zo[:, 4:8, L:T].unsqueeze(3).broadcast_to([128, HC, NS, 2]), ALU.mult).then_inc(qk_ready, 1)
            drained(dve, ("bs",))
            dve.wait_ge(bias_in, 16)
            attend("moba", H, 64, HD ** -0.5)
            full(dve, ("sc", "moba", 0))
            drain(V.tensor_copy(sraw, bank(("sc", "moba", 0))[:, :]), ("sc", "moba", 0))
            drained(dve, ("sc", "moba", 0))
            spg = lambda v: v.rearrange("p (s n) -> p s n", s=NS)
            step(stt(spg(ssc), spg(sraw), HD ** -0.5, bsp.unsqueeze(1).broadcast_to([128, NS, 64]),
                     ALU.mult, ALU.add))
            full(dve, ("gate",))
            g5 = bank(("gate",))[:, :].rearrange("p (a b h) -> p a h b", a=32, b=2)
            drain(V.tensor_reduce(gt[:, 0:256].rearrange("p (a h) -> p a h", a=32), g5, AX, ALU.add), ("gate",))
            drained(dve, ("gate",))
            gv = gt[:, 0:256].rearrange("p (s b h) -> p s b h", s=NS, b=4)
            cnt = gt[:, 256:512].rearrange("p (s b h) -> p s b h", s=NS, b=4)
            cmp_ = gsm[:, 0, :].rearrange("p (s h) -> p s h", s=NS)
            for b in range(4):
                first = True
                for b2 in range(4):
                    if b2 == b:
                        continue
                    op = ALU.is_ge if b2 < b else ALU.is_gt
                    if first:
                        step(tt(cnt[:, :, b, :], gv[:, :, b2, :], gv[:, :, b, :], op))
                    else:
                        step(tt(cmp_, gv[:, :, b2, :], gv[:, :, b, :], op))
                        step(tt(cnt[:, :, b, :], cnt[:, :, b, :], cmp_, ALU.add))
                    first = False
            step(V.tensor_scalar(gt[:, 0:256], gt[:, 256:512], 3.0, BIG, ALU.is_ge, ALU.mult))
            s4 = ssc.rearrange("p (a b h) -> p a b h", a=32, b=2)
            step(tt(s4, s4, gt[:, 0:256].rearrange("p (a h) -> p a h", a=32).unsqueeze(2)
                    .broadcast_to([128, 32, 2, H]), ALU.add))
            V.tensor_reduce(gsm[:, 5, :].rearrange("p (s h) -> p s h", s=NS),
                            ssc.rearrange("p (s g h) -> p s h g", s=NS, g=PAGES), AX, ALU.max).then_inc(mx_ready, 1)
            full(dve, ("self",))
            sv = bank(("self",))[:, 0:64].rearrange("p (c s b) -> p s c b", c=HC, s=NS)
            sh_ = lambda v: v.rearrange("p (s c b) -> p s c b", s=NS, c=HC)
            drain(V.tensor_scalar(sh_(gsm[:, 1, :]), sv, HD ** -0.5, None, ALU.mult), ("self",))
            drained(dve, ("self",))
            step(tt(gsm[:, 2, :].rearrange("p (s h) -> p s h", s=NS), gsm[:, 1, :].rearrange("p (s h) -> p s h", s=NS),
                    cols("relb0", H).unsqueeze(1).broadcast_to([128, NS, H]), ALU.add))
            full(dve, ("mxt", "moba", 0))
            drain(V.tensor_reduce(gsm[0:64, 7, 0:1], bank(("mxt", "moba", 0))[0:64, 0:128], AX, ALU.max),
                  ("mxt", "moba", 0))
            drained(dve, ("mxt", "moba", 0))
            V.tensor_scalar(gsm[0:64, 6, :], ident[0:64, 0:64], gsm[0:64, 7, 0:1], None, ALU.mult).then_inc(dg_ready, 1)
            full(dve, ("mxb", "moba", 0))
            drain(tt(gsm[:, 8, :], gsm[:, 2, :], bank(("mxb", "moba", 0))[:, 0:64], ALU.max), ("mxb", "moba", 0))
            drained(dve, ("mxb", "moba", 0))
            step(tt(gsm[:, 3, :], gsm[:, 2, :], gsm[:, 8, :], ALU.subtract))
            s4 = ssc.rearrange("p (s g h) -> p s g h", s=NS, g=PAGES)
            tt(s4, s4, gsm[:, 8, :].rearrange("p (s h) -> p s h", s=NS).unsqueeze(2)
               .broadcast_to([128, NS, PAGES, H]), ALU.subtract).then_inc(ssub_ready, 1)
            full(dve, ("sum", "moba", 0))
            drain(V.tensor_reduce(gsm[:, 9, :].rearrange("p (s h) -> p s h", s=NS),
                                  bank(("sum", "moba", 0))[:, :].rearrange("p (s g h) -> p s h g", s=NS, g=PAGES),
                                  AX, ALU.add), ("sum", "moba", 0))
            drained(dve, ("sum", "moba", 0))
            dve.wait_ge(pp_ready, 2)
            step(tt(gsm[:, 10, :], gsm[:, 9, :], gsm[:, 4, :], ALU.add))
            step(V.reciprocal(gsm[:, 11, :], gsm[:, 10, :]))
            full(dve, ("so", "moba", 0))
            for p in range(2):
                ps = slice(64 * p, 64 * p + 64)
                half = lambda r: gsm[ps, r, :].rearrange("p (s c b) -> p c s b", s=NS, c=HC)[:, :, :, p]
                ob = bank(("so", "moba", 0))[ps, 0:64].rearrange("p (s c b) -> p c s b", s=NS, c=HC)[:, :, :, p]
                w = gt[ps, 0:32].rearrange("p (c s) -> p c s", c=HC)
                step(tt(w, zo[ps, 8:12, L:T], half(4), ALU.mult))
                if p == 0:
                    step(tt(w, w, ob, ALU.add))
                else:
                    drain(tt(w, w, ob, ALU.add), ("so", "moba", 0))
                    drained(dve, ("so", "moba", 0))
                ins = tt(mix[ps, 0:4, L:T], w, half(11), ALU.mult)
                if p == 0:
                    step(ins)
            ins.then_inc(samp_o, 1)
            for j in range(4):
                full(dve, ("s5s", j))
                src = bank(("s5s", j))[:, 0:64].rearrange("p (c q s) -> p q c s", c=HC, q=2)
                for q in range(2):
                    ins = V.tensor_copy(hsS[:, q].rearrange("p (c j) s -> p c j s", j=4)[:, :, j, :], src[:, q])
                drain(ins, ("s5s", j))
            for j in range(4):
                drained(dve, ("s5s", j))
            sb8 = lambda v: v.unsqueeze(2).broadcast_to([128, NT, NS])
            for q, (a, b, c, d, op) in enumerate(((ar, ai, cr, ci, ALU.subtract), (ai, ar, ci, cr, ALU.add))):
                out = s5o[:, q, :, 1:9]
                step(tt(w3, s5h[:, 0], sb8(a), ALU.mult))
                step(tt(w4, s5h[:, 1], sb8(b), ALU.mult))
                step(tt(w3, w3, w4, op))
                step(tt(w4, hsS[:, 0], sb8(c), ALU.mult))
                step(tt(w3, w3, w4, ALU.add))
                step(tt(w4, hsS[:, 1], sb8(d), ALU.mult))
                step(tt(out, w3, w4, op))
            for q in range(2):
                V.tensor_copy(hsS[:, q], s5o[:, q, :, 1:9]).then_inc(s5_hs, 1)
            def y_out(c):
                key = ("s5y", c)
                full(dve, key)
                drain(stt(tmpy[:, c, :], zo[:, 12 + c, :], col("s5_d", c), bank(key)[:, 0:T], ALU.mult, ALU.add), key)

            for n in range(NT):
                key = ("s5x", n)
                b = n % 2
                full(dve, key)
                xv = bank(key)[:, :].rearrange("p (q t) -> p q t", q=2)
                tab = lambda v: v[:, n, :].unsqueeze(1).broadcast_to([128, 2, L])
                tt(ta[:, b], xv, tab(cosT), ALU.mult)
                drain(tt(tb[:, b], xv, tab(sinT), ALU.mult), key)
                drained(dve, key)
                tt(ta[:, b, 0, :], ta[:, b, 0, :], tb[:, b, 1, :], ALU.add)
                step(tt(ta[:, b, 1, :], ta[:, b, 1, :], tb[:, b, 0, :], ALU.subtract))
                if n >= 2:
                    dve.wait_ge(s5_hi, 2 * (n - 1))
                for q in range(2):
                    V.tensor_tensor_scan(gg[:, b, q, :], par[:, 1, n:n + 1].broadcast_to([128, L]), ta[:, b, q, :],
                                         0.0, ALU.mult, ALU.add).then_inc(s5_g, 1)
                dve.wait_ge(s5_g, 2 * (n + 1))
                tt(ta[:, b, 0, :], gg[:, b, 0, :], cosT[:, n, :], ALU.mult)
                step(tt(ta[:, b, 1, :], gg[:, b, 1, :], sinT[:, n, :], ALU.mult))
                if n >= NHB:
                    full(dve, ("s5y", (n - NHB) // 4))
                tt(hh[:, n % NHB, 0, :], ta[:, b, 0, :], ta[:, b, 1, :], ALU.subtract).then_inc(s5_hr, 1)
                dve.wait_ge(s5_hr, n + 1)
                ins = V.tensor_copy(hl[:, 0, n:n + 1], hh[:, n % NHB, 0, L - 1:L])
                if n == NT - 1:
                    step(ins)
                if n >= 6 and n % 4 == 2:
                    y_out((n - 6) // 4)
            y_out(3)
            dve.wait_ge(s5_hi, 2 * NT)
            for q, (a, b, op) in enumerate(((cr, ci, ALU.subtract), (ci, cr, ALU.add))):
                step(tt(t16[:, 0, :], hl[:, 0, :], a, ALU.mult))
                step(tt(t16[:, 1, :], hl[:, 1, :], b, ALU.mult))
                ins = tt(s5o[:, q, :, 0], t16[:, 0, :], t16[:, 1, :], op)
                if q == 0:
                    step(ins)
            ins.then_inc(s5_hs, 1)
            for c in range(HC):
                key = ("lin", "glu", 2 * c)
                full(dve, key)
                drained(dve, ("lin", "glu", 2 * c + 1))
                drain(tt(mix[:, 4 + c, :], bank(key)[:, 0:T], tmp[:, c % 2, :], ALU.mult), key)
            residual("od_out")
            memory(1)
            ffn(1)


_OUT = {"y": (128, KC, T), "o_gconv": (128, 12, 27), "o_gdn": (128, HC, HD), "o_sgs": (128, HC, NS, HD),
        "o_hgrn": (128, HC, HD), "o_shs": (128, HC, NS, HD), "o_k": (128, HC, T), "o_v": (128, HC, T),
        "o_s5": (128, 2, NT, 9), "o_memk": (2, 128, MH, NM), "o_memv": (2, 128, MH, NM), "o_ffn": (2, 128, FT, 18)}


def feats(a):
    n, f = a.shape
    return a.T.reshape(f // 128, 128, n).transpose(1, 0, 2)


def stream(w, per):
    k, m = w.shape
    a = w.reshape(k // 128, 128, m // 128, 128).transpose(2, 1, 0, 3)
    a = a.reshape(m // 128 // per, per, 128, k // 128, 128).transpose(0, 2, 1, 3, 4)
    return np.ascontiguousarray(a.reshape(m // 128 // per, 128, -1))


def layout(i):
    g = {k: np.asarray(v) for k, v in i.items()}
    a = {"con": constants()}
    a["x"] = feats(np.concatenate([g["x_prompt"][0], g["x_sample"][:, 0]], 0))
    a["memx"] = feats(g["mem_prompt"][0])
    vec = np.zeros((128, VECW), np.float32)

    def put(name, v, at=0):
        v = np.asarray(v)
        vec[:v.shape[0], VEC[name] + at:VEC[name] + at + v.shape[1]] = v

    for n in ("norm_mix", "norm_mem", "norm_memkv", "norm_ffn"):
        put(n, g[n].reshape(16, 128).T)
    put("mem_gq", g["mem_gq"].T)
    put("mem_gk", g["mem_gk"].T)
    put("ffn_w", g["ffn_conv_w"].reshape(6 * FT, 128).T)
    put("ffn_b", g["ffn_conv_b"].reshape(2 * FT, 128).T)
    put("conv_w", g["gdn_conv_w"][0].reshape(48, 128).T)
    for n in ("gdn_norm", "hgrn_norm", "moba_gq", "moba_gk"):
        put(n, np.concatenate([g[n][0], g[n][0]])[:, None])
    put("lb", g["hgrn_lb_raw"].reshape(12, 128).T)
    put("s5_re", g["s5_A_re"][0].reshape(NT, 128).T)
    put("s5_im", g["s5_A_im"][0].reshape(NT, 128).T)
    put("s5_dt", np.repeat(g["s5_log_dt"][0], 64).reshape(NT, 128).T)
    put("s5_d", g["s5_D"][0].reshape(4, 128).T)
    vec[32:40, VEC["small"]] = g["gdn_dt_bias"][0]
    vec[0:8, VEC["small"] + 1] = g["gdn_A_log"][0]
    put("relb", g["rel_bias"])
    vec[:, VEC["relb0"]:VEC["relb0"] + H] = np.broadcast_to(g["rel_bias"][0], (128, H))
    w = g["ev_w_in"][0]
    z = 4 * 512
    for k in range(KC):
        vec[:, VEC["w_ab"] + 40 * k:VEC["w_ab"] + 40 * k + 8] = w[128 * k:128 * k + 128, z:z + 8]
        vec[:, VEC["w_ab"] + 40 * k + 32:VEC["w_ab"] + 40 * k + 40] = w[128 * k:128 * k + 128, z + 8:z + 16]
    a["vec"] = vec
    a["pages"] = g["page_table"].reshape(1, NS * PAGES)
    a["ev_in_a"] = stream(w[:, :z], 2)
    a["ev_in_b"] = stream(w[:, z + 16:], 2)
    a["ev_out"] = stream(g["ev_w_out"][0], 2)
    a["od_in"] = stream(g["od_w_in"][0], 2)
    a["od_out"] = stream(g["od_w_out"][0], 2)
    glu = g["s5_glu_w"][0].reshape(512, 2, 4, 128).transpose(0, 2, 1, 3).reshape(512, 1024)
    a["glu"] = stream(glu, 4)
    for l in range(2):
        a[f"memk{l}"] = stream(g["mem_wkv"][l][:, :512], 2)
        a[f"memv{l}"] = stream(g["mem_wkv"][l][:, 512:], 2)
        a[f"wq{l}"] = stream(g["mem_wq"][l], 2)
        a[f"wo{l}"] = stream(g["mem_wo"][l], 4)
        gu = g["ffn_w_gu"][l].reshape(D, 2, FT, 128).transpose(0, 2, 1, 3).reshape(D, 2 * DFF)
        a[f"gu{l}"] = stream(gu, 2)
        a[f"down{l}"] = stream(g["ffn_w_down"][l], 1)
        k = g["cache_mem_k"][l]
        a[f"ck{l}"] = k.reshape(4, 2, NM, MH, 128).transpose(0, 4, 1, 3, 2).reshape(4, 128, 2048)
        v = g["cache_mem_v"][l]
        a[f"cv{l}"] = v.reshape(4, 2, 2, 128, MH, 128).transpose(0, 3, 1, 4, 2, 5).reshape(4, 128, 2048)
    a["gconv"] = g["state_gdn_conv"][0].reshape(NS, 3, 12, 128).transpose(3, 2, 1, 0).reshape(128, 12, 24)
    for n, k in (("sgs", "state_gdn"), ("shs", "state_hgrn")):
        a[n] = g[k][0].reshape(NS, HC, 2, 64, 64).transpose(2, 3, 1, 0, 4).reshape(128, HC, NS, HD)
    a["fh"] = g["state_ffn_conv"].reshape(2, NS, 2, FT, 128).transpose(0, 4, 3, 2, 1).reshape(2, 128, FT, 16)
    a["s5h"] = np.stack([g[k][0].reshape(NS, NT, 128).transpose(2, 1, 0) for k in ("state_s5_re", "state_s5_im")], 1)
    b = np.zeros((4, 2, 16, 2, 4, 2, 64), np.float32)
    c = np.zeros((2, 64, 2, NT, 2, 16), np.float32)
    for q in range(2):
        bq = g[("s5_B_re", "s5_B_im")[q]][0].reshape(4, 4, 2, 64, 16)
        cq = g[("s5_C_re", "s5_C_im")[q]][0].reshape(NT, 2, 16, 64)
        for e in range(2):
            b[:, e, :, q, :, e, :] = bq[:, :, e].transpose(1, 3, 0, 2)
            c[e, :, q, :, e, :] = cq[:, e].transpose(2, 0, 1)
    a["s5b"] = b.reshape(128, 2, 4, 128)
    a["s5c"] = c.reshape(128, 2, NT, 32)
    a["pool_k"] = g["cache_moba_k"][0].reshape(POOL_PAGES, 128, HC, 128).transpose(0, 3, 2, 1).reshape(
        POOL_PAGES, 128, 512)
    a["pool_v"] = g["cache_moba_v"][0].reshape(POOL_PAGES, 128, 512)
    return {k: np.ascontiguousarray(v) for k, v in a.items()}


def kernel(**inputs):
    import concourse.bacc as bacc
    from concourse.bass_utils import run_bass_kernel_spmd

    nc = bacc.Bacc("TRN2", target_bir_lowering=False, num_devices=1)
    arrays, A = {}, {}
    for name, a in layout(inputs).items():
        arrays[f"in_{name}"] = a
        A[name] = nc.dram_tensor(f"in_{name}", a.shape, mybir.dt.from_np(a.dtype), kind="ExternalInput").ap()
    for name, shape in _OUT.items():
        A[name] = nc.dram_tensor(f"out_{name}", shape, F32, kind="ExternalOutput").ap()
    A["bias_x"] = nc.dram_tensor("bias_x", (8, 512), F32, kind="Internal").ap()
    build(nc, A)
    r = run_bass_kernel_spmd(nc, [arrays], core_ids=[0]).results[0]
    o = {name: np.asarray(r[f"out_{name}"]) for name in _OUT}

    def rows(a):
        return a.transpose(2, 1, 0).reshape(a.shape[2], -1)

    y = rows(o["y"])
    gc = o["o_gconv"]
    k, v = rows(o["o_k"]), rows(o["o_v"])
    pst = lambda a: a.reshape(2, 64, HC, 64).transpose(2, 0, 1, 3).reshape(1, 1, H, 64, 64)
    sst = lambda a: a.reshape(2, 64, HC, NS, 64).transpose(3, 2, 0, 1, 4).reshape(1, NS, H, 64, 64)
    s5 = o["o_s5"].transpose(1, 3, 2, 0).reshape(2, 9, 32, 64)
    memo = lambda a: np.stack([rows(a[l]) for l in range(2)]).reshape(2, 1, NM, MH, 128)
    ff = o["o_ffn"]
    ffp = ff[..., 0:2].transpose(0, 3, 2, 1).reshape(2, 1, 2, DFF)
    ffs = ff[..., 2:18].reshape(2, 128, FT, 2, NS).transpose(0, 4, 3, 2, 1).reshape(2, NS, 2, DFF)
    out = (y[None, :L], y[L:, None], rows(gc[:, :, 0:3]).reshape(1, 1, 3, 1536), pst(o["o_gdn"]), pst(o["o_hgrn"]),
           k[:L].reshape(1, 1, L, H, HD), v[:L].reshape(1, 1, L, H, HD), s5[0:1, 0:1], s5[1:2, 0:1],
           memo(o["o_memk"]), memo(o["o_memv"]), ffp,
           gc[:, :, 3:].reshape(128, 12, 3, NS).transpose(3, 2, 1, 0).reshape(1, NS, 3, 1536),
           sst(o["o_sgs"]), sst(o["o_shs"]), k[L:].reshape(1, NS, 1, H, HD), v[L:].reshape(1, NS, 1, H, HD),
           s5[0:1, 1:], s5[1:2, 1:], ffs)
    return tuple(np.ascontiguousarray(a) for a in out)
```

```python
import math
from contextlib import ExitStack

import numpy as np
import concourse.bass as bass
from concourse import mybir

F32 = mybir.dt.float32
I32 = mybir.dt.int32
ALU = mybir.AluOpType
ACT = mybir.ActivationFunctionType
AX = mybir.AxisListType.X

D = 1024
KC = D // 128
L = 256
NS = 8
T = L + NS
H = 8
HC = 4
HD = 64
CHK = 128
NCH = L // CHK
HCK = 32
MH = 4
NM = 256
DFF = 2816
FT = DFF // 128
PAGES = 8
POOL_PAGES = 80
NT = 16
EPS = 1e-6
BIG = -1.0e30
LEV = 7
SLOTS = 4
SLOTW = FT * 128
NBANK = 8
TWO_PI = 2.0 * math.pi
MAGIC = 12582912.0

VEC = {}
_off = 0
for _name, _w in [("norm_mix", 16), ("norm_mem", 16), ("norm_memkv", 16), ("norm_ffn", 16), ("mem_gq", 2),
                  ("mem_gk", 2), ("ffn_w", 2 * 3 * FT), ("ffn_b", 2 * FT), ("conv_w", 48), ("gdn_norm", 1),
                  ("hgrn_norm", 1), ("moba_gq", 1), ("moba_gk", 1), ("lb", 12), ("s5_re", NT), ("s5_im", NT),
                  ("s5_dt", NT), ("s5_d", 4), ("small", 2), ("relb", H), ("relb0", 1), ("w_ab", KC * 40)]:
    VEC[_name] = _off
    _off += _w
VECW = _off
CON = {}
_off = 0
for _name, _w in [("ident", 128), ("ones", 128), ("bd", 128), ("neg", 128), ("i2", 64), ("lev", LEV * 128),
                  ("selh", H * 128), ("nselh", H * 128), ("selc", HC * 128), ("hotx", 512), ("hots", 1024),
                  ("cmask", 128), ("sel", 4 * H)]:
    CON[_name] = _off
    _off += _w
CONW = _off


def constants():
    c = np.zeros((128, CONW), np.float32)
    p = np.arange(128)

    def put(name, a):
        c[:a.shape[0], CON[name]:CON[name] + a.shape[1]] = a

    put("ident", np.eye(128))
    put("ones", np.ones((128, 128)))
    put("bd", (p[:, None] // 64 == p[None] // 64) * 1.0)
    put("neg", np.where(p[None] >= p[:, None], 0.0, BIG))
    put("i2", (p[:, None] % 64 == np.arange(64)[None]) * 1.0)
    for l in range(LEV):
        b = 1 << l
        m = (p[None] // (2 * b) == p[:, None] // (2 * b)) & (p[None] // b % 2 == 1) & (p[:, None] // b % 2 == 0)
        c[:, CON["lev"] + 128 * l:CON["lev"] + 128 * (l + 1)] = m
    for h in range(H):
        c[h, CON["selh"] + 128 * h:CON["selh"] + 128 * (h + 1)] = 1.0
        c[h, CON["nselh"] + 128 * h:CON["nselh"] + 128 * (h + 1)] = -1.0
        at = CON["selc"] + 64 * h
        c[h, at:at + 64] = 1.0

    def bucket(n):
        if n < 16:
            return n
        return min(16 + int(math.log(n / 16) / math.log(8.0) * 16 + 1e-9), 31)
    for j in range(512):
        dist = j - 255
        c[32 if dist < 0 else bucket(dist), CON["hotx"] + j] = 1.0
    for k in range(1024):
        c[bucket(1024 - k), CON["hots"] + k] = 1.0
    for q in range(H):
        for j in range(4):
            c[32 * j + q, CON["sel"] + 4 * q + j] = 1.0
    put("cmask", ((p[:, None] // HCK == p[None] // HCK) & (p[None] >= p[:, None])) * 1.0)
    return c


def make_plan():
    order, slots, slot_of = [], [], {}
    used = [0]

    def lin(name, tiles, per_slot, cols):
        for m in range(tiles):
            if m % per_slot == 0:
                slots.append(("w", name, m // per_slot, cols, None))
            slot_of[(name, m)] = len(slots) - 1
            order.append(("lin", name, m))
            slots[-1] = slots[-1][:4] + (("lin", name, m),)

    def stream(name, i, cols, last):
        if last is None:
            used[0] += 1
            last = ("used", used[0])
        slots.append(("w" if name[0] == "c" else "page", name, i, cols, last))
        slot_of[(name, i)] = len(slots) - 1

    def memory(l):
        order.append(("ss", "memkv", l))
        lin(f"memk{l}", MH, 2, 2048)
        for h in range(MH):
            order.append(("hn", f"memk{l}", h))
        lin(f"memv{l}", MH, 2, 2048)
        order.extend([("mvt", l, 0), ("mvt", l, 1)])
        order.append(("ss", "mem", l))
        lin(f"wq{l}", MH, 2, 2048)
        for h in range(MH):
            order.append(("hn", f"memq{l}", h))
        name = f"mem{l}"

        def keys(i, part):
            if part == 0 and i < 4:
                stream(f"ck{l}", i, 2048, ("sc", name, i // 2) if i % 2 else None)
                if i % 2:
                    order.append(("sc", name, i // 2))
        attend(name, MH, keys)
        order.append(("pt", name, 0))
        for i in range(4):
            stream(f"cv{l}", i, 2048, ("so", name, i // 2) if i % 2 else None)
            if i % 2:
                order.append(("so", name, i // 2))
        order.append(("sx", name))
        lin(f"wo{l}", KC, 4, 2048)

    def attend(name, n, between):
        for i in range(n + 2):
            if i < n:
                order.append(("S", name, i))
            between(i, 0)
            if 0 <= i - 1 < n:
                order.append(("PT", name, i - 1))
            between(i, 1)
            if 0 <= i - 2 < n:
                order.append(("O", name, i - 2))

    def ffn(l):
        order.append(("ss", "ffn", l))
        lin(f"gu{l}", 2 * FT, 2, 2048)
        lin(f"down{l}", KC, 1, SLOTW)

    order.append(("ss", "mix", 0))
    order.append(("ab",))
    lin("ev_in_a", 16, 2, 2048)
    for i in range(8):
        order.append(("hn", "l2", i))
    for c in range(HC):
        order.extend([("bcB", c), ("bcG", c), ("bcL", c)])
    for t in range(NCH):
        order.extend([("trk", t), ("trv", t)])
    G4 = [(t, par) for t in range(NCH) for par in range(2)]
    for g in G4:
        order.extend([("DT", g), ("QK", g), ("KK", g)])
    for g in G4:
        order.append(("X1", g))
    for l in range(1, LEV):
        for g in G4:
            order.append(("T1", l, g))
        for g in G4:
            order.append(("ZT", l, g))
            if l < LEV - 1:
                order.append(("Z", l, g))
    for t in range(NCH):
        if t:
            order.extend([("ks", 0), ("ks", 1)])
        order.extend([("u", t), ("o", t, 0), ("o", t, 1), ("S", "gdn", t)])
    for i in range(HC):
        order.append(("su", "gdn", i))
    order.extend([("sO", "gdn", 0), ("sO", "gdn", 1)])
    for c in range(HC):
        order.append(("hn", "gdn", c))
    lin("ev_in_b", 16, 2, 2048)
    for t in range(NCH):
        order.extend([("htk", t), ("htv", t)])
    for g in G4:
        order.append(("att", g))
    for k in range(L // HCK):
        order.append(("kv", k))
    for g in G4:
        order.append(("ho", g))
    for i in range(HC):
        order.append(("su", "hgrn", i))
    order.extend([("sO", "hgrn", 0), ("sO", "hgrn", 1)])
    for c in range(HC):
        order.append(("hn", "hgrn", c))
    lin("ev_out", KC, 2, 2048)
    memory(0)
    ffn(0)
    order.append(("ss", "mix", 1))
    lin("od_in", 16, 2, 2048)
    for i in range(8):
        order.append(("hn", "moba", i))
    order.extend([("vt", 0), ("vt", 1), ("bx",), ("bs", 0), ("bs", 1), ("self",)])

    def pages(i, part):
        if i < H:
            n = 2 * i + part
            stream("pk", n, 2048, ("sc", "moba", n // 4) if n % 4 == 3 else None)
            if n % 4 == 3:
                order.append(("sc", "moba", n // 4))
    attend("moba", H, pages)
    for j in range(4):
        order.append(("s5s", j))
    order.extend([("s5x", 0), ("s5x", 1)])
    for i in range(4):
        order.append(("pt", "moba", i))
    for n in range(NT):
        stream("pv", n, 2048, ("so", "moba", n // 4) if n % 4 == 3 else None)
        if n % 4 == 3:
            order.append(("so", "moba", n // 4))
        if n + 2 < NT:
            order.append(("s5x", n + 2))
        if n % 4 == 2 and n > 2:
            order.append(("s5y", n // 4 - 1))
    order.extend([("s5y", 3), ("sx", "moba")])
    lin("glu", 8, 4, 2048)
    lin("od_out", KC, 2, 2048)
    memory(1)
    ffn(1)
    return order, slots, slot_of


def build(nc, A):
    order, slots, slot_of = make_plan()
    no = {k: i for i, k in enumerate(order)}
    assert len(no) == len(order)
    hn_no = {}
    at_no = {}
    for k in order:
        if k[0] == "hn":
            hn_no[k[1:]] = len(hn_no)
        if k[0] == "PT":
            at_no[k[1:]] = len(at_no)

    slot_value, seen = [], [0] * SLOTS
    for s, (kind, _, _, _, _) in enumerate(slots):
        seen[s % SLOTS] += 16 * (4 if kind == "page" else 1)
        slot_value.append(seen[s % SLOTS])

    with ExitStack() as ctx:
        def sb(name, shape, dt=F32):
            return ctx.enter_context(nc.sbuf_tensor(name, shape, dt))

        def sem(name):
            return ctx.enter_context(nc.semaphore(name))

        banks = [ctx.enter_context(nc.psum_tensor(f"bank{i}", [128, 512], F32)) for i in range(NBANK)]

        def bank(key):
            return banks[no[key] % NBANK]

        def blocks(key, n=4, p0=0, p1=128):
            return bank(key)[p0:p1, 0:n * 128].rearrange("p (n k) -> p n k", n=n)

        con = sb("con", [128, CONW])
        vec = sb("vec", [128, VECW])
        pages = sb("pages_sb", [1, NS * PAGES], I32)
        ring = sb("ring", [128, SLOTS, SLOTW])
        x = sb("x", [128, KC, T])
        h = sb("h", [128, KC, T])
        sq = sb("sq", [128, KC, T])
        mix = sb("mix", [128, KC, T])
        oT = sb("oT", [128, HC, T])
        tmp = sb("tmp", [128, 2, T])
        lnb = sb("lnb", [128, T])
        rs = sb("rs", [128, T])
        hsq = sb("hsq", [128, 2, T])
        hr = sb("hr", [128, 2, T])
        rmask = sb("rmask", [128, L])
        cvo = sb("cvo", [128, 12, 27])
        egc = sb("egc", [128, HC, 9])
        ch = sb("ch", [128, 12, 24])
        sg = sb("sg", [128, HC, HD])
        lbt = sb("lbt", [128, 8, HC])
        par = sb("s5par", [128, 24, NT])
        relb = sb("relb", [64, H])
        aexp = sb("aexp", [8, 1])
        epst = sb("epst", [128, 1])
        onec = sb("onec", [128, 1])
        WORK = 21700
        work = sb("work", [128, WORK])

        def place(at, *dims):
            n = int(np.prod(dims))
            assert at + n <= WORK, (at, n)
            v = work[:, at:at + n]
            if len(dims) == 2:
                v = v.rearrange("p (a b) -> p a b", a=dims[0])
            if len(dims) == 3:
                v = v.rearrange("p (a b c) -> p a b c", a=dims[0], b=dims[1])
            if len(dims) == 4:
                v = v.rearrange("p (a b c d) -> p a b c d", a=dims[0], b=dims[1], c=dims[2])
            return v, at + n

        def cst(name, w=128, i=0, p=128):
            return con[0:p, CON[name] + i * w:CON[name] + (i + 1) * w]

        def col(name, i=0, p0=0, p1=128):
            return vec[p0:p1, VEC[name] + i:VEC[name] + i + 1]

        def cols(name, n, i=0, p0=0, p1=128):
            return vec[p0:p1, VEC[name] + i:VEC[name] + i + n]

        ident, ones, bd = cst("ident"), cst("ones"), cst("bd")

        def four(ap):
            return ap.unsqueeze(1).broadcast_to([128, 4, 128])

        psum_full = sem("psum_full")
        psum_free = [sem(f"psum_free{i}") for i in range(NBANK)]
        ring_full = [sem(f"ring_full{i}") for i in range(SLOTS)]
        (con_in, vec_in, x_in, pages_in, hist_in, memx_in, sgs_in, shs_in, fh_in, s5_in, bias_in) = [
            sem(n) for n in ("con_in", "vec_in", "x_in", "pages_in", "hist_in", "memx_in", "sgs_in", "shs_in",
                             "fh_in", "s5_in", "bias_in")]
        act_step, dve_step, pool_step = sem("act_step"), sem("dve_step"), sem("pool_step")
        msq_ready, pages_used = sem("msq_ready"), sem("pages_used")
        sq_ready, r_ready, h_ready = sem("sq_ready"), sem("r_ready"), sem("h_ready")
        hsq_ready, hr_ready, hn_done = sem("hsq_ready"), sem("hr_ready"), sem("hn_done")
        mix_ready, stored, sgs_out = sem("mix_ready"), sem("stored"), sem("sgs_out")
        pads_ready, lb_step, gate_rows, conv_done, silu_done = [
            sem(n) for n in ("pads_ready", "lb_step", "gate_rows", "conv_done", "silu_done")]
        cvo_ready, scaled_ready, xt_ready, ml_ready = [
            sem(n) for n in ("cvo_ready", "scaled_ready", "xt_ready", "ml_ready")]
        w_ready, sdec_ready, sst_ready = sem("w_ready"), sem("sdec_ready"), sem("sst_ready")
        fk_ready, lf_ready, dec_ready, exp_ready, hg_dve, hg_pool, att_zero, sh_ready = [
            sem(n) for n in ("fk_ready", "lf_ready", "dec_ready", "exp_ready", "hg_dve", "hg_pool", "att_zero",
                             "sh_ready")]
        smax_ready, p_exp, p_ready = [sem(n) for n in ("smax_ready", "p_exp", "p_ready")]
        mx_ready, pp_ready, sel_ready, qz_ready = [sem(n) for n in ("mx_ready", "pp_ready", "sel_ready", "qz_ready")]
        fpads, fconv_done, fsilu_done, act_ready, fcopy_done = [
            sem(n) for n in ("fpads", "fconv_done", "fsilu_done", "act_ready", "fcopy_done")]
        bx_stored, qk_ready, samp_o = [sem(n) for n in ("bx_stored", "qk_ready", "samp_o")]
        s5_par, s5_hr, s5_g, s5_hi, s5_y, s5_gelu, s5_hs = [
            sem(n) for n in ("s5_par", "s5_hr", "s5_g", "s5_hi", "s5_y", "s5_gelu", "s5_hs")]
        eps_ready, relb_ready, s5_gl2 = [sem(n) for n in ("eps_ready", "relb_ready", "s5_gl2")]
        hg_stored, mem_stored, ffn_stored, kv_stored = [
            sem(n) for n in ("hg_stored", "mem_stored", "ffn_stored", "kv_stored")]

        def full(eng, key):
            eng.wait_ge(psum_full, no[key] + 1)

        def drained(eng, key):
            eng.wait_ge(psum_free[no[key] % NBANK], no[key] // NBANK + 1)

        def drain(ins, key):
            return ins.then_inc(psum_free[no[key] % NBANK], 1)

        class Steps:
            def __init__(self, eng, s):
                self.eng, self.s, self.n = eng, s, 0

            def __call__(self, ins):
                self.n += 1
                ins.then_inc(self.s, 1)
                self.eng.wait_ge(self.s, self.n)

        norms = [k[1:] for k in order if k[0] == "ss"]
        xnorms = [n for n in norms if n[0] != "memkv"]
        NORM_G = {"mix": "norm_mix", "memkv": "norm_memkv", "mem": "norm_mem", "ffn": "norm_ffn"}
        G4 = [(t, p) for t in range(NCH) for p in range(2)]

        MXN = {"mem0": 0, "moba": 2, "mem1": 3}
        QZN = {"mem0": 0, "moba": 2, "mem1": 4}
        SELN = {"mem0": 1, "moba": 2, "mem1": 3}

        zqkv, e = place(0, 12, 3 + T)
        qkv, e = place(e, 12, T)
        kb, e = place(e, HC, T)
        bk, e = place(e, HC, T)
        qe, e = place(e, HC, T)
        vb, e = place(e, HC, T)
        ke, e = place(e, HC, L)
        ketok, e = place(e, NCH, 512)
        vbtok, e = place(e, NCH, 512)
        qkd, e = place(e, 4, 512)
        ws1, _ = place(e - 2048, HC, NS, HD)
        gs, _ = place(e, 5, T)
        xx, e = place(e, 4, 512)
        ws2, _ = place(e - 2048, HC, NS, HD)
        dt_, e = place(e, 2, 512)
        rhst, e = place(e, 512)
        utok, e = place(e, 512)
        assert e <= WORK - HC * T
        zg, _ = place(WORK - HC * T, HC, T)
        mt, _ = place(0, 4, 512)
        ml, _ = place(2048, 2, 512)
        sgs, _ = place(0, HC, NS, HD)
        flat = "p a b -> p (a b)"
        xt = sq[:, :, :].rearrange(flat)[:, 0:2048].rearrange("p (g n) -> p g n", g=4)
        t1 = mix[:, :, :].rearrange(flat)[:, 0:2048].rearrange("p (g n) -> p g n", g=4)
        zq, e = place(2816, HC, T)
        zf, e = place(e, HC, T)
        zk, e = place(e, HC, T)
        zi, e = place(e, HC, T)
        zh, e = place(e, HC, T)
        hkt, _ = place(e, NCH, 512)
        hvt, _ = place(e + 1024, NCH, 512)
        lf, e = place(e, HC, L)
        bcs, e = place(e, HC, L)
        hws1, _ = place(e, HC, NS, HD)
        d1, e = place(e, HC, L)
        d2, e = place(e, HC, L)
        hws2, _ = place(e, HC, NS, HD)
        qx, e = place(e, HC, L)
        kx, e = place(e, HC, L)
        qin, e = place(e, HC, L)
        ko, e = place(e, HC, L)
        fl, e = place(e, HC, L // HCK)
        attb, e = place(e, 4, 512)
        sh0 = e
        SH = [place(sh0 + 256 * (k % 8), HC, HD)[0] for k in range(8)]
        e = sh0 + 2048
        assert e <= WORK - HC * T, e
        shs, _ = place(0, HC, NS, HD)
        mh, e = place(0, KC, NM)
        mk, e = place(e, MH, NM)
        mv, e = place(e, MH, NM)
        mvt, e = place(e, 2, 512)
        mq, e = place(e, MH, T)
        msb, e = place(e, 2, 512)
        mpt, e = place(e, 2, 512)
        mqz, e = place(e, MH, NS, 32)
        mpm, e = place(e, 2, NM)
        mps, e = place(e, 4, 4, MH)
        mos, e = place(e, 2, 512)
        msm, e = place(e, 2, 4)
        msel, e = place(e, 2, 4 * MH)
        att_buf = {"mem0": (msb, mpt), "mem1": (msb, mpt)}
        act_, e = place(e, FT, T)
        gb, e = place(e, 3, 2 + T)
        cacc, e = place(e, 2, T)
        csil, e = place(e, 2, T)
        fo, e = place(e, FT, 18)
        fh, e = place(e, FT, 16)
        zo, e = place(0, 16, T)
        hank, e = place(e, H, 384)
        ovt, e = place(e, 2, 512)
        osb, e = place(e, 2, 512)
        opt, e = place(e, 2, 512)
        att_buf["moba"] = (osb, opt)
        bsp, e = place(e, 2, 512)
        spt, _ = place(e - 1024, 4, 4, 4, H)
        ssc, e = place(e, 2, 1024)
        kz, _ = place(e - 2048, HC, NS, 32)
        WTMP = e - 1024
        cosT, e = place(e, NT, L)
        sinT, e = place(e, NT, L)
        ygl = zo[:, 8:12, :]
        s0 = 16 * T
        TABTMP = s0
        NHB = 8
        tmpy = zo[:, 0:4, :]
        ta, e2 = place(s0, 2, 2, L)
        tb, e2 = place(e2, 2, 2, L)
        gg, e2 = place(e2, 2, 2, L)
        pt_, e2 = place(e2, 2, 2, L)
        HH = [place(e2 + 512 * i if i < 4 else e - 2 * NT * L - 2048 + 512 * (i - 4), 2, L)[0] for i in range(NHB)]
        e2 += 4 * 512
        assert e2 <= e - 2 * NT * L - 3072
        e2 = e - 2 * NT * L - 2560
        hsS, e2 = place(e2, 2, NT, NS)
        w3, e2 = place(e2, NT, NS)
        w4, e2 = place(e2, NT, NS)
        mixf, tmpf = mix[:, :, :].rearrange(flat), tmp[:, :, :].rearrange("p a b -> p (a b)")
        qz = mixf[:, 1056:2080].rearrange("p (c s h) -> p c s h", c=HC, s=NS)
        osm = mixf[:, 1056:2080].rearrange("p (g n) -> p g n", g=2)
        relr = tmpf[0:32, 0:128]
        sel2 = tmpf[:, 128:256].rearrange("p (a g n) -> p a g n", a=2, g=2)
        gsm = tmpf[:, 256:256 + 72].rearrange("p (r n) -> p r n", r=9)
        gs2 = tmpf[:, 336:336 + 20].rearrange("p (r g) -> p r g", g=2)
        sqf, hf_ = sq[:, :, :].rearrange(flat), h[:, :, :].rearrange(flat)
        s5b = sqf[:, 0:1024].rearrange("p (q c n) -> p q c n", q=2, c=4)
        s5c = sqf[:, 1024:2048].rearrange("p (q n k) -> p q n k", q=2, n=NT)
        s5cp = hf_[:, 0:1536].rearrange("p (q n k) -> p q n k", q=3, n=NT)
        s5h = hf_[:, 1536:1792].rearrange("p (q n s) -> p q n s", q=2, n=NT)
        s5o = sb("s5o", [128, 2, NT, 9])
        hl = sb("hl", [128, 2, NT])
        t16 = sb("t16", [128, 4, NT])
        bxs = hsq[0:8, :, :].rearrange(flat)[:, 0:512]
        smx = sb("smx", [128, 2, 4, 2])

        s_slots = list(enumerate(slots))

        block = ctx.enter_context(nc.Block())

        @block.sync
        def _(sp):
            sp.dma_start(con[:, :], A["con"]).then_inc(con_in, 16)
            sp.dma_start(x[:, :, :], A["x"]).then_inc(x_in, 16)
            sp.dma_start(vec[:, :], A["vec"]).then_inc(vec_in, 16)
            sp.dma_start(pages[:, :], A["pages"]).then_inc(pages_in, 16)
            sp.wait_ge(pages_in, 16)
            for s, (kind, name, i, w, _) in s_slots:
                if s >= SLOTS:
                    last = slots[s - SLOTS][4]
                    if last[0] == "used":
                        sp.wait_ge(pages_used, last[1])
                    else:
                        full(sp, last)
                dst = ring[:, s % SLOTS, 0:w]
                if kind == "w":
                    sp.dma_start(dst, A[name][i]).then_inc(ring_full[s % SLOTS], 16)
                    continue
                pool = A["pool_k"] if name == "pk" else A["pool_v"]
                if name == "pk":
                    i = 2 * (4 * (i // 8) + i % 4) + i // 4 % 2
                for j in range(4):
                    at = 4 * i + j
                    page = sp.value_load(pages[0:1, at:at + 1], min_val=0, max_val=POOL_PAGES - 1)
                    sp.dma_start(dst[:, 512 * j:512 * (j + 1)].unsqueeze(1),
                                 pool[bass.ds(page, 1)].rearrange("a p n -> p a n")).then_inc(ring_full[s % SLOTS], 16)

        @block.gpsimd
        def _(pool):
            step = Steps(pool, pool_step)
            stores = [0]

            def store(dst, src, done=None):
                pool.dma_start(dst, src).then_inc(done or stored, 16)
                if not done:
                    stores[0] += 1

            step(nc.gpsimd.memset(rmask[:, :], 1.0))
            nc.gpsimd.memset(rmask[:, :].rearrange("p (k c) -> p k c", c=HCK)[:, :, 0:1], 0.0).then_inc(pads_ready, 1)
            nc.gpsimd.memset(zqkv[:, :, 0:3], 0.0).then_inc(pads_ready, 1)
            pool.dma_start(ch[:, :, :], A["gconv"]).then_inc(hist_in, 16)

            pool.wait_ge(hist_in, 16)
            drained(pool, ("lin", "ev_in_a", 11))
            nc.gpsimd.tensor_copy(cvo[:, :, 0:3], zqkv[:, :, 256:259])
            nc.gpsimd.tensor_copy(cvo[:, :, 3:19], ch[:, :, 8:24])
            nc.gpsimd.tensor_copy(cvo[:, :, 19:27], zqkv[:, :, 259:267]).then_inc(cvo_ready, 1)
            pool.wait_ge(cvo_ready, 1)
            store(A["o_gconv"], cvo[:, :, :])
            pool.wait_ge(xt_ready, 4)
            for l in range(1, LEV):
                for gi, g in enumerate(G4):
                    n = (l - 1) * 4 + gi
                    if n >= 2:
                        pn = n - 2
                        full(pool, ("T1", pn // 4 + 1, G4[pn % 4]))
                    nc.gpsimd.tensor_tensor(ml[:, n % 2, :].rearrange("p (n k) -> p n k", n=4),
                                            mt[:, gi, :].rearrange("p (n k) -> p n k", n=4),
                                            four(cst("lev", i=l)), ALU.mult).then_inc(ml_ready, 1)
            full(pool, ("T1", LEV - 1, G4[3]))
            pool.dma_start(sgs, A["sgs"]).then_inc(sgs_in, 16)
            drained(pool, ("S", "gdn", NCH - 1))
            store(A["o_gdn"], sg[:, :, :])
            pool.wait_ge(sgs_in, 16)
            pool.wait_ge(w_ready, 1)
            nc.gpsimd.tensor_tensor(sgs, sgs, egc[:, :, 1:9].unsqueeze(3).broadcast_to([128, HC, NS, HD]),
                                    ALU.mult).then_inc(sdec_ready, 1)
            pool.wait_ge(sst_ready, 4)
            pool.dma_start(A["o_sgs"], sgs).then_inc(sgs_out, 16)
            pool.wait_ge(sgs_out, 16)
            full(pool, ("sO", "gdn", 1))
            pool.dma_start(shs, A["shs"]).then_inc(shs_in, 16)
            nc.gpsimd.memset(attb, 0.0).then_inc(att_zero, 1)
            for m in range(4):
                drained(pool, ("lin", "ev_in_b", m))
            pool.wait_ge(exp_ready, 4)
            pool.wait_ge(fk_ready, HC)
            nc.gpsimd.tensor_copy(fl, qin[:, :, HCK - 1::HCK]).then_inc(hg_pool, 1)
            pool.wait_ge(hg_pool, 1)
            nc.gpsimd.tensor_tensor(ko, ko, zk[:, :, 0:L], ALU.mult).then_inc(hg_pool, 1)
            nc.gpsimd.tensor_tensor(qin, qin, zq[:, :, 0:L], ALU.mult).then_inc(hg_pool, 1)
            full(pool, ("ho", G4[3]))
            drained(pool, ("lin", "ev_in_b", 11))
            nc.gpsimd.tensor_tensor(hws2, cst("i2", 64).unsqueeze(1).unsqueeze(1).broadcast_to([128, HC, NS, HD]),
                                    zi[:, :, L:T].unsqueeze(3).broadcast_to([128, HC, NS, HD]),
                                    ALU.mult).then_inc(w_ready, 1)
            pool.wait_ge(shs_in, 16)
            nc.gpsimd.tensor_tensor(shs, shs, zf[:, :, L:T].unsqueeze(3).broadcast_to([128, HC, NS, HD]),
                                    ALU.mult).then_inc(sdec_ready, 1)
            drained(pool, ("kv", 7))
            store(A["o_hgrn"], SH[0], hg_stored)
            pool.wait_ge(sst_ready, 8)
            store(A["o_shs"], shs, hg_stored)

            def memory_io(l):
                full(pool, ("lin", "ev_out" if l == 0 else "od_out", KC - 1))
                pool.dma_start(h[:, :, 0:NM], A["memx"]).then_inc(memx_in, 16)
                pool.wait_ge(hn_done, hn_no[(f"memk{l}", MH - 1)] + 1)
                store(A["o_memk"][l], mk, mem_stored)
                drained(pool, ("lin", f"memv{l}", MH - 1))
                store(A["o_memv"][l], mv, mem_stored)

            def ffn_rows(l):
                full(pool, ("ss", "ffn", l))
                nc.gpsimd.memset(gb[:, :, 0:2], 0.0).then_inc(fpads, 1)
                pool.dma_start(fh, A["fh"][l]).then_inc(fh_in, 16)
                pool.wait_ge(fh_in, 16 * (l + 1))
                for i in range(FT):
                    drained(pool, ("lin", f"gu{l}", 2 * i))
                    nc.gpsimd.tensor_copy(fo[:, i, 0:2], gb[:, i % 3, 2 + L - 2:2 + L])
                    nc.gpsimd.tensor_copy(fo[:, i, 10:18], gb[:, i % 3, 2 + L:2 + T]).then_inc(fcopy_done, 1)
                nc.gpsimd.tensor_copy(fo[:, :, 2:10], fh[:, :, 8:16]).then_inc(fcopy_done, 1)
                pool.wait_ge(fcopy_done, (FT + 1) * (l + 1))
                store(A["o_ffn"][l], fo, ffn_stored)

            memory_io(0)
            ffn_rows(0)
            full(pool, ("ss", "mix", 1))
            pool.dma_start(s5b, A["s5b"]).then_inc(s5_in, 16)
            pool.dma_start(s5c, A["s5c"]).then_inc(s5_in, 16)
            full(pool, ("lin", "od_in", 15))
            pool.dma_start(s5h, A["s5h"]).then_inc(s5_in, 16)
            pool.wait_ge(hn_done, hn_no[("moba", 7)] + 1)
            store(A["o_k"], zo[:, 4:8, :], kv_stored)
            drained(pool, ("lin", "od_in", 11))
            store(A["o_v"], zo[:, 8:12, :], kv_stored)
            drained(pool, ("bx",))
            pool.dma_start(A["bias_x"], bxs).then_inc(bx_stored, 16)
            pool.wait_ge(bx_stored, 16)
            bx = A["bias_x"]
            pool.dma_start(hank, bass.AP(tensor=bx.tensor, offset=bx.offset,
                                         ap=[[1, 128], [512, H], [1, 384]])).then_inc(bias_in, 16)
            for n in range(NT):
                pool.wait_ge(s5_g, 2 * (n + 1))
                b = n % 2
                step(nc.gpsimd.tensor_tensor(pt_[:, b, 0, :], gg[:, b, 0, :], sinT[:, n, :], ALU.mult))
                step(nc.gpsimd.tensor_tensor(pt_[:, b, 1, :], gg[:, b, 1, :], cosT[:, n, :], ALU.mult))
                if n == 4:
                    full(pool, ("pt", "moba", 3))
                if n >= NHB:
                    full(pool, ("s5y", (n - NHB) // 4))
                nc.gpsimd.tensor_tensor(HH[n % NHB][:, 1, :], pt_[:, b, 0, :], pt_[:, b, 1, :],
                                        ALU.add).then_inc(s5_hi, 1)
                pool.wait_ge(s5_hi, 2 * n + 1)
                nc.gpsimd.tensor_copy(hl[:, 1, n:n + 1], HH[n % NHB][:, 1, L - 1:L]).then_inc(s5_hi, 1)
            pool.wait_ge(s5_hs, 3)
            store(A["o_s5"], s5o[:, :, :, :])
            memory_io(1)
            ffn_rows(1)
            drained(pool, ("lin", "down1", KC - 1))
            store(A["y"], x[:, :, :])
            for s_, n in ((stored, stores[0]), (hg_stored, 2), (mem_stored, 4), (ffn_stored, 2), (kv_stored, 2)):
                pool.wait_ge(s_, 16 * n)

        @block.scalar
        def _(act):
            step = Steps(act, act_step)

            def f(out, in_, func, **k):
                return nc.scalar.activation(out, in_, func, **k)

            def norm(i):
                kind, l = norms[i]
                w = NM if kind == "memkv" else T
                key = ("ss", kind, l)
                full(act, key)
                if seen["hn"]:
                    act.wait_ge(hr_ready, seen["hn"])
                seen["norm"] += 1
                f(lnb[:, 0:w], bank(key)[:, 0:w], ACT.Ln, scale=1.0 / D, bias=epsc).then_inc(
                    psum_free[no[key] % NBANK], 1)
                drained(act, key)
                f(rs[:, 0:w], lnb[:, 0:w], ACT.Exp, scale=-0.5).then_inc(r_ready, 1)

            seen = {"hn": 0, "norm": 0}

            def squares(name):
                for m in range(KC):
                    drained(act, ("lin", name, m))
                    f(sq[:, m, :], x[:, m, :], ACT.Square).then_inc(sq_ready, 1)

            def headnorm(name, n, w, mean, src, ready):
                base = hn_no[(name, 0)]
                for i in range(n + 1):
                    if i < n:
                        ready(i)
                        f(hsq[:, (base + i) % 2, 0:w], src(i), ACT.Square).then_inc(hsq_ready, 1)
                    if i >= 1:
                        j = base + i - 1
                        key = ("hn", name, i - 1)
                        full(act, key)
                        act.wait_ge(r_ready, seen["norm"])
                        if j:
                            act.wait_ge(hr_ready, j)
                        seen["hn"] = j + 1
                        drain(f(lnb[:, 0:w], bank(key)[:, 0:w], ACT.Ln, scale=mean, bias=epsc), key)
                        drained(act, key)
                        if j >= 2:
                            act.wait_ge(hn_done, j - 1)
                        f(hr[:, j % 2, 0:w], lnb[:, 0:w], ACT.Exp, scale=-0.5).then_inc(hr_ready, 1)

            def copy_out(key, dst, src):
                full(act, key)
                drain(f(dst, src, ACT.Copy), key)

            def samples_out(name, dst, nh):
                n = 2 if nh == MH else 4
                act.wait_ge(qz_ready, ["mem0", "moba", "mem1"].index(name) * 2 + 2)
                for i in range(n):
                    key = ("so", name, i)
                    full(act, key)
                    for s_ in range(NS // n * i, NS // n * (i + 1)):
                        r = 32 * (s_ % 4)
                        ins = f(dst[r:r + nh, s_ // 4, :], bank(key)[r:r + nh, :], ACT.Copy)
                    drain(ins, key)

            def attend(name, n, hd, after=None):
                pbuf, ptb = att_buf[name]
                for i in range(n + 2):
                    if i < n:
                        j = at_no[(name, i)]
                        act.wait_ge(smax_ready, j + 1)
                        b = j % 2
                        for qt in range(2):
                            v = pbuf[:, i % 2, qt * L:(qt + 1) * L]
                            ins = f(v, v, ACT.Exp, bias=smx[:, b, 0, qt:qt + 1], scale=1.0,
                                    accum_out=smx[:, b, 1, qt:qt + 1])
                        ins.then_inc(p_exp, 1)
                    if 0 <= i - 1 < n:
                        key = ("PT", name, i - 1)
                        full(act, key)
                        drain(f(ptb[:, (i - 1) % 2, :], bank(key)[:, :], ACT.Copy), key)
                    if 0 <= i - 2 < n:
                        k = i - 2
                        key = ("O", name, k)
                        p0 = 0 if hd == 128 else 64 * (k % 2)
                        c = k if hd == 128 else k // 2
                        copy_out(key, mix[p0:p0 + hd, c, 0:L], bank(key)[p0:p0 + hd, 0:L])
                    if after:
                        after(i)

            epsc = epst[:, 0:1]
            act.wait_ge(eps_ready, 1)
            act.wait_ge(x_in, 16)
            for m in range(KC):
                f(sq[:, m, :], x[:, m, :], ACT.Square).then_inc(sq_ready, 1)
            act.wait_ge(vec_in, 16)
            act.wait_ge(lb_step, 1)
            f(lbt[:, 0:3, :], lbt[:, 0:3, :], ACT.Exp).then_inc(lb_step, 1)
            f(par[:, 0, :], cols("s5_dt", NT), ACT.Exp).then_inc(s5_par, 1)
            norm(0)
            act.wait_ge(s5_par, 2)
            f(par[:, 1, :], par[:, 1, :], ACT.Exp)
            f(par[:, 4, :], par[:, 4, :], ACT.Sin)
            f(par[:, 5, :], par[:, 5, :], ACT.Sin).then_inc(s5_par, 1)
            full(act, ("ab",))
            f(gs[0:8, 0, :], bank(("ab",))[0:8, 0:T], ACT.Exp, scale=-1.0).then_inc(gate_rows, 1)
            f(aexp[0:8, :], col("small", 1, 0, 8), ACT.Exp).then_inc(gate_rows, 1)
            act.wait_ge(gate_rows, 3)
            step(f(gs[0:8, 4, :], gs[0:8, 4, :], ACT.Exp))
            f(gs[0:8, 4, :], gs[0:8, 4, :], ACT.Ln, bias=onec[0:8, 0:1]).then_inc(gate_rows, 1)
            act.wait_ge(gate_rows, 5)
            f(gs[0:8, 2, :], gs[0:8, 4, :], ACT.Exp)
            f(gs[0:8, 3, 0:L], gs[0:8, 3, 0:L], ACT.Exp).then_inc(gate_rows, 1)
            for m in range(16):
                key = ("lin", "ev_in_a", m)
                full(act, key)
                if m < 12:
                    drain(f(zqkv[:, m, 3:3 + T], bank(key)[:, 0:T], ACT.Copy), key)
                else:
                    drain(f(zg[:, m - 12, :], bank(key)[:, 0:T], ACT.Silu), key)
                if 2 <= m < 14:
                    act.wait_ge(conv_done, m - 1)
                    f(qkv[:, m - 2, :], qkv[:, m - 2, :], ACT.Silu).then_inc(silu_done, 1)
            act.wait_ge(silu_done, 12)
            headnorm("l2", 8, T, 1.0, lambda i: qkv[:, i, :], lambda i: None)
            for t in range(NCH):
                copy_out(("trk", t), ketok[:, t, :], bank(("trk", t))[:, :])
                copy_out(("trv", t), vbtok[:, t, :], bank(("trv", t))[:, :])
            for gi, g in enumerate(G4):
                if gi >= 2:
                    drained(act, ("KK", G4[gi - 2]))
                full(act, ("DT", g))
                drain(f(dt_[:, gi % 2, :], bank(("DT", g))[:, :], ACT.Exp), ("DT", g))
            for gi, g in enumerate(G4):
                copy_out(("X1", g), xx[:, gi, :], bank(("X1", g))[:, :])
            for l in range(1, LEV):
                for gi, g in enumerate(G4):
                    copy_out(("T1", l, g), t1[:, gi, :], bank(("T1", l, g))[:, :])

            def o_copy(key, p, at, t):
                full(act, key)
                drain(f(oT[64 * p:64 * p + 64, :, t * 128:(t + 1) * 128],
                        blocks(key, 4, 64 * p, 64 * p + 64), ACT.Copy), key)

            def so_copy(name):
                for p in range(2):
                    key = ("sO", name, p)
                    full(act, key)
                    drain(f(oT[64 * p:64 * p + 64, :, L:T],
                            bank(key)[64 * p:64 * p + 64, 0:32].rearrange("p (c s) -> p c s", c=HC),
                            ACT.Copy), key)

            for t in range(NCH):
                copy_out(("u", t), utok, bank(("u", t))[:, :])
                for p in range(2):
                    o_copy(("o", t, p), p, 0, t)
            so_copy("gdn")

            def so_done(name):
                for p in range(2):
                    drained(act, ("sO", name, p))

            headnorm("gdn", HC, T, 1.0 / HD, lambda i: oT[:, i, :], lambda i: so_done("gdn") if i == 0 else None)
            for m in range(16):
                key = ("lin", "ev_in_b", m)
                b = bank(key)[:, 0:T]
                full(act, key)
                if m < 4:
                    drain(f(zq[:, m, :], b, ACT.Silu), key)
                elif m < 8:
                    f(zf[:, m - 4, :], b, ACT.Sigmoid)
                    drain(f(zk[:, m - 4, :], b, ACT.Sigmoid, scale=-1.0), key)
                elif m < 12:
                    drain(f(zi[:, m - 8, :], b, ACT.Copy), key)
                else:
                    drain(f(zh[:, m - 12, :], b, ACT.Silu), key)
            act.wait_ge(fk_ready, HC)
            f(lf, zf[:, :, 0:L], ACT.Ln).then_inc(lf_ready, 1)
            act.wait_ge(dec_ready, 2)
            f(qx, d1, ACT.Exp).then_inc(exp_ready, 1)
            f(kx, d1, ACT.Exp, scale=-1.0).then_inc(exp_ready, 1)
            f(qin, bcs, ACT.Exp).then_inc(exp_ready, 1)
            f(ko, d2, ACT.Exp).then_inc(exp_ready, 1)
            for t in range(NCH):
                copy_out(("htk", t), hkt[:, t, :], bank(("htk", t))[:, :])
                copy_out(("htv", t), hvt[:, t, :], bank(("htv", t))[:, :])
            act.wait_ge(mix_ready, HC)
            for t, p in G4:
                o_copy(("ho", (t, p)), p, 0, t)
            so_copy("hgrn")
            headnorm("hgrn", HC, T, 1.0 / HD, lambda i: oT[:, i, :], lambda i: so_done("hgrn") if i == 0 else None)
            squares("ev_out")

            def memory(l):
                act.wait_ge(memx_in, 16 * (l + 1))
                act.wait_ge(hg_stored if l == 0 else kv_stored, 32)
                full(act, ("lin", "ev_out" if l == 0 else "od_out", KC - 1))
                for m in range(KC):
                    f(mh[:, m, :], h[:, m, 0:NM], ACT.Square).then_inc(msq_ready, 1)
                norm(norms.index(("memkv", l)))
                for m in range(MH):
                    copy_out(("lin", f"memk{l}", m), mk[:, m, :], bank(("lin", f"memk{l}", m))[:, 0:NM])
                headnorm(f"memk{l}", MH, NM, 1.0 / 128, lambda i: mk[:, i, :],
                         lambda i: drained(act, ("lin", f"memk{l}", i)))
                for m in range(MH):
                    copy_out(("lin", f"memv{l}", m), mv[:, m, :], bank(("lin", f"memv{l}", m))[:, 0:NM])
                for t in range(2):
                    copy_out(("mvt", l, t), mvt[:, t, :], bank(("mvt", l, t))[:, :])
                norm(norms.index(("mem", l)))
                for m in range(MH):
                    copy_out(("lin", f"wq{l}", m), mq[:, m, :], bank(("lin", f"wq{l}", m))[:, 0:T])
                headnorm(f"memq{l}", MH, T, 1.0 / 128, lambda i: mq[:, i, :],
                         lambda i: drained(act, ("lin", f"wq{l}", i)))
                name = f"mem{l}"

                def probs(i):
                    if i in (2, 4):
                        g = i // 2 - 1
                        key = ("sc", name, g)
                        act.wait_ge(mx_ready, MXN[name] + g + 1)
                        drain(f(mpm[:, g, :], bank(key)[:, 0:NM], ACT.Exp, bias=msm[:, g, 1:2], scale=128 ** -0.5,
                                accum_out=msm[:, g, 2:3]), key)
                attend(name, MH, 128, probs)
                copy_out(("pt", name, 0), mps, bank(("pt", name, 0))[:, :].rearrange(
                    "p (n j h) -> p n j h", n=4, j=4)[:, :, :, 0:MH])
                samples_out(name, mos, MH)
                squares(f"wo{l}")

            def ffn(l):
                norm(norms.index(("ffn", l)))
                act.wait_ge(fpads, l + 1)
                for i in range(FT + 1):
                    if i < FT:
                        key = ("lin", f"gu{l}", 2 * i)
                        full(act, key)
                        n = l * FT + i
                        if i >= 3:
                            act.wait_ge(fconv_done, n - 2)
                            act.wait_ge(fcopy_done, l * (FT + 1) + i - 2)
                        drain(f(gb[:, i % 3, 2:2 + T], bank(key)[:, 0:T], ACT.Copy), key)
                    if i >= 1:
                        n = l * FT + i - 1
                        act.wait_ge(fconv_done, n + 1)
                        if i >= 3:
                            drained(act, ("lin", f"gu{l}", 2 * (i - 3) + 1))
                        f(csil[:, (i - 1) % 2, :], cacc[:, (i - 1) % 2, :], ACT.Silu).then_inc(fsilu_done, 1)
                if l == 0:
                    squares("down0")

            memory(0)
            ffn(0)
            norm(norms.index(("mix", 1)))
            act.wait_ge(mem_stored, 32)
            for m in range(16):
                key = ("lin", "od_in", m)
                copy_out(key, zo[:, m, :], bank(key)[:, 0:T])
            headnorm("moba", 8, T, 1.0 / HD, lambda i: zo[:, i, :],
                     lambda i: drained(act, ("lin", "od_in", i)))
            for t in range(2):
                copy_out(("vt", t), ovt[:, t, :], bank(("vt", t))[:, :])
            copy_out(("bx",), bxs, bank(("bx",))[0:8, 0:512])
            for i in range(2):
                copy_out(("bs", i), bsp[:, i, :], bank(("bs", i))[:, :])
            attend("moba", H, 64)
            act.wait_ge(mx_ready, MXN["moba"] + 1)
            for g in range(2):
                for b in range(4):
                    v = ssc[:, g, 256 * b:256 * (b + 1)]
                    ins = f(v, v, ACT.Exp, bias=gsm[:, 5, 4 * g + b:4 * g + b + 1], scale=1.0,
                            accum_out=gsm[:, 6, 4 * g + b:4 * g + b + 1])
                    if b % 2:
                        ins.then_inc(pp_ready, 1)
                f(gs2[:, 4, g:g + 1], gs2[:, 2, g:g + 1], ACT.Exp, bias=gs2[:, 3, g:g + 1], scale=1.0)
            ins = f(gs2[:, 9, 0:1], gs2[:, 2, 0:1], ACT.Copy)
            ins.then_inc(pp_ready, 1)
            for i in range(4):
                key = ("pt", "moba", i)
                copy_out(key, spt[:, i], bank(key)[:, :].rearrange("p (n j h) -> p n j h", n=4, j=4)[:, :, :, 0:H])
            samples_out("moba", osm, H)
            act.wait_ge(kv_stored, 32)
            for c in range(HC):
                drained(act, ("s5y", c))
                f(ygl[:, c, :], tmpy[:, c, :], ACT.Gelu_apprx_tanh).then_inc(s5_gl2, 1)
            drained(act, ("sx", "moba"))
            for c in range(HC):
                key = ("lin", "glu", 2 * c + 1)
                full(act, key)
                if c >= 2:
                    drained(act, ("lin", "glu", 2 * (c - 2)))
                drain(f(tmp[:, c % 2, :], bank(key)[:, 0:T], ACT.Sigmoid), key)
            squares("od_out")
            memory(1)
            ffn(1)

        @block.tensor
        def _(pe):
            at = [0]

            def begin(key):
                assert order[at[0]] == key, (order[at[0]], key)
                if at[0] >= NBANK:
                    pe.wait_ge(psum_free[at[0] % NBANK], at[0] // NBANK)
                return bank(key)

            def end(ins):
                ins.then_inc(psum_full, 1)
                at[0] += 1

            def mm(out, lhsT, rhs, start=True, stop=True):
                return nc.tensor.matmul(out, lhsT, rhs, start=start, stop=stop, skip_group_check=True)

            def tr(out, in_):
                return nc.tensor.transpose(out, in_, ident)

            def norm(i):
                kind, l = norms[i]
                w = NM if kind == "memkv" else T
                b = begin(("ss", kind, l))
                src = mh if kind == "memkv" else sq
                for k in range(KC):
                    if kind == "memkv":
                        pe.wait_ge(msq_ready, KC * l + k + 1)
                    else:
                        pe.wait_ge(sq_ready, KC * xnorms.index((kind, l)) + k + 1)
                    ins = mm(b[:, 0:w], ones, src[:, k, 0:w], k == 0, k == KC - 1)
                end(ins)

            def hready(i):
                return lambda k: pe.wait_ge(h_ready, KC * i + k + 1)

            def open_(key):
                assert at[0] <= no[key] < at[0] + NBANK
                if no[key] >= NBANK:
                    pe.wait_ge(psum_free[no[key] % NBANK], no[key] // NBANK)
                return bank(key)

            def close(ins, key):
                assert order[at[0]] == key
                end(ins)

            def slot(name, i):
                n = slot_of[(name, i)]
                pe.wait_ge(ring_full[n % SLOTS], slot_value[n])
                return ring[:, n % SLOTS, :]

            def slot_done(ins, name, i):
                last = slots[slot_of[(name, i)]][4]
                if last[0] == "used":
                    ins.then_inc(pages_used, 1)
                else:
                    close(ins, last)

            def lin(name, m, kc, per_slot, src, w, ready=None):
                b = begin(("lin", name, m))
                s = slot_of[(name, m)]
                if m % per_slot == 0:
                    pe.wait_ge(ring_full[s % SLOTS], slot_value[s])
                for k in range(kc):
                    if ready and m == 0:
                        ready(k)
                    o = ((m % per_slot) * kc + k) * 128
                    ins = mm(b[:, 0:w], ring[:, s % SLOTS, o:o + 128], src[:, k, 0:w], k == 0, k == kc - 1)
                end(ins)

            def headnorm(name, n, w, lhsT):
                base = hn_no[(name, 0)]
                for i in range(n):
                    b = begin(("hn", name, i))
                    pe.wait_ge(hsq_ready, base + i + 1)
                    end(mm(b[:, 0:w], lhsT, hsq[:, (base + i) % 2, 0:w]))

            def transposes(key, srcs):
                b = begin(key)
                for j, v in enumerate(srcs):
                    ins = tr(b[:, 128 * j:128 * (j + 1)], v)
                end(ins)

            def attend(name, n, hd, q, k, vt, between):
                pbuf, ptb = att_buf[name]
                for i in range(n + 2):
                    if i < n:
                        b = begin(("S", name, i))
                        p0, c = (0, i) if hd == 128 else (64 * (i % 2), i // 2)
                        for qt in range(2):
                            ins = mm(b[:, qt * L:(qt + 1) * L], q[p0:p0 + hd, c, qt * 128:(qt + 1) * 128],
                                     k[p0:p0 + hd, c, 0:L])
                        end(ins)
                    between(i, 0)
                    if 0 <= i - 1 < n:
                        b = begin(("PT", name, i - 1))
                        pe.wait_ge(p_ready, at_no[(name, i - 1)] + 1)
                        for kt in range(2):
                            for qt in range(2):
                                ins = tr(b[:, kt * L + qt * 128:kt * L + (qt + 1) * 128],
                                         pbuf[:, (i - 1) % 2, qt * L + kt * 128:qt * L + (kt + 1) * 128])
                        end(ins)
                    between(i, 1)
                    if 0 <= i - 2 < n:
                        j = i - 2
                        b = begin(("O", name, j))
                        drained(pe, ("PT", name, j))
                        p0 = 0 if hd == 128 else 64 * (j % 2)
                        for kt in range(2):
                            ins = mm(b[p0:p0 + hd, 0:L], vt[:, kt, j * hd:(j + 1) * hd],
                                     ptb[:, j % 2, kt * L:(kt + 1) * L], kt == 0, kt == 1)
                        end(ins)

            def state_update(name, w2, n):
                pe.wait_ge(w_ready, n)
                for c in range(HC):
                    b = begin(("su", name, c))
                    end(mm(b[:, :], bd, w2[:, c, :, :].rearrange("p s v -> p (s v)")))

            def state_out(name, st, q, n):
                pe.wait_ge(sst_ready, 4 * n)
                for p in range(2):
                    b = begin(("sO", name, p))
                    for c in range(HC):
                        for s in range(NS):
                            ins = mm(b[64 * p:64 * p + 64, c * NS + s:c * NS + s + 1],
                                     st[64 * p:64 * p + 64, c, s, :], q[64 * p:64 * p + 64, c, L + s:L + s + 1])
                    end(ins)

            pe.wait_ge(con_in, 16)
            norm(0)
            b = begin(("ab",))
            pe.wait_ge(vec_in, 16)
            for k in range(KC):
                hready(0)(k)
                ins = mm(b[0:40, 0:T], cols("w_ab", 40, 40 * k), h[:, k, :], k == 0, k == KC - 1)
            end(ins)
            for m in range(16):
                lin("ev_in_a", m, KC, 2, h, T)
            headnorm("l2", 8, T, bd)
            pe.wait_ge(gate_rows, 6)
            for c in range(HC):
                for name, r, w in (("bcB", 0, T), ("bcG", 2, T), ("bcL", 3, L)):
                    b = begin((name, c))
                    end(mm(b[:, 0:w], cst("selc", i=c, p=8), gs[0:8, r, 0:w]))
            for t in range(NCH):
                drained(pe, ("bcL", HC - 1))
                transposes(("trk", t), [ke[:, c, t * 128:(t + 1) * 128] for c in range(HC)])
                transposes(("trv", t), [vb[:, c, t * 128:(t + 1) * 128] for c in range(HC)])
            kn = qkv[:, 4:8, :]
            for gi, (t, p) in enumerate(G4):
                ts, ps = slice(t * 128, (t + 1) * 128), slice(64 * p, 64 * p + 64)
                b = begin(("DT", (t, p)))
                for c in range(HC):
                    hh_, o = 2 * c + p, b[:, c * 128:(c + 1) * 128]
                    mm(o, cst("selh", i=hh_, p=8), gs[0:8, 4, ts], True, False)
                    mm(o, gs[0:8, 4, ts], cst("nselh", i=hh_, p=8), False, False)
                    ins = mm(o, ident, cst("neg"), False, True)
                end(ins)
                b = begin(("QK", (t, p)))
                for c in range(HC):
                    ins = mm(b[:, c * 128:(c + 1) * 128], kn[ps, c, ts], qkv[ps, c, ts])
                end(ins)
                b = begin(("KK", (t, p)))
                for c in range(HC):
                    ins = mm(b[:, c * 128:(c + 1) * 128], kn[ps, c, ts], kb[ps, c, ts])
                end(ins)

            def blk(v, gi, c):
                return v[:, gi, c * 128:(c + 1) * 128]

            for gi, g in enumerate(G4):
                pe.wait_ge(xt_ready, gi + 1)
                transposes(("X1", g), [blk(xt, gi, c) for c in range(HC)])
            for l in range(1, LEV):
                for gi, g in enumerate(G4):
                    n = (l - 1) * 4 + gi
                    b = begin(("T1", l, g))
                    pe.wait_ge(ml_ready, n + 1)
                    drained(pe, ("X1", g) if l == 1 else ("Z", l - 1, g))
                    for c in range(HC):
                        ins = mm(b[:, c * 128:(c + 1) * 128], blk(ml, n % 2, c), blk(xx, gi, c))
                    end(ins)
                for gi, g in enumerate(G4):
                    b = begin(("ZT", l, g))
                    drained(pe, ("T1", l, g))
                    if l > 1:
                        drained(pe, ("ZT", l - 1, g))
                    for c in range(HC):
                        ins = mm(b[:, c * 128:(c + 1) * 128], blk(t1, gi, c), blk(xt, gi, c))
                    end(ins)
                    if l < LEV - 1:
                        b = begin(("Z", l, g))
                        for c in range(HC):
                            ins = mm(b[:, c * 128:(c + 1) * 128], blk(xt, gi, c), blk(t1, gi, c))
                        end(ins)
            for g in G4:
                drained(pe, ("ZT", LEV - 1, g))
            for t in range(NCH):
                ts = slice(t * 128, (t + 1) * 128)
                if t:
                    drained(pe, ("S", "gdn", t - 1))
                    for p in range(2):
                        ps = slice(64 * p, 64 * p + 64)
                        b = begin(("ks", p))
                        for c in range(HC):
                            ins = mm(b[:, c * 64:(c + 1) * 64], bk[ps, c, ts], sg[ps, c, :])
                        end(ins)
                    drained(pe, ("ks", 1))
                b = begin(("u", t))
                for hh_ in range(H):
                    cs = slice(hh_ * 64, (hh_ + 1) * 64)
                    ins = mm(b[:, cs], blk(xt, 2 * t + hh_ % 2, hh_ // 2), (rhst if t else vbtok[:, 0, :])[:, cs])
                end(ins)
                drained(pe, ("u", t))
                for p in range(2):
                    ps = slice(64 * p, 64 * p + 64)
                    b = begin(("o", t, p))
                    for c in range(HC):
                        hh_, o = 2 * c + p, b[ps, c * 128:(c + 1) * 128]
                        if t:
                            mm(o, sg[ps, c, :], qe[ps, c, ts], True, False)
                        ins = mm(o, utok[:, hh_ * 64:(hh_ + 1) * 64], blk(qkd, 2 * t + p, c), t == 0, True)
                    end(ins)
                b = begin(("S", "gdn", t))
                for hh_ in range(H):
                    ps, cs = slice(64 * (hh_ % 2), 64 * (hh_ % 2) + 64), slice(hh_ * 64, (hh_ + 1) * 64)
                    ins = mm(b[ps, (hh_ // 2) * 64:(hh_ // 2 + 1) * 64], ketok[:, t, cs], utok[:, cs])
                end(ins)
            state_update("gdn", ws2, 2)
            state_out("gdn", sgs, qkv, 1)
            headnorm("gdn", HC, T, bd)
            for m in range(16):
                lin("ev_in_b", m, KC, 2, h, T)
            pe.wait_ge(hg_dve, 2)
            pe.wait_ge(hg_pool, 3)
            for t in range(NCH):
                ts = slice(t * 128, (t + 1) * 128)
                transposes(("htk", t), [ko[:, c, ts] for c in range(HC)])
                drained(pe, ("lin", "ev_in_b", 11))
                transposes(("htv", t), [zi[:, c, ts] for c in range(HC)])
            for t, p in G4:
                ts, ps = slice(t * 128, (t + 1) * 128), slice(64 * p, 64 * p + 64)
                b = begin(("att", (t, p)))
                for c in range(HC):
                    ins = mm(b[:, c * 128:(c + 1) * 128], kx[ps, c, ts], qx[ps, c, ts])
                end(ins)
            for t in range(NCH):
                drained(pe, ("htk", t))
                drained(pe, ("htv", t))
            for k in range(L // HCK):
                t, r = k // 4, k % 4
                rs_ = slice(32 * r, 32 * r + 32)
                b = begin(("kv", k))
                for hh_ in range(H):
                    ps, cs = slice(64 * (hh_ % 2), 64 * (hh_ % 2) + 64), slice(hh_ * 64, (hh_ + 1) * 64)
                    ins = mm(b[ps, (hh_ // 2) * 64:(hh_ // 2 + 1) * 64], hkt[rs_, t, cs], hvt[rs_, t, cs])
                end(ins)
            drained(pe, ("kv", 7))
            for gi, (t, p) in enumerate(G4):
                ps = slice(64 * p, 64 * p + 64)
                b = begin(("ho", (t, p)))
                drained(pe, ("att", (t, p)))
                for c in range(HC):
                    hh_ = 2 * c + p
                    ins = mm(b[ps, c * 128:(c + 1) * 128], hvt[:, t, hh_ * 64:(hh_ + 1) * 64],
                             blk(attb, gi, c), True, False)
                    for r in range(4):
                        k = 4 * t + r
                        if k:
                            ins = mm(b[ps, c * 128 + 32 * r:c * 128 + 32 * r + 32], SH[k][ps, c, :],
                                     qin[ps, c, 32 * k:32 * k + 32], False, r == 3)
                end(ins)
            state_update("hgrn", hws2, 3)
            state_out("hgrn", shs, zq, 2)
            headnorm("hgrn", HC, T, bd)
            for m in range(KC):
                lin("ev_out", m, KC, 2, mix, T, lambda k: pe.wait_ge(mix_ready, k + 1))

            def memory(l):
                i = norms.index(("memkv", l))
                norm(i)
                for m in range(MH):
                    lin(f"memk{l}", m, KC, 2, mh, NM, hready(i))
                headnorm(f"memk{l}", MH, NM, ones)
                for m in range(MH):
                    lin(f"memv{l}", m, KC, 2, mh, NM)
                for t in range(2):
                    drained(pe, ("lin", f"memv{l}", MH - 1))
                    transposes(("mvt", l, t), [mv[:, hh_, t * 128:(t + 1) * 128] for hh_ in range(MH)])
                norm(i + 1)
                for m in range(MH):
                    lin(f"wq{l}", m, KC, 2, h, T, hready(i + 1))
                headnorm(f"memq{l}", MH, T, ones)
                pe.wait_ge(hn_done, hn_no[(f"memq{l}", MH - 1)] + 1)
                for t in range(2):
                    drained(pe, ("mvt", l, t))
                name = f"mem{l}"

                def keys(i, part):
                    if part or i >= 4:
                        return
                    key = ("sc", name, i // 2)
                    b = open_(key) if i % 2 == 0 else bank(key)
                    if i == 0:
                        pe.wait_ge(qz_ready, QZN[name] + 1)
                    r = slot(f"ck{l}", i)
                    for s in (2 * i, 2 * i + 1):
                        j = s % 4
                        for hh_ in range(MH):
                            o = (s % 2) * 1024 + hh_ * 256
                            ins = mm(b[32 * j:32 * j + 32, 0:NM], mqz[:, hh_, s, :], r[:, o:o + NM],
                                     hh_ == 0, hh_ == MH - 1)
                    slot_done(ins, f"ck{l}", i)
                attend(name, MH, 128, mq, mk, mvt, keys)
                b = begin(("pt", name, 0))
                for g in range(2):
                    drained(pe, ("sc", name, g))
                    for t in range(2):
                        ins = tr(b[:, (2 * g + t) * 128:(2 * g + t + 1) * 128], mpm[:, g, 128 * t:128 * t + 128])
                end(ins)
                drained(pe, ("pt", name, 0))
                for i in range(4):
                    key = ("so", name, i // 2)
                    b = open_(key) if i % 2 == 0 else bank(key)
                    r = slot(f"cv{l}", i)
                    for s in (2 * i, 2 * i + 1):
                        j = s % 4
                        for t in range(2):
                            o = (s % 2) * 1024 + t * 512
                            ins = mm(b[32 * j:32 * j + MH, :], mps[:, 2 * (s // 4) + t, j, :], r[:, o:o + 512],
                                     t == 0, t == 1)
                    slot_done(ins, f"cv{l}", i)
                b = begin(("sx", name))
                for g in range(2):
                    drained(pe, ("so", name, g))
                pe.wait_ge(sel_ready, SELN[name])
                for c in range(MH):
                    for g in range(2):
                        ins = mm(b[:, 8 * c + 4 * g:8 * c + 4 * g + 4], mos[:, g, 128 * c:128 * c + 128],
                                 msel[:, g, 4 * c:4 * c + 4])
                end(ins)
                for hh_ in range(MH):
                    drained(pe, ("O", f"mem{l}", hh_))
                drained(pe, ("sx", name))
                for m in range(KC):
                    lin(f"wo{l}", m, MH, 4, mix, T)

            def ffn(l):
                i = norms.index(("ffn", l))
                norm(i)
                for m in range(2 * FT):
                    lin(f"gu{l}", m, KC, 2, h, T, hready(i))
                for m in range(KC):
                    lin(f"down{l}", m, FT, 1, act_, T, lambda k: drained(pe, ("lin", f"gu{l}", 2 * k + 1)))

            memory(0)
            ffn(0)
            norm(norms.index(("mix", 1)))
            for m in range(16):
                lin("od_in", m, KC, 2, h, T, hready(norms.index(("mix", 1))))
            headnorm("moba", 8, T, bd)
            for m in range(8, 12):
                drained(pe, ("lin", "od_in", m))
            for t in range(2):
                transposes(("vt", t), [zo[:, 8 + c, t * 128:(t + 1) * 128] for c in range(HC)])
            b = begin(("bx",))
            pe.wait_ge(relb_ready, 2)
            end(mm(b[0:8, :], relb[0:33, :], cst("hotx", 512, p=33)))
            for i in range(2):
                b = begin(("bs", i))
                o = CON["hots"] + 512 * i
                end(mm(b[:, :], relr, con[0:32, o:o + 512]))
            b = begin(("self",))
            pe.wait_ge(qk_ready, 1)
            for g in range(2):
                for c in range(HC):
                    ins = mm(b[:, g:g + 1], kz[:, c, 4 * g:4 * g + 4, :].rearrange("p s h -> p (s h)"),
                             ones[:, 0:1], c == 0, c == HC - 1)
            end(ins)
            pe.wait_ge(hn_done, hn_no[("moba", 7)] + 1)
            for t in range(2):
                drained(pe, ("vt", t))

            def pages(i, part):
                if i >= H:
                    return
                n = 2 * i + part
                key = ("sc", "moba", n // 4)
                b = open_(key) if n % 4 == 0 else bank(key)
                r = slot("pk", n)
                s, j = 4 * (n // 8) + n % 4, n % 4
                for c in range(HC):
                    ins = mm(b[32 * j:32 * j + 32, :], qz[:, c, s, :],
                             r[:, 0:2048].rearrange("p (g c t) -> p g c t", g=4, c=HC)[:, :, c, :],
                             c == 0, c == HC - 1)
                slot_done(ins, "pk", n)
            pe.wait_ge(qz_ready, QZN["moba"] + 1)
            attend("moba", H, 64, zo[:, 0:4, :], zo[:, 4:8, :], ovt, pages)
            pe.wait_ge(s5_in, 48)
            pe.wait_ge(s5_in, 48)
            for c in range(HC):
                drained(pe, ("lin", "od_in", 12 + c))
            for j in range(4):
                b = begin(("s5s", j))
                js = slice(32 * j, 32 * j + 32)
                for c in range(HC):
                    for q in range(2):
                        i_ = (c * 2 + q) * NS
                        ins = mm(b[:, i_:i_ + NS], s5b[js, q, c, :], zo[js, 12 + c, L:T])
                end(ins)

            def y_tile(c):
                b = begin(("s5y", c))
                if c == 0:
                    pe.wait_ge(s5_hs, 2)
                for j in range(4):
                    n = 4 * c + j
                    o = b[32 * j:32 * j + 32, 0:L]
                    pe.wait_ge(s5_hr, n + 1)
                    pe.wait_ge(s5_hi, 2 * n + 1)
                    mm(o, s5cp[:, 0, n, :], HH[n % NHB][:, 0, :], True, False)
                    mm(o, s5cp[:, 1, n, :], HH[n % NHB][:, 1, :], False, True)
                    o = b[32 * j:32 * j + 32, L:T]
                    mm(o, s5c[:, 0, n, :], hsS[:, 0, n, :], True, False)
                    ins = mm(o, s5cp[:, 2, n, :], hsS[:, 1, n, :], False, True)
                end(ins)

            def x_tile(n):
                c, js = n // 4, slice(32 * (n % 4), 32 * (n % 4) + 32)
                b = begin(("s5x", n))
                for q in range(2):
                    ins = mm(b[:, q * L:(q + 1) * L], s5b[js, q, c, :], zo[js, 12 + c, 0:L])
                end(ins)

            x_tile(0)
            x_tile(1)
            for i in range(4):
                b = begin(("pt", "moba", i))
                pe.wait_ge(pp_ready, i + 1)
                for n in range(4):
                    ins = tr(b[:, 128 * n:128 * n + 128],
                             ssc[:, i // 2, 512 * (i % 2) + 128 * n:512 * (i % 2) + 128 * n + 128])
                end(ins)
            for i in range(4):
                drained(pe, ("pt", "moba", i))
            for n in range(NT):
                key = ("so", "moba", n // 4)
                b = open_(key) if n % 4 == 0 else bank(key)
                r = slot("pv", n)
                s, half = n // 2, n % 2
                j = s % 4
                for g in range(4):
                    ins = mm(b[32 * j:32 * j + H, :], spt[:, 2 * (s // 4) + half, g, j, :],
                             r[:, 512 * g:512 * g + 512], half == 0 and g == 0, half == 1 and g == 3)
                slot_done(ins, "pv", n)
                if n + 2 < NT:
                    x_tile(n + 2)
                if n % 4 == 2 and n > 2:
                    y_tile(n // 4 - 1)
            y_tile(3)
            b = begin(("sx", "moba"))
            for i in range(4):
                drained(pe, ("so", "moba", i))
            pe.wait_ge(sel_ready, SELN["moba"])
            for p in range(2):
                ps = slice(64 * p, 64 * p + 64)
                for c in range(HC):
                    for g in range(2):
                        hh_ = 2 * c + p
                        mm(b[ps, 8 * c + 4 * g:8 * c + 4 * g + 4], osm[:, g, 64 * hh_:64 * hh_ + 64],
                           sel2[:, 0, g, 4 * hh_:4 * hh_ + 4])
                for c in range(HC):
                    for g in range(2):
                        hh_ = 2 * c + p
                        ins = mm(b[ps, 32 + 8 * c + 4 * g:32 + 8 * c + 4 * g + 4], ones[:, 0:64],
                                 sel2[:, 1, g, 4 * hh_:4 * hh_ + 4])
            end(ins)
            for m in range(8):
                lin("glu", m, HC, 4, ygl, T, lambda k: pe.wait_ge(s5_gl2, k + 1))
            for j in range(H):
                drained(pe, ("O", "moba", j))
            for c in range(HC):
                drained(pe, ("lin", "glu", 2 * c))
            drained(pe, ("sx", "moba"))
            for m in range(KC):
                lin("od_out", m, KC, 2, mix, T)
            memory(1)
            ffn(1)
            assert at[0] == len(order)

        @block.vector
        def _(dve):
            step = Steps(dve, dve_step)
            V = nc.vector

            def tt(out, a, b, op):
                return V.tensor_tensor(out, a, b, op)

            def stt(out, a, s, b, op0, op1):
                return V.scalar_tensor_tensor(out, a, s, b, op0, op1)

            def norm(i):
                kind, l = norms[i]
                w = NM if kind == "memkv" else T
                dst = mh if kind == "memkv" else h
                src = h if kind == "memkv" else x
                dve.wait_ge(r_ready, i + 1)
                for k in range(KC):
                    stt(dst[:, k, 0:w], src[:, k, 0:w], col(NORM_G[kind], KC * l + k), rs[:, 0:w],
                        ALU.mult, ALU.mult).then_inc(h_ready, 1)

            def residual(name):
                for m in range(KC):
                    key = ("lin", name, m)
                    full(dve, key)
                    drain(tt(x[:, m, :], x[:, m, :], bank(key)[:, 0:T], ALU.add), key)

            def headnorm(name, n, w, src, gain, dst, after=None):
                base = hn_no[(name, 0)]
                for i in range(n):
                    dve.wait_ge(hr_ready, base + i + 1)
                    stt(dst(i), src(i), gain(i), hr[:, (base + i) % 2, 0:w], ALU.mult, ALU.mult).then_inc(hn_done, 1)
                    if after:
                        dve.wait_ge(hn_done, base + i + 1)
                        after(i)

            def attend(name, n, hd, scale, after):
                pbuf, _ = att_buf[name]

                def scores(i):
                    j = at_no[(name, i)]
                    key = ("S", name, i)
                    full(dve, key)
                    v = pbuf[:, i % 2, :].rearrange("p (q k) -> p q k", q=2)
                    sv = bank(key)[:, :].rearrange("p (q k) -> p q k", q=2)
                    if i >= 2:
                        full(dve, ("PT", name, i - 2))
                    if hd == 128:
                        drain(V.tensor_scalar(v, sv, scale, None, ALU.mult), key)
                    else:
                        bv = hank[:, i, 255:256]
                        bv = bass.AP(tensor=bv.tensor, offset=bv.offset, ap=[list(bv.ap[0]), [128, 2], [-1, L]])
                        drain(stt(v, sv, scale, bv, ALU.mult, ALU.add), key)
                    drained(dve, key)
                    step(V.tensor_reduce(smx[:, j % 2, 2, 0:2], v, AX, ALU.max))
                    V.tensor_scalar(smx[:, j % 2, 0, 0:2], smx[:, j % 2, 2, 0:2], -1.0, None,
                                    ALU.mult).then_inc(smax_ready, 1)

                def normalise(i):
                    j = at_no[(name, i)]
                    dve.wait_ge(p_exp, j + 1)
                    step(V.reciprocal(smx[:, j % 2, 3, 0:2], smx[:, j % 2, 1, 0:2]))
                    for qt in range(2):
                        v = pbuf[:, i % 2, qt * L:(qt + 1) * L]
                        ins = V.tensor_scalar(v, v, smx[:, j % 2, 3, qt:qt + 1], None, ALU.mult)
                    ins.then_inc(p_ready, 1)

                for i in range(n + 1):
                    if i < n:
                        scores(i)
                    if i >= 1:
                        normalise(i - 1)
                    after(i)

            dve.wait_ge(vec_in, 16)
            V.memset(epst[:, :], EPS).then_inc(eps_ready, 1)
            step(V.memset(onec[:, :], 1.0))
            step(V.tensor_copy(relb[0:32, :], cols("relb", H, 0, 0, 32)))
            V.memset(relb[32:33, :], BIG).then_inc(relb_ready, 1)
            lb = lambda i: cols("lb", 4, 4 * i)
            step(tt(lbt[:, 5, :], lb(0), lb(1), ALU.max))
            step(tt(lbt[:, 6, :], lbt[:, 5, :], lb(2), ALU.max))
            for i in range(3):
                ins = tt(lbt[:, i, :], lb(i), lbt[:, 6, :], ALU.subtract)
            ins.then_inc(lb_step, 1)
            dve.wait_ge(lb_step, 2)
            step(tt(lbt[:, 5, :], lbt[:, 0, :], lbt[:, 1, :], ALU.add))
            step(tt(lbt[:, 6, :], lbt[:, 5, :], lbt[:, 2, :], ALU.add))
            step(V.reciprocal(lbt[:, 7, :], lbt[:, 6, :]))
            step(tt(lbt[:, 3, :], lbt[:, 0, :], lbt[:, 7, :], ALU.mult))
            step(V.tensor_scalar(lbt[:, 4, :], lbt[:, 3, :], -1.0, 1.0, ALU.mult, ALU.add))
            dt0, lrd, th, k0, r_s, r_c = [par[:, i, :] for i in range(6)]
            lr, li = cols("s5_re", NT), cols("s5_im", NT)
            dve.wait_ge(s5_par, 1)
            step(tt(lrd, lr, dt0, ALU.mult))
            step(tt(th, li, dt0, ALU.mult))
            hi_, mid_ = 6.28125, 0.0019350051879882812
            lo_ = TWO_PI - hi_ - mid_
            for add, r in ((0.0, r_s), (0.25, r_c)):
                step(V.tensor_scalar(k0, th, 1.0 / TWO_PI, add, ALU.mult, ALU.add))
                step(V.tensor_scalar(k0, k0, MAGIC, None, ALU.add))
                step(V.tensor_scalar(k0, k0, -MAGIC, None, ALU.add))
                step(stt(r, k0, -hi_, th, ALU.mult, ALU.add))
                step(stt(r, k0, -mid_, r, ALU.mult, ALU.add))
                step(stt(r, k0, -lo_, r, ALU.mult, ALU.add))
                step(V.tensor_scalar(r, r, add * TWO_PI, 3.1415925, ALU.add, ALU.min))
                ins = V.tensor_scalar(r, r, -3.1415925, None, ALU.max)
                if add == 0.0:
                    step(ins)
            ins.then_inc(s5_par, 1)
            norm(0)
            dve.wait_ge(s5_par, 3)
            mag, sn, cs_ = par[:, 1, :], par[:, 4, :], par[:, 5, :]
            ar, ai, den, nr, cr, ci, q1, q2, nci = [par[:, i, :] for i in range(6, 15)]
            step(tt(ar, mag, cs_, ALU.mult))
            step(tt(ai, mag, sn, ALU.mult))
            step(tt(q1, lr, lr, ALU.mult))
            step(tt(q2, li, li, ALU.mult))
            step(tt(q1, q1, q2, ALU.add))
            step(V.reciprocal(den, q1))
            step(V.tensor_scalar(nr, ar, -1.0, None, ALU.add))
            for out, a, b, c, d, op in ((cr, nr, lr, ai, li, ALU.add), (ci, ai, lr, nr, li, ALU.subtract)):
                step(tt(q1, a, b, ALU.mult))
                step(tt(q2, c, d, ALU.mult))
                step(tt(q1, q1, q2, op))
                step(tt(out, q1, den, ALU.mult))
            full(dve, ("ab",))
            dve.wait_ge(gate_rows, 2)
            step(V.tensor_scalar(gs[0:8, 1, :], bank(("ab",))[32:40, 0:T], col("small", 0, 32, 40), None, ALU.add))
            step(V.tensor_scalar(gs[0:8, 2, :], gs[0:8, 1, :], -1.0, None, ALU.mult))
            step(tt(gs[0:8, 4, :], gs[0:8, 1, :], gs[0:8, 2, :], ALU.min))
            drain(V.tensor_scalar(gs[0:8, 0, :], gs[0:8, 0, :], 1.0, None, ALU.add), ("ab",))
            drained(dve, ("ab",))
            V.reciprocal(gs[0:8, 0, :], gs[0:8, 0, :]).then_inc(gate_rows, 1)
            dve.wait_ge(gate_rows, 4)
            step(stt(gs[0:8, 1, :], gs[0:8, 1, :], 0.0, gs[0:8, 4, :], ALU.max, ALU.add))
            step(V.tensor_scalar(gs[0:8, 1, :], gs[0:8, 1, :], aexp[0:8, 0:1], -1.0, ALU.mult, ALU.mult))
            for t in range(NCH):
                ts = slice(t * 128, (t + 1) * 128)
                step(V.tensor_tensor_scan(gs[0:8, 4, ts], cst("ones", p=8), gs[0:8, 1, ts], 0.0, ALU.mult, ALU.add))
                step(V.tensor_scalar(gs[0:8, 3, ts], gs[0:8, 4, ts], -1.0,
                                     gs[0:8, 4, (t + 1) * 128 - 1:(t + 1) * 128], ALU.mult, ALU.add))
            V.tensor_copy(gs[0:8, 4, L:T], gs[0:8, 1, L:T]).then_inc(gate_rows, 1)
            dve.wait_ge(pads_ready, 2)
            dve.wait_ge(hist_in, 16)
            cw = lambda k, m: col("conv_w", 12 * k + m)
            for m in range(12):
                drained(dve, ("lin", "ev_in_a", m))
                o, os_ = qkv[:, m, 0:L], qkv[:, m, L:T]
                V.tensor_scalar(o, zqkv[:, m, 0:L], cw(0, m), None, ALU.mult)
                step(V.tensor_scalar(os_, ch[:, m, 0:8], cw(0, m), None, ALU.mult))
                for k in range(1, 4):
                    stt(o, zqkv[:, m, k:k + L], cw(k, m), o, ALU.mult, ALU.add)
                    v = ch[:, m, 8 * k:8 * k + 8] if k < 3 else zqkv[:, m, 3 + L:3 + T]
                    ins = stt(os_, v, cw(k, m), os_, ALU.mult, ALU.add)
                    if k < 3:
                        step(ins)
                ins.then_inc(conv_done, 1)
            headnorm("l2", 8, T, lambda i: qkv[:, i, :], lambda i: HD ** -0.5 if i < 4 else 1.0,
                     lambda i: qkv[:, i, :])
            dve.wait_ge(silu_done, 12)
            dve.wait_ge(hn_done, 8)
            for c in range(HC):
                full(dve, ("bcL", c))
                B, G, E_ = bank(("bcB", c))[:, 0:T], bank(("bcG", c))[:, 0:T], bank(("bcL", c))[:, 0:L]
                tt(vb[:, c, :], qkv[:, 8 + c, :], B, ALU.mult)
                drain(tt(kb[:, c, :], qkv[:, 4 + c, :], B, ALU.mult), ("bcB", c))
                drained(dve, ("bcB", c))
                tt(bk[:, c, :], kb[:, c, :], G, ALU.mult)
                tt(qe[:, c, :], qkv[:, c, :], G, ALU.mult)
                drain(V.tensor_copy(egc[:, c, :], G[:, L - 1:T]), ("bcG", c))
                drain(tt(ke[:, c, :], qkv[:, 4 + c, 0:L], E_, ALU.mult), ("bcL", c))
            dve.wait_ge(cvo_ready, 1)
            for gi, g in enumerate(G4):
                d = dt_[:, gi % 2, :]
                drained(dve, ("DT", g))
                full(dve, ("QK", g))
                drain(tt(qkd[:, gi, :], bank(("QK", g))[:, :], d, ALU.mult), ("QK", g))
                full(dve, ("KK", g))
                drain(tt(mt[:, gi, :], bank(("KK", g))[:, :], d, ALU.mult), ("KK", g))
                drained(dve, ("KK", g))
                m4 = mt[:, gi, :].rearrange("p (n k) -> p n k", n=4)
                x4 = xt[:, gi, :].rearrange("p (n k) -> p n k", n=4)
                step(stt(x4, m4, -1.0, four(cst("lev", i=0)), ALU.mult, ALU.mult))
                tt(x4, x4, four(ident), ALU.add).then_inc(xt_ready, 1)
            for l in range(1, LEV):
                for gi, g in enumerate(G4):
                    key = ("ZT", l, g)
                    last = l == LEV - 1
                    full(dve, key if last else ("Z", l, g))
                    drain(tt(xt[:, gi, :], xt[:, gi, :], bank(key)[:, :], ALU.subtract), key)
                    if not last:
                        key = ("Z", l, g)
                        drain(tt(xx[:, gi, :], xx[:, gi, :], bank(key)[:, :], ALU.subtract), key)
            full(dve, ("S", "gdn", 0))
            drain(V.tensor_copy(sg[:, :, :], bank(("S", "gdn", 0))[:, 0:256].rearrange("p (c v) -> p c v", c=HC)),
                  ("S", "gdn", 0))
            for p in range(2):
                full(dve, ("ks", p))
                ap = lambda v: v.rearrange("p (c b v) -> p c b v", c=HC, b=2)[:, :, p, :]
                drain(tt(ap(rhst), ap(vbtok[:, 1, :]), bank(("ks", p))[:, 0:256].rearrange("p (c v) -> p c v", c=HC),
                         ALU.subtract), ("ks", p))
            full(dve, ("S", "gdn", 1))
            for c in range(HC):
                ins = stt(sg[:, c, :], sg[:, c, :], egc[:, c, 0:1], bank(("S", "gdn", 1))[:, c * 64:(c + 1) * 64],
                          ALU.mult, ALU.add)
            drain(ins, ("S", "gdn", 1))

            bc4 = lambda v: v.unsqueeze(3).broadcast_to([128, HC, NS, HD])
            bc3 = lambda v: v.unsqueeze(2).broadcast_to([128, NS, HD])

            def state_update(name, w1, st, k, n):
                for c in range(HC):
                    key = ("su", name, c)
                    full(dve, key)
                    drain(tt(w1[:, c], bank(key)[:, :].rearrange("p (s v) -> p s v", s=NS), bc3(k[:, c, L:T]),
                             ALU.mult), key)
                dve.wait_ge(sdec_ready, n)
                for c in range(HC):
                    drained(dve, ("su", name, c))
                    tt(st[:, c], st[:, c], w1[:, c], ALU.add).then_inc(sst_ready, 1)

            dve.wait_ge(sgs_in, 16)
            tt(ws1, sgs, bc4(bk[:, :, L:T]), ALU.mult).then_inc(w_ready, 1)
            dve.wait_ge(w_ready, 1)
            step(tt(ws2, cst("i2", 64).unsqueeze(1).unsqueeze(1).broadcast_to([128, HC, NS, HD]),
                    bc4(vb[:, :, L:T]), ALU.mult))
            tt(ws2, ws2, ws1, ALU.subtract).then_inc(w_ready, 1)
            state_update("gdn", ws1, sgs, qkv[:, 4:8, :], 1)

            def gated(gate, at):
                def after(i):
                    tt(mix[:, at + i, :], tmp[:, i % 2, :], gate[:, i, :], ALU.mult).then_inc(mix_ready, 1)
                return after

            for m in range(12, 16):
                drained(dve, ("lin", "ev_in_a", m))
            headnorm("gdn", HC, T, lambda i: oT[:, i, :], lambda i: col("gdn_norm"), lambda i: tmp[:, i % 2, :],
                     gated(zg, 0))
            for c in range(HC):
                drained(dve, ("lin", "ev_in_b", 4 + c))
                V.tensor_scalar(zk[:, c, :], zk[:, c, :], lbt[:, 4, c:c + 1], None, ALU.mult)
                V.tensor_scalar(zf[:, c, :], zf[:, c, :], lbt[:, 4, c:c + 1], lbt[:, 3, c:c + 1],
                                ALU.mult, ALU.add).then_inc(fk_ready, 1)
            dve.wait_ge(lf_ready, 1)
            for c in range(HC):
                ins = V.tensor_tensor_scan(bcs[:, c, :], rmask[:, :], lf[:, c, :], 0.0, ALU.mult, ALU.add)
            step(ins)
            ch4 = lambda v: v.rearrange("p c (k i) -> p (c k) i", i=HCK)
            mid, end_ = (HCK - 1) // 2, HCK - 1
            b4 = ch4(bcs)
            tt(ch4(d1), b4, b4[:, :, mid:mid + 1].broadcast_to([128, 32, HCK]), ALU.subtract).then_inc(dec_ready, 1)
            tt(ch4(d2), b4[:, :, end_:end_ + 1].broadcast_to([128, 32, HCK]), b4, ALU.subtract).then_inc(dec_ready, 1)
            dve.wait_ge(exp_ready, 2)
            for m in range(HC):
                drained(dve, ("lin", "ev_in_b", m))
            tt(qx, qx, zq[:, :, 0:L], ALU.mult).then_inc(hg_dve, 1)
            dve.wait_ge(fk_ready, HC)
            tt(kx, kx, zk[:, :, 0:L], ALU.mult).then_inc(hg_dve, 1)
            dve.wait_ge(att_zero, 1)
            for gi, g in enumerate(G4):
                full(dve, ("att", g))
                drain(V.copy_predicated(attb[:, gi, :].rearrange("p (n k) -> p n k", n=4),
                                        four(cst("cmask").bitcast(I32)),
                                        blocks(("att", g))), ("att", g))
            dve.wait_ge(hg_pool, 1)
            for k in range(8):
                key = ("kv", k)
                full(dve, key)
                kv = bank(key)[:, 0:256].rearrange("p (c v) -> p c v", c=HC)
                nxt = SH[(k + 1) % 8]
                if k:
                    drained(dve, ("kv", k - 1))
                    step(tt(nxt, SH[k], fl[:, :, k:k + 1].broadcast_to([128, HC, HD]), ALU.mult))
                    drain(tt(nxt, nxt, kv, ALU.add), key)
                else:
                    drain(V.tensor_copy(nxt, kv), key)
            state_update("hgrn", hws1, shs, zk, 2)
            headnorm("hgrn", HC, T, lambda i: oT[:, i, :], lambda i: col("hgrn_norm"), lambda i: tmp[:, i % 2, :],
                     gated(zh, 4))
            residual("ev_out")

            def memory(l):
                norm(norms.index(("memkv", l)))
                headnorm(f"memk{l}", MH, NM, lambda i: mk[:, i, :], lambda i: col("mem_gk", l),
                         lambda i: mk[:, i, :])
                norm(norms.index(("mem", l)))
                headnorm(f"memq{l}", MH, T, lambda i: mq[:, i, :], lambda i: col("mem_gq", l),
                         lambda i: mq[:, i, :])
                step(V.memset(mqz, 0.0))
                for hh_ in range(MH):
                    ins = V.tensor_copy(mqz[:, hh_, :, hh_], mq[:, hh_, L:T])
                ins.then_inc(qz_ready, 1)
                V.memset(mos, 0.0).then_inc(qz_ready, 1)
                name = f"mem{l}"

                def maxima(i):
                    if i in (2, 4):
                        g = i // 2 - 1
                        key = ("sc", name, g)
                        full(dve, key)
                        step(V.tensor_reduce(msm[:, g, 0:1], bank(key)[:, 0:NM], AX, ALU.max))
                        V.tensor_scalar(msm[:, g, 1:2], msm[:, g, 0:1], -128 ** -0.5, None,
                                        ALU.mult).then_inc(mx_ready, 1)
                attend(name, MH, 128, 128 ** -0.5, maxima)
                for g in range(2):
                    drained(dve, ("sc", name, g))
                step(V.reciprocal(msm[:, :, 3], msm[:, :, 2]))
                for g in range(2):
                    ins = V.tensor_scalar(msel[:, g, :], cst("sel", 4 * MH), msm[:, g, 3:4], None, ALU.mult)
                ins.then_inc(sel_ready, 1)
                full(dve, ("sx", name))
                drain(V.tensor_copy(mix[:, 0:4, L:T], bank(("sx", name))[:, 0:32].rearrange("p (h s) -> p h s", h=MH)),
                      ("sx", name))
                residual(f"wo{l}")

            def ffn(l):
                norm(norms.index(("ffn", l)))
                dve.wait_ge(fh_in, 16 * (l + 1))
                fw = lambda k, i: col("ffn_w", (l * 3 + k) * FT + i)
                for i in range(FT + 1):
                    if i < FT:
                        g, c = gb[:, i % 3, :], cacc[:, i % 2, :]
                        drained(dve, ("lin", f"gu{l}", 2 * i))
                        if i >= 2:
                            dve.wait_ge(fsilu_done, l * FT + i - 1)
                        fb = col("ffn_b", l * FT + i)
                        V.tensor_scalar(c[:, 0:L], g[:, 0:L], fw(0, i), fb, ALU.mult, ALU.add)
                        step(V.tensor_scalar(c[:, L:T], fh[:, i, 0:8], fw(0, i), fb, ALU.mult, ALU.add))
                        stt(c[:, 0:L], g[:, 1:1 + L], fw(1, i), c[:, 0:L], ALU.mult, ALU.add)
                        step(stt(c[:, L:T], fh[:, i, 8:16], fw(1, i), c[:, L:T], ALU.mult, ALU.add))
                        stt(c[:, 0:L], g[:, 2:2 + L], fw(2, i), c[:, 0:L], ALU.mult, ALU.add)
                        stt(c[:, L:T], g[:, 2 + L:2 + T], fw(2, i), c[:, L:T], ALU.mult,
                            ALU.add).then_inc(fconv_done, 1)
                    if i >= 1:
                        j = i - 1
                        key = ("lin", f"gu{l}", 2 * j + 1)
                        full(dve, key)
                        dve.wait_ge(fsilu_done, l * FT + j + 1)
                        drain(tt(act_[:, j, :], csil[:, j % 2, :], bank(key)[:, 0:T], ALU.mult), key)
                residual(f"down{l}")

            memory(0)
            ffn(0)
            norm(norms.index(("mix", 1)))
            step(V.memset(relr, 0.0))
            V.tensor_copy(relr.rearrange("p (j h) -> p j h", j=4)[:, :, 0:H],
                          relb[0:32, :].unsqueeze(1).broadcast_to([32, 4, H])).then_inc(relb_ready, 1)
            ms = lambda v, c_: V.memset(v, c_)
            dve.wait_ge(ffn_stored, 16)
            ms(cosT[:, :, 0:1], 1.0)
            step(ms(sinT[:, :, 0:1], 0.0))
            c0, s0_, c1, s1_ = [t16[:, i, :] for i in range(4)]
            step(V.tensor_copy(c0, cs_))
            step(V.tensor_copy(s0_, sn))
            wt = lambda i, n: place(TABTMP + i * 2048, NT, n)[0]
            n = 1
            while n < L:
                bb = lambda v: v.unsqueeze(2).broadcast_to([128, NT, n])
                wa, wb, wc, wd = [wt(i, n) for i in range(4)]
                C_, S_ = cosT[:, :, 0:n], sinT[:, :, 0:n]
                tt(wa, C_, bb(c0), ALU.mult)
                tt(wb, S_, bb(s0_), ALU.mult)
                tt(wc, C_, bb(s0_), ALU.mult)
                step(tt(wd, S_, bb(c0), ALU.mult))
                tt(cosT[:, :, n:2 * n], wa, wb, ALU.subtract)
                step(tt(sinT[:, :, n:2 * n], wc, wd, ALU.add))
                n *= 2
                if n < L:
                    step(tt(c1, c0, c0, ALU.mult))
                    step(tt(q1, s0_, s0_, ALU.mult))
                    step(tt(s1_, c0, s0_, ALU.mult))
                    step(tt(c0, c1, q1, ALU.subtract))
                    step(V.tensor_scalar(s0_, s1_, 2.0, None, ALU.mult))
            headnorm("moba", 8, T, lambda i: zo[:, i, :],
                     lambda i: col("moba_gq") if i < 4 else col("moba_gk"), lambda i: zo[:, i, :])
            dve.wait_ge(s5_in, 48)
            full(dve, ("lin", "od_in", 15))
            cb = lambda v: v.unsqueeze(2).broadcast_to([128, NT, 32])
            w1_, w2_ = place(WTMP, NT, 32)[0], place(WTMP + 512, NT, 32)[0]
            step(tt(w1_, s5c[:, 0], cb(cr), ALU.mult))
            step(tt(w2_, s5c[:, 1], cb(ci), ALU.mult))
            step(tt(s5cp[:, 0], w1_, w2_, ALU.subtract))
            step(tt(w1_, s5c[:, 0], cb(ci), ALU.mult))
            step(tt(w2_, s5c[:, 1], cb(cr), ALU.mult))
            step(stt(s5cp[:, 1].rearrange("p a b -> p (a b)"), w1_.rearrange("p a b -> p (a b)"), -1.0,
                     w2_.rearrange("p a b -> p (a b)"), ALU.mult, ALU.subtract))
            step(V.tensor_scalar(s5cp[:, 2].rearrange("p a b -> p (a b)"), s5c[:, 1].rearrange("p a b -> p (a b)"),
                                 -1.0, None, ALU.mult))
            step(ms(qz, 0.0))
            dve.wait_ge(hn_done, hn_no[("moba", 7)] + 1)
            for c in range(HC):
                for p in range(2):
                    ps = slice(64 * p, 64 * p + 64)
                    ins = V.tensor_copy(qz[ps, c, :, 2 * c + p], zo[ps, c, L:T])
            ins.then_inc(qz_ready, 1)
            dve.wait_ge(qz_ready, QZN["moba"] + 1)
            for c in range(HC):
                ins = tt(kz[:, c], qz[:, c], zo[:, 4 + c, L:T].unsqueeze(2).broadcast_to([128, NS, 32]), ALU.mult)
            ins.then_inc(qk_ready, 1)
            vs = tmpf[:, 400:432].rearrange("p (c s) -> p c s", c=HC)
            V.tensor_copy(vs, zo[:, 8:12, L:T])
            full(dve, ("self",))
            drain(V.tensor_scalar(gs2[:, 2, :], bank(("self",))[:, 0:2], HD ** -0.5, col("relb0"), ALU.mult, ALU.add),
                  ("self",))
            for i in range(2):
                drained(dve, ("bs", i))
            dve.wait_ge(bias_in, 16)

            def score_rows(i):
                if i < 2 or i % 2:
                    return
                k = i // 2 - 1
                g, half = k // 2, k % 2
                key = ("sc", "moba", k)
                full(dve, key)
                dst = ssc[:, g, 512 * half:512 * half + 512]
                V.tensor_reduce(gsm[:, 0, 4 * g + 2 * half:4 * g + 2 * half + 2],
                                bank(key)[:, :].rearrange("p (b t) -> p b t", b=2), AX, ALU.add)
                drain(stt(dst, bank(key)[:, :], HD ** -0.5, bsp[:, half, :], ALU.mult, ALU.add), key)
                drained(dve, key)
                step(V.tensor_reduce(gsm[:, 1, 4 * g + 2 * half:4 * g + 2 * half + 2],
                                     dst.rearrange("p (b t) -> p b t", b=2), AX, ALU.max))
            attend("moba", H, 64, HD ** -0.5, score_rows)
            gv = gsm[:, 0, :].rearrange("p (g b) -> p g b", g=2)
            cnt = gsm[:, 2, :].rearrange("p (g b) -> p g b", g=2)
            cmp_ = gs2[:, 0, :]
            for b in range(4):
                first = True
                for b2 in range(4):
                    if b2 == b:
                        continue
                    op = ALU.is_ge if b2 < b else ALU.is_gt
                    if first:
                        step(tt(cnt[:, :, b], gv[:, :, b2], gv[:, :, b], op))
                    else:
                        step(tt(cmp_, gv[:, :, b2], gv[:, :, b], op))
                        step(tt(cnt[:, :, b], cnt[:, :, b], cmp_, ALU.add))
                    first = False
            step(V.tensor_scalar(gsm[:, 3, :], gsm[:, 2, :], 3.0, BIG, ALU.is_ge, ALU.mult))
            step(tt(gsm[:, 4, :], gsm[:, 1, :], gsm[:, 3, :], ALU.add))
            step(V.tensor_reduce(gs2[:, 1, :], gsm[:, 4, :].rearrange("p (g b) -> p g b", g=2), AX, ALU.max))
            step(tt(gs2[:, 5, :], gs2[:, 1, :], gs2[:, 2, :], ALU.max))
            step(V.tensor_scalar(gs2[:, 3, :], gs2[:, 5, :], -1.0, None, ALU.mult))
            for g in range(2):
                ins = V.tensor_scalar(gsm[:, 5, 4 * g:4 * g + 4], gsm[:, 3, 4 * g:4 * g + 4], gs2[:, 3, g:g + 1], None,
                                      ALU.add)
            ins.then_inc(mx_ready, 1)
            V.memset(osm, 0.0).then_inc(qz_ready, 1)
            dve.wait_ge(pp_ready, 5)
            step(V.tensor_reduce(gs2[:, 6, :], gsm[:, 6, :].rearrange("p (g b) -> p g b", g=2), AX, ALU.add))
            step(tt(gs2[:, 7, :], gs2[:, 6, :], gs2[:, 4, :], ALU.add))
            step(V.reciprocal(gs2[:, 8, :], gs2[:, 7, :]))
            for g in range(2):
                ins = V.tensor_scalar(sel2[:, 0, g, :], cst("sel", 4 * H), gs2[:, 8, g:g + 1], None, ALU.mult)
                ins = V.tensor_scalar(sel2[:, 1, g, :], cst("sel", 4 * H), gs2[:, 8, g:g + 1], gs2[:, 4, g:g + 1],
                                      ALU.mult, ALU.mult)
            ins.then_inc(sel_ready, 1)
            for j in range(4):
                full(dve, ("s5s", j))
                src = bank(("s5s", j))[:, 0:64].rearrange("p (c q s) -> p q c s", c=HC, q=2)
                for q in range(2):
                    ins = V.tensor_copy(hsS[:, q].rearrange("p (c j) s -> p c j s", j=4)[:, :, j, :], src[:, q])
                drain(ins, ("s5s", j))
            for j in range(4):
                drained(dve, ("s5s", j))
            sb8 = lambda v: v.unsqueeze(2).broadcast_to([128, NT, NS])
            for q, (a, b, c, d, op) in enumerate(((ar, ai, cr, ci, ALU.subtract), (ai, ar, ci, cr, ALU.add))):
                out = s5o[:, q, :, 1:9]
                step(tt(w3, s5h[:, 0], sb8(a), ALU.mult))
                step(tt(w4, s5h[:, 1], sb8(b), ALU.mult))
                step(tt(w3, w3, w4, op))
                step(tt(w4, hsS[:, 0], sb8(c), ALU.mult))
                step(tt(w3, w3, w4, ALU.add))
                step(tt(w4, hsS[:, 1], sb8(d), ALU.mult))
                step(tt(out, w3, w4, op))
            for q in range(2):
                V.tensor_copy(hsS[:, q], s5o[:, q, :, 1:9]).then_inc(s5_hs, 1)
            def y_out(c):
                key = ("s5y", c)
                full(dve, key)
                drain(stt(tmpy[:, c, :], zo[:, 12 + c, :], col("s5_d", c), bank(key)[:, 0:T], ALU.mult, ALU.add), key)

            for n in range(NT):
                key = ("s5x", n)
                b = n % 2
                full(dve, key)
                xv = bank(key)[:, :].rearrange("p (q t) -> p q t", q=2)
                tab = lambda v: v[:, n, :].unsqueeze(1).broadcast_to([128, 2, L])
                tt(ta[:, b], xv, tab(cosT), ALU.mult)
                drain(tt(tb[:, b], xv, tab(sinT), ALU.mult), key)
                drained(dve, key)
                tt(ta[:, b, 0, :], ta[:, b, 0, :], tb[:, b, 1, :], ALU.add)
                step(tt(ta[:, b, 1, :], ta[:, b, 1, :], tb[:, b, 0, :], ALU.subtract))
                if n >= 2:
                    dve.wait_ge(s5_hi, 2 * (n - 1))
                for q in range(2):
                    V.tensor_tensor_scan(gg[:, b, q, :], par[:, 1, n:n + 1].broadcast_to([128, L]), ta[:, b, q, :],
                                         0.0, ALU.mult, ALU.add).then_inc(s5_g, 1)
                dve.wait_ge(s5_g, 2 * (n + 1))
                tt(ta[:, b, 0, :], gg[:, b, 0, :], cosT[:, n, :], ALU.mult)
                step(tt(ta[:, b, 1, :], gg[:, b, 1, :], sinT[:, n, :], ALU.mult))
                if n == 4:
                    full(dve, ("pt", "moba", 3))
                if n >= NHB:
                    full(dve, ("s5y", (n - NHB) // 4))
                tt(HH[n % NHB][:, 0, :], ta[:, b, 0, :], ta[:, b, 1, :], ALU.subtract).then_inc(s5_hr, 1)
                dve.wait_ge(s5_hr, n + 1)
                ins = V.tensor_copy(hl[:, 0, n:n + 1], HH[n % NHB][:, 0, L - 1:L])
                if n == NT - 1:
                    step(ins)
                if n >= 6 and n % 4 == 2:
                    y_out((n - 6) // 4)
            y_out(3)
            full(dve, ("sx", "moba"))
            w = tmpf[:, 360:392].rearrange("p (c s) -> p c s", c=HC)
            b = bank(("sx", "moba"))
            ob, pb = [b[:, 32 * i:32 * i + 32].rearrange("p (c s) -> p c s", c=HC) for i in range(2)]
            step(tt(w, vs, pb, ALU.mult))
            drain(tt(mix[:, 0:4, L:T], w, ob, ALU.add), ("sx", "moba"))
            drained(dve, ("sx", "moba"))
            dve.wait_ge(s5_hi, 2 * NT)
            for q, (a, b, op) in enumerate(((cr, ci, ALU.subtract), (ci, cr, ALU.add))):
                step(tt(t16[:, 0, :], hl[:, 0, :], a, ALU.mult))
                step(tt(t16[:, 1, :], hl[:, 1, :], b, ALU.mult))
                ins = tt(s5o[:, q, :, 0], t16[:, 0, :], t16[:, 1, :], op)
                if q == 0:
                    step(ins)
            ins.then_inc(s5_hs, 1)
            for c in range(HC):
                key = ("lin", "glu", 2 * c)
                full(dve, key)
                drained(dve, ("lin", "glu", 2 * c + 1))
                drain(tt(mix[:, 4 + c, :], bank(key)[:, 0:T], tmp[:, c % 2, :], ALU.mult), key)
            residual("od_out")
            memory(1)
            ffn(1)


_OUT = {"y": (128, KC, T), "o_gconv": (128, 12, 27), "o_gdn": (128, HC, HD), "o_sgs": (128, HC, NS, HD),
        "o_hgrn": (128, HC, HD), "o_shs": (128, HC, NS, HD), "o_k": (128, HC, T), "o_v": (128, HC, T),
        "o_s5": (128, 2, NT, 9), "o_memk": (2, 128, MH, NM), "o_memv": (2, 128, MH, NM), "o_ffn": (2, 128, FT, 18)}


def feats(a):
    n, f = a.shape
    return a.T.reshape(f // 128, 128, n).transpose(1, 0, 2)


def stream(w, per):
    k, m = w.shape
    a = w.reshape(k // 128, 128, m // 128, 128).transpose(2, 1, 0, 3)
    a = a.reshape(m // 128 // per, per, 128, k // 128, 128).transpose(0, 2, 1, 3, 4)
    return np.ascontiguousarray(a.reshape(m // 128 // per, 128, -1))


def layout(i):
    g = {k: np.asarray(v) for k, v in i.items()}
    a = {"con": constants()}
    a["x"] = feats(np.concatenate([g["x_prompt"][0], g["x_sample"][:, 0]], 0))
    a["memx"] = feats(g["mem_prompt"][0])
    vec = np.zeros((128, VECW), np.float32)

    def put(name, v, at=0):
        v = np.asarray(v)
        vec[:v.shape[0], VEC[name] + at:VEC[name] + at + v.shape[1]] = v

    for n in ("norm_mix", "norm_mem", "norm_memkv", "norm_ffn"):
        put(n, g[n].reshape(16, 128).T)
    put("mem_gq", g["mem_gq"].T)
    put("mem_gk", g["mem_gk"].T)
    put("ffn_w", g["ffn_conv_w"].reshape(6 * FT, 128).T)
    put("ffn_b", g["ffn_conv_b"].reshape(2 * FT, 128).T)
    put("conv_w", g["gdn_conv_w"][0].reshape(48, 128).T)
    for n in ("gdn_norm", "hgrn_norm", "moba_gq", "moba_gk"):
        put(n, np.concatenate([g[n][0], g[n][0]])[:, None])
    put("lb", g["hgrn_lb_raw"].reshape(12, 128).T)
    put("s5_re", g["s5_A_re"][0].reshape(NT, 128).T)
    put("s5_im", g["s5_A_im"][0].reshape(NT, 128).T)
    put("s5_dt", np.repeat(g["s5_log_dt"][0], 64).reshape(NT, 128).T)
    put("s5_d", g["s5_D"][0].reshape(4, 128).T)
    vec[32:40, VEC["small"]] = g["gdn_dt_bias"][0]
    vec[0:8, VEC["small"] + 1] = g["gdn_A_log"][0]
    put("relb", g["rel_bias"])
    for j in range(4):
        vec[32 * j:32 * j + H, VEC["relb0"]] = g["rel_bias"][0]
    w = g["ev_w_in"][0]
    z = 4 * 512
    for k in range(KC):
        vec[:, VEC["w_ab"] + 40 * k:VEC["w_ab"] + 40 * k + 8] = w[128 * k:128 * k + 128, z:z + 8]
        vec[:, VEC["w_ab"] + 40 * k + 32:VEC["w_ab"] + 40 * k + 40] = w[128 * k:128 * k + 128, z + 8:z + 16]
    a["vec"] = vec
    a["pages"] = g["page_table"].reshape(1, NS * PAGES)
    a["ev_in_a"] = stream(w[:, :z], 2)
    a["ev_in_b"] = stream(w[:, z + 16:], 2)
    a["ev_out"] = stream(g["ev_w_out"][0], 2)
    a["od_in"] = stream(g["od_w_in"][0], 2)
    a["od_out"] = stream(g["od_w_out"][0], 2)
    glu = g["s5_glu_w"][0].reshape(512, 2, 4, 128).transpose(0, 2, 1, 3).reshape(512, 1024)
    a["glu"] = stream(glu, 4)
    for l in range(2):
        a[f"memk{l}"] = stream(g["mem_wkv"][l][:, :512], 2)
        a[f"memv{l}"] = stream(g["mem_wkv"][l][:, 512:], 2)
        a[f"wq{l}"] = stream(g["mem_wq"][l], 2)
        a[f"wo{l}"] = stream(g["mem_wo"][l], 4)
        gu = g["ffn_w_gu"][l].reshape(D, 2, FT, 128).transpose(0, 2, 1, 3).reshape(D, 2 * DFF)
        a[f"gu{l}"] = stream(gu, 2)
        a[f"down{l}"] = stream(g["ffn_w_down"][l], 1)
        k = g["cache_mem_k"][l]
        a[f"ck{l}"] = k.reshape(4, 2, NM, MH, 128).transpose(0, 4, 1, 3, 2).reshape(4, 128, 2048)
        v = g["cache_mem_v"][l]
        a[f"cv{l}"] = v.reshape(4, 2, 2, 128, 512).transpose(0, 3, 1, 2, 4).reshape(4, 128, 2048)
    a["gconv"] = g["state_gdn_conv"][0].reshape(NS, 3, 12, 128).transpose(3, 2, 1, 0).reshape(128, 12, 24)
    for n, k in (("sgs", "state_gdn"), ("shs", "state_hgrn")):
        a[n] = g[k][0].reshape(NS, HC, 2, 64, 64).transpose(2, 3, 1, 0, 4).reshape(128, HC, NS, HD)
    a["fh"] = g["state_ffn_conv"].reshape(2, NS, 2, FT, 128).transpose(0, 4, 3, 2, 1).reshape(2, 128, FT, 16)
    a["s5h"] = np.stack([g[k][0].reshape(NS, NT, 128).transpose(2, 1, 0) for k in ("state_s5_re", "state_s5_im")], 1)
    b = np.zeros((4, 2, 16, 2, 4, 2, 64), np.float32)
    c = np.zeros((2, 64, 2, NT, 2, 16), np.float32)
    for q in range(2):
        bq = g[("s5_B_re", "s5_B_im")[q]][0].reshape(4, 4, 2, 64, 16)
        cq = g[("s5_C_re", "s5_C_im")[q]][0].reshape(NT, 2, 16, 64)
        for e in range(2):
            b[:, e, :, q, :, e, :] = bq[:, :, e].transpose(1, 3, 0, 2)
            c[e, :, q, :, e, :] = cq[:, e].transpose(2, 0, 1)
    a["s5b"] = b.reshape(128, 2, 4, 128)
    a["s5c"] = c.reshape(128, 2, NT, 32)
    a["pool_k"] = g["cache_moba_k"][0].reshape(POOL_PAGES, 128, HC, 128).transpose(0, 3, 2, 1).reshape(
        POOL_PAGES, 128, 512)
    a["pool_v"] = g["cache_moba_v"][0].reshape(POOL_PAGES, 128, 512)
    return {k: np.ascontiguousarray(v) for k, v in a.items()}


def kernel(**inputs):
    import concourse.bacc as bacc
    from concourse.bass_utils import run_bass_kernel_spmd

    nc = bacc.Bacc("TRN2", target_bir_lowering=False, num_devices=1)
    arrays, A = {}, {}
    for name, a in layout(inputs).items():
        arrays[f"in_{name}"] = a
        A[name] = nc.dram_tensor(f"in_{name}", a.shape, mybir.dt.from_np(a.dtype), kind="ExternalInput").ap()
    for name, shape in _OUT.items():
        A[name] = nc.dram_tensor(f"out_{name}", shape, F32, kind="ExternalOutput").ap()
    A["bias_x"] = nc.dram_tensor("bias_x", (8, 512), F32, kind="Internal").ap()
    build(nc, A)
    r = run_bass_kernel_spmd(nc, [arrays], core_ids=[0]).results[0]
    o = {name: np.asarray(r[f"out_{name}"]) for name in _OUT}

    def rows(a):
        return a.transpose(2, 1, 0).reshape(a.shape[2], -1)

    y = rows(o["y"])
    gc = o["o_gconv"]
    k, v = rows(o["o_k"]), rows(o["o_v"])
    pst = lambda a: a.reshape(2, 64, HC, 64).transpose(2, 0, 1, 3).reshape(1, 1, H, 64, 64)
    sst = lambda a: a.reshape(2, 64, HC, NS, 64).transpose(3, 2, 0, 1, 4).reshape(1, NS, H, 64, 64)
    s5 = o["o_s5"].transpose(1, 3, 2, 0).reshape(2, 9, 32, 64)
    memo = lambda a: np.stack([rows(a[l]) for l in range(2)]).reshape(2, 1, NM, MH, 128)
    ff = o["o_ffn"]
    ffp = ff[..., 0:2].transpose(0, 3, 2, 1).reshape(2, 1, 2, DFF)
    ffs = ff[..., 2:18].reshape(2, 128, FT, 2, NS).transpose(0, 4, 3, 2, 1).reshape(2, NS, 2, DFF)
    out = (y[None, :L], y[L:, None], rows(gc[:, :, 0:3]).reshape(1, 1, 3, 1536), pst(o["o_gdn"]), pst(o["o_hgrn"]),
           k[:L].reshape(1, 1, L, H, HD), v[:L].reshape(1, 1, L, H, HD), s5[0:1, 0:1], s5[1:2, 0:1],
           memo(o["o_memk"]), memo(o["o_memv"]), ffp,
           gc[:, :, 3:].reshape(128, 12, 3, NS).transpose(3, 2, 1, 0).reshape(1, NS, 3, 1536),
           sst(o["o_sgs"]), sst(o["o_shs"]), k[L:].reshape(1, NS, 1, H, HD), v[L:].reshape(1, NS, 1, H, HD),
           s5[0:1, 1:], s5[1:2, 1:], ffs)
    return tuple(np.ascontiguousarray(a) for a in out)
```

```python
import math
from contextlib import ExitStack

import numpy as np
import concourse.bass as bass
from concourse import mybir

F32 = mybir.dt.float32
I32 = mybir.dt.int32
R32 = mybir.dt.float32r
ALU = mybir.AluOpType
ACT = mybir.ActivationFunctionType
AX = mybir.AxisListType.X

D = 1024
KC = D // 128
L = 256
NS = 8
T = L + NS
H = 8
HC = 4
HD = 64
CHK = 128
NCH = L // CHK
HCK = 32
MH = 4
NM = 256
DFF = 2816
FT = DFF // 128
PAGES = 8
POOL_PAGES = 80
NT = 16
EPS = 1e-6
BIG = -1.0e30
LEV = 7
SLOTS = 4
SLOTW = FT * 128
NBANK = 8
TWO_PI = 2.0 * math.pi
MAGIC = 12582912.0

VEC = {}
_off = 0
for _name, _w in [("norm_mix", 16), ("norm_mem", 16), ("norm_memkv", 16), ("norm_ffn", 16), ("mem_gq", 2),
                  ("mem_gk", 2), ("ffn_w", 2 * 3 * FT), ("ffn_b", 2 * FT), ("conv_w", 48), ("gdn_norm", 1),
                  ("hgrn_norm", 1), ("moba_gq", 1), ("moba_gk", 1), ("lb", 12), ("s5_re", NT), ("s5_im", NT),
                  ("s5_dt", NT), ("s5_d", 4), ("small", 2), ("relb", H), ("relb0", 1), ("w_ab", KC * 40)]:
    VEC[_name] = _off
    _off += _w
VECW = _off
CON = {}
_off = 0
for _name, _w in [("ident", 128), ("ones", 128), ("bd", 128), ("neg", 128), ("i2", 64), ("lev", LEV * 128),
                  ("selh", H * 128), ("nselh", H * 128), ("selc", HC * 128), ("hotx", 512), ("hots", 1024),
                  ("cmask", 128), ("sel", 4 * H)]:
    CON[_name] = _off
    _off += _w
CONW = _off


def constants():
    c = np.zeros((128, CONW), np.float32)
    p = np.arange(128)

    def put(name, a):
        c[:a.shape[0], CON[name]:CON[name] + a.shape[1]] = a

    put("ident", np.eye(128))
    put("ones", np.ones((128, 128)))
    put("bd", (p[:, None] // 64 == p[None] // 64) * 1.0)
    put("neg", np.where(p[None] >= p[:, None], 0.0, BIG))
    put("i2", (p[:, None] % 64 == np.arange(64)[None]) * 1.0)
    for l in range(LEV):
        b = 1 << l
        m = (p[None] // (2 * b) == p[:, None] // (2 * b)) & (p[None] // b % 2 == 1) & (p[:, None] // b % 2 == 0)
        c[:, CON["lev"] + 128 * l:CON["lev"] + 128 * (l + 1)] = m
    for h in range(H):
        c[h, CON["selh"] + 128 * h:CON["selh"] + 128 * (h + 1)] = 1.0
        c[h, CON["nselh"] + 128 * h:CON["nselh"] + 128 * (h + 1)] = -1.0
        at = CON["selc"] + 64 * h
        c[h, at:at + 64] = 1.0

    def bucket(n):
        if n < 16:
            return n
        return min(16 + int(math.log(n / 16) / math.log(8.0) * 16 + 1e-9), 31)
    for j in range(512):
        dist = j - 255
        c[32 if dist < 0 else bucket(dist), CON["hotx"] + j] = 1.0
    for k in range(1024):
        c[bucket(1024 - k), CON["hots"] + k] = 1.0
    for q in range(H):
        for j in range(4):
            c[32 * j + q, CON["sel"] + 4 * q + j] = 1.0
    put("cmask", ((p[:, None] // HCK == p[None] // HCK) & (p[None] >= p[:, None])) * 1.0)
    return c


def make_plan():
    order, slots, slot_of = [], [], {}
    used = [0]

    def lin(name, tiles, per_slot, cols, first=0, after=None):
        for m in range(first, tiles):
            if m % per_slot == 0:
                slots.append(("w", name, m // per_slot, cols, None))
            slot_of[(name, m)] = len(slots) - 1
            order.append(("lin", name, m))
            slots[-1] = slots[-1][:4] + (("lin", name, m),)
            if after:
                after(m)

    def stream(name, i, cols, last):
        if last is None:
            used[0] += 1
            last = ("used", used[0])
        slots.append(("w" if name[0] == "c" else "page", name, i, cols, last))
        slot_of[(name, i)] = len(slots) - 1

    def memory(l):
        lin(f"memk{l}", MH, 2, 2048)
        order.append(("ss", "mem", l))
        lin(f"memv{l}", MH, 2, 2048, after=lambda m: order.append(("hn", f"memk{l}", m)))
        order.extend([("mvt", l, 0), ("mvt", l, 1)])
        lin(f"wq{l}", MH, 2, 2048, after=lambda m: m and order.append(("hn", f"memq{l}", m - 1)))
        order.append(("hn", f"memq{l}", MH - 1))
        name = f"mem{l}"

        def keys(i, part):
            if part == 0 and i < 4:
                stream(f"ck{l}", i, 2048, ("sc", name, i // 2) if i % 2 else None)
                if i % 2:
                    order.append(("sc", name, i // 2))
        attend(name, MH, keys)
        order.append(("pt", name, 0))
        for i in range(4):
            stream(f"cv{l}", i, 2048, ("so", name, i // 2) if i % 2 else None)
            if i % 2:
                order.append(("so", name, i // 2))
        order.append(("sx", name))
        lin(f"wo{l}", KC, 4, 2048)

    def attend(name, n, between):
        for i in range(n + 2):
            if i < n:
                order.append(("S", name, i))
            between(i, 0)
            if 0 <= i - 1 < n:
                order.append(("PT", name, i - 1))
            between(i, 1)
            if 0 <= i - 2 < n:
                order.append(("O", name, i - 2))

    def ffn(l):
        order.append(("ss", "ffn", l))
        lin(f"gu{l}", 2 * FT, 2, 2048)
        lin(f"down{l}", KC, 1, SLOTW)

    order.append(("ss", "mix", 0))
    order.append(("ab",))
    lin("ev_in_a", 8, 2, 2048)
    lin("ev_in_a", 16, 2, 2048, 8, lambda m: order.append(("hn", "l2", m - 8)))
    for c in range(HC):
        order.extend([("bcB", c), ("bcG", c), ("bcL", c)])
    for t in range(NCH):
        order.extend([("trk", t), ("trv", t)])
    G4 = [(t, par) for t in range(NCH) for par in range(2)]
    for g in G4:
        order.extend([("DT", g), ("QK", g), ("KK", g)])
    for g in G4:
        order.append(("X1", g))
    for l in range(1, LEV):
        for g in G4:
            order.append(("T1", l, g))
        for g in G4:
            order.append(("ZT", l, g))
            if l < LEV - 1:
                order.append(("Z", l, g))
    for t in range(NCH):
        if t:
            order.extend([("ks", 0), ("ks", 1)])
        order.extend([("u", t), ("o", t, 0), ("o", t, 1), ("S", "gdn", t)])
    lin("ev_in_b", 4, 2, 2048)
    for i in range(HC):
        order.append(("su", "gdn", i))
    lin("ev_in_b", 8, 2, 2048, 4)
    order.append(("sO", "gdn"))
    lin("ev_in_b", 12, 2, 2048, 8)
    lin("ev_in_b", 16, 2, 2048, 12, lambda m: order.append(("hn", "gdn", m - 12)))
    for t in range(NCH):
        order.extend([("htk", t), ("htv", t)])
    for g in G4:
        order.append(("att", g))
    for k in range(L // HCK):
        order.append(("kv", k))
    for g in G4:
        order.append(("ho", g))
    for i in range(HC):
        order.append(("su", "hgrn", i))
    order.append(("sO", "hgrn"))
    for c in range(HC):
        order.append(("hn", "hgrn", c))
    lin("ev_out", 4, 2, 2048)
    order.append(("ss", "memkv", 0))
    lin("ev_out", KC, 2, 2048, 4)
    memory(0)
    ffn(0)
    order.append(("ss", "mix", 1))
    lin("od_in", 8, 2, 2048)
    order.append(("bx",))
    lin("od_in", 16, 2, 2048, 8, lambda m: order.append(("hn", "moba", m - 8)))
    order.extend([("vt", 0), ("vt", 1), ("bs", 0), ("bs", 1)])

    def pages(i, part):
        if (i, part) == (2, 0):
            order.append(("self",))
        if i < H and part == 0:
            for n in (2 * i, 2 * i + 1):
                stream("pk", n, 2048, ("sc", "moba", n // 4) if n % 4 == 3 else None)
            if n % 4 == 3:
                order.append(("sc", "moba", n // 4))
    attend("moba", H, pages)
    order.extend([("s5x", 0), ("s5x", 1)])
    for i in range(4):
        order.append(("pt", "moba", i))
    for n in range(0, NT, 2):
        for m in (n, n + 1):
            stream("pv", m, 2048, ("so", "moba", m // 4) if m % 4 == 3 else None)
        if m % 4 == 3:
            order.append(("so", "moba", m // 4))
        if n + 2 < NT:
            order.extend([("s5x", n + 2), ("s5x", n + 3)])
        if n < 4:
            order.extend([("s5s", n), ("s5s", n + 1)])
        if n % 4 == 0 and n:
            order.append(("s5y", n // 4 - 1))
    order.extend([("s5y", 3), ("sx", "moba")])
    lin("glu", 8, 4, 2048)
    lin("od_out", 4, 2, 2048)
    order.append(("ss", "memkv", 1))
    lin("od_out", KC, 2, 2048, 4)
    memory(1)
    ffn(1)
    return order, slots, slot_of


def build(nc, A):
    order, slots, slot_of = make_plan()
    no = {k: i for i, k in enumerate(order)}
    assert len(no) == len(order)
    hn_no = {}
    at_no = {}
    for k in order:
        if k[0] == "hn":
            hn_no[k[1:]] = len(hn_no)
        if k[0] == "PT":
            at_no[k[1:]] = len(at_no)

    slot_value, seen = [], [0] * SLOTS
    for s, (kind, _, _, _, _) in enumerate(slots):
        seen[s % SLOTS] += 16 * (4 if kind == "page" else 1)
        slot_value.append(seen[s % SLOTS])

    with ExitStack() as ctx:
        def sb(name, shape, dt=F32):
            return ctx.enter_context(nc.sbuf_tensor(name, shape, dt))

        def split_sb(name, shape):
            with nc.sbuf_tensor(name, shape, F32) as plain:
                pass
            return plain, sb(name + "_r", shape, R32)

        def sem(name):
            return ctx.enter_context(nc.semaphore(name))

        banks = [ctx.enter_context(nc.psum_tensor(f"bank{i}", [128, 512], F32)) for i in range(NBANK)]

        def bank(key):
            return banks[no[key] % NBANK]

        def blocks(key, n=4, p0=0, p1=128):
            return bank(key)[p0:p1, 0:n * 128].rearrange("p (n k) -> p n k", n=n)

        con = sb("con", [128, CONW])
        vec = sb("vec", [128, VECW])
        pages = sb("pages_sb", [1, NS * PAGES], I32)
        ring, ring_r = split_sb("ring", [128, SLOTS, SLOTW])
        x = sb("x", [128, KC, T])
        h, h_r = split_sb("h", [128, KC, T])
        sq = sb("sq", [128, KC, T])
        mix, mix_r = split_sb("mix", [128, KC, T])
        oT = sb("oT", [128, HC, T])
        tmp = sb("tmp", [128, 2, T])
        lnb = sb("lnb", [128, 2, T])
        rs = sb("rs", [128, T])
        hsq = sb("hsq", [128, 2, T])
        hr = sb("hr", [128, 2, T])
        cvo = sb("cvo", [128, 12, 27])
        egc = sb("egc", [128, HC, 9])
        ch = sb("ch", [128, 12, 24])
        sg = sb("sg", [128, HC, HD])
        lbt = sb("lbt", [128, 8, HC])
        par = sb("s5par", [128, 24, NT])
        relb = sb("relb", [64, H])
        aexp = sb("aexp", [8, 1])
        epst = sb("epst", [128, 1])
        onec = sb("onec", [128, 1])
        WORK = 21700
        work, work_r = split_sb("work", [128, WORK])

        def place(at, *dims, of=None):
            n = int(np.prod(dims))
            assert at + n <= WORK, (at, n)
            v = (work if of is None else of)[:, at:at + n]
            if len(dims) == 2:
                v = v.rearrange("p (a b) -> p a b", a=dims[0])
            if len(dims) == 3:
                v = v.rearrange("p (a b c) -> p a b c", a=dims[0], b=dims[1])
            if len(dims) == 4:
                v = v.rearrange("p (a b c d) -> p a b c d", a=dims[0], b=dims[1], c=dims[2])
            return v, at + n

        def cst(name, w=128, i=0, p=128):
            return con[0:p, CON[name] + i * w:CON[name] + (i + 1) * w]

        def col(name, i=0, p0=0, p1=128):
            return vec[p0:p1, VEC[name] + i:VEC[name] + i + 1]

        def cols(name, n, i=0, p0=0, p1=128):
            return vec[p0:p1, VEC[name] + i:VEC[name] + i + n]

        ident, ones, bd = cst("ident"), cst("ones"), cst("bd")

        def four(ap):
            return ap.unsqueeze(1).broadcast_to([128, 4, 128])

        psum_full = sem("psum_full")
        psum_free = [sem(f"psum_free{i}") for i in range(NBANK)]
        ring_full = [sem(f"ring_full{i}") for i in range(SLOTS)]
        con2_in = sem("con2_in")
        (con_in, vec_in, x_in, pages_in, hist_in, memx_in, sgs_in, shs_in, fh_in, s5_in, bias_in) = [
            sem(n) for n in ("con_in", "vec_in", "x_in", "pages_in", "hist_in", "memx_in", "sgs_in", "shs_in",
                             "fh_in", "s5_in", "bias_in")]
        act_step, dve_step, pool_step = sem("act_step"), sem("dve_step"), sem("pool_step")
        msq_ready, pages_used = sem("msq_ready"), sem("pages_used")
        sq_ready, r_ready, h_ready = sem("sq_ready"), sem("r_ready"), sem("h_ready")
        hsq_ready, hr_ready, hn_done = sem("hsq_ready"), sem("hr_ready"), sem("hn_done")
        mix_ready, stored, sgs_out = sem("mix_ready"), sem("stored"), sem("sgs_out")
        pads_ready, lb_step, gate_rows, conv_done, silu_done = [
            sem(n) for n in ("pads_ready", "lb_step", "gate_rows", "conv_done", "silu_done")]
        cvo_ready, xt_ready, ml_ready = [sem(n) for n in ("cvo_ready", "xt_ready", "ml_ready")]
        w_ready, sdec_ready, sst_ready = sem("w_ready"), sem("sdec_ready"), sem("sst_ready")
        fk_ready, lf_ready, dec_ready, exp_ready, hg_dve, hg_pool, att_zero = [
            sem(n) for n in ("fk_ready", "lf_ready", "dec_ready", "exp_ready", "hg_dve", "hg_pool", "att_zero")]
        smax_ready, p_exp, p_ready = [sem(n) for n in ("smax_ready", "p_exp", "p_ready")]
        mx_ready, pp_ready, sel_ready, qz_ready = [sem(n) for n in ("mx_ready", "pp_ready", "sel_ready", "qz_ready")]
        fpads, fconv_done, fsilu_done, fcopy_done = [
            sem(n) for n in ("fpads", "fconv_done", "fsilu_done", "fcopy_done")]
        wh_ready, wl_ready, xh_ready, xl_ready, ah_ready, al_ready = [
            sem(n) for n in ("wh_ready", "wl_ready", "xh_ready", "xl_ready", "ah_ready", "al_ready")]
        bx_stored, qk_ready = sem("bx_stored"), sem("qk_ready")
        s5_par, s5_hr, s5_g, s5_hi, s5_hs = [sem(n) for n in ("s5_par", "s5_hr", "s5_g", "s5_hi", "s5_hs")]
        eps_ready, relb_ready, s5_gl2 = [sem(n) for n in ("eps_ready", "relb_ready", "s5_gl2")]
        hg_stored, mem_stored, ffn_stored, kv_stored = [
            sem(n) for n in ("hg_stored", "mem_stored", "ffn_stored", "kv_stored")]

        def full(eng, key):
            eng.wait_ge(psum_full, no[key] + 1)

        def drained(eng, key):
            eng.wait_ge(psum_free[no[key] % NBANK], no[key] // NBANK + 1)

        def drain(ins, key):
            return ins.then_inc(psum_free[no[key] % NBANK], 1)

        class Steps:
            def __init__(self, eng, s):
                self.eng, self.s, self.n = eng, s, 0

            def __call__(self, ins):
                self.n += 1
                ins.then_inc(self.s, 1)
                self.eng.wait_ge(self.s, self.n)

        norms = [k[1:] for k in order if k[0] == "ss"]
        xnorms = [n for n in norms if n[0] != "memkv"]
        NORM_G = {"mix": "norm_mix", "memkv": "norm_memkv", "mem": "norm_mem", "ffn": "norm_ffn"}
        G4 = [(t, p) for t in range(NCH) for p in range(2)]

        MXN = {"mem0": 0, "moba": 2, "mem1": 3}
        QZN = {"mem0": 0, "moba": 2, "mem1": 4}
        SELN = {"mem0": 1, "moba": 2, "mem1": 3}

        zqkv, e = place(0, 12, 3 + T)
        qkv, e = place(e, 12, T)
        kb, e = place(e, HC, T)
        bk, e = place(e, HC, T)
        qe, e = place(e, HC, T)
        vb, e = place(e, HC, T)
        ke, e = place(e, HC, L)
        ketok, e = place(e, NCH, 512)
        vbtok, e = place(e, NCH, 512)
        qkd, e = place(e, 4, 512)
        ws1, _ = place(e - 2048, HC, NS, HD)
        gs, _ = place(e, 5, T)
        xx, e = place(e, 4, 512)
        ws2, _ = place(e - 2048, HC, NS, HD)
        dt_, e = place(e, 2, 512)
        rhst, e = place(e, 512)
        utok, e = place(e, 512)
        rmask, e = place(e, L)
        assert e <= WORK - HC * T
        zg, _ = place(WORK - HC * T, HC, T)
        mt, _ = place(0, 4, 512)
        ml, _ = place(2048, 2, 512)
        sgs, _ = place(0, HC, NS, HD)
        flat = "p a b -> p (a b)"
        xt = sq[:, :, :].rearrange(flat)[:, 0:2048].rearrange("p (g n) -> p g n", g=4)
        t1 = mix[:, :, :].rearrange(flat)[:, 0:2048].rearrange("p (g n) -> p g n", g=4)
        KB, BK, QE, VB, KE, QKD, XX = [3204 + 12 * T + n for n in (0, 4 * T, 8 * T, 12 * T, 16 * T, 16 * T + 3072,
                                                                   16 * T + 5120)]
        zq, _ = place(KB, HC, T)
        zh, _ = place(BK, HC, T)
        zi, _ = place(QE, HC, T)
        zf, _ = place(KE, HC, T)
        zk, e = place(KE + 4 * T, HC, T)
        fl, e = place(e, HC, L // HCK)
        assert e <= QKD
        lf, _ = place(VB, HC, L)
        bcs, _ = place(2048, HC, L)
        d1, e = place(XX + 2048, HC, L)
        d2, e = place(e, HC, L)
        assert e <= WORK - HC * T, e
        qx, kx, qin, ko = lf, d1, bcs, d2
        attb, e = place(3204, 4, 512)
        hws2, _ = place(3204, HC, NS, HD)
        hkt, e = place(e, NCH, 512)
        assert e <= KB
        SH = [place(QKD + 256 * (k % 8), HC, HD)[0] for k in range(8)]
        hvt, _ = place(XX, NCH, 512)
        hws1, _ = place(XX, HC, NS, HD)
        shs, _ = place(0, HC, NS, HD)
        mh, e = place(0, KC, NM)
        mk, e = place(e, MH, NM)
        mv, e = place(e, MH, NM)
        mvt, e = place(e, 2, 512)
        mq, e = place(e, MH, T)
        msb, e = place(e, 2, 512)
        mpt, e = place(e, 2, 512)
        mqz, e = place(e, MH, NS, 32)
        mpm, e = place(e, 2, NM)
        mps, e = place(e, 4, 4, MH)
        mos, e = place(e, 2, 512)
        msm, e = place(e, 2, 4)
        msel, e = place(e, 2, 4 * MH)
        att_buf = {"mem0": (msb, mpt), "mem1": (msb, mpt)}
        act_, _ = place(0, FT, T)
        act_lo, e = place(0, FT, T, of=work_r)
        act_hi, e = place(e, FT, T, of=work_r)
        w_hi, e = place(e, 2, SLOTW, of=work_r)
        gb, e = place(e, 3, 2 + T)
        cacc, e = place(e, 2, T)
        csil, e = place(e, 2, T)
        fo, e = place(e, FT, 18)
        fh, e = place(e, FT, 16)
        split_slots = [n for n, v in enumerate(slots) if v[1][:2] == "gu" or v[1][:4] == "down"]
        split_no = {n: k for k, n in enumerate(split_slots)}
        FFN_SLOTS = len(split_slots) // 2
        zo, e = place(0, 16, T)
        hank, e = place(e, H, 384)
        ovt, e = place(e, 2, 512)
        osb, e = place(e, 2, 512)
        opt, e = place(e, 2, 512)
        att_buf["moba"] = (osb, opt)
        bsp, e = place(e, 2, 512)
        spt, _ = place(e - 1024, 4, 4, 4, H)
        ssc, e = place(e, 2, 1024)
        kz, _ = place(e - 1024, HC, NS, 32)
        WTMP = e - 1024
        cosT, e = place(e, NT, L)
        sinT, e = place(e, NT, L)
        ygl = zo[:, 8:12, :]
        s0 = 16 * T
        TABTMP = s0
        NHB = 8
        tmpy = zo[:, 0:4, :]
        ta, e2 = place(s0, 2, 2, L)
        tb, e2 = place(e2, 2, 2, L)
        gg, e2 = place(e2, 2, 2, L)
        pt_, e2 = place(e2, 2, 2, L)
        HH = [place(e2 + 512 * i if i < 4 else e - 2 * NT * L - 2048 + 512 * (i - 4), 2, L)[0] for i in range(NHB)]
        e2 += 4 * 512
        assert e2 <= e - 2 * NT * L - 3072
        oTf = oT[:, :, :].rearrange(flat)
        hsS = oTf[:, 0:256].rearrange("p (q n s) -> p q n s", q=2, n=NT)
        w3, w4 = [oTf[:, o:o + 128].rearrange("p (n s) -> p n s", n=NT) for o in (256, 384)]
        mixf, tmpf = mix[:, :, :].rearrange(flat), tmp[:, :, :].rearrange("p a b -> p (a b)")
        qz = mixf[:, 1056:2080].rearrange("p (c s h) -> p c s h", c=HC, s=NS)
        osm = mixf[:, 1056:2080].rearrange("p (g n) -> p g n", g=2)
        relr = tmpf[0:32, 0:128]
        sel2 = tmpf[:, 128:256].rearrange("p (a g n) -> p a g n", a=2, g=2)
        gsm = tmpf[:, 256:256 + 72].rearrange("p (r n) -> p r n", r=9)
        gs2 = tmpf[:, 336:336 + 20].rearrange("p (r g) -> p r g", g=2)
        sqf, hf_ = sq[:, :, :].rearrange(flat), h[:, :, :].rearrange(flat)
        s5b = sqf[:, 0:1024].rearrange("p (q c n) -> p q c n", q=2, c=4)
        s5c = sqf[:, 1024:2048].rearrange("p (q n k) -> p q n k", q=2, n=NT)
        s5cp = hf_[:, 0:1536].rearrange("p (q n k) -> p q n k", q=3, n=NT)
        s5h = hf_[:, 1536:1792].rearrange("p (q n s) -> p q n s", q=2, n=NT)
        s5o = sb("s5o", [128, 2, NT, 9])
        hl = sb("hl", [128, 2, NT])
        t16 = sb("t16", [128, 4, NT])
        bxs = mixf[0:8, 0:512]
        smx = sb("smx", [128, 2, 4, 2])

        s_slots = list(enumerate(slots))

        block = ctx.enter_context(nc.Block())

        @block.sync
        def _(sp):
            early = CON["neg"]
            sp.dma_start(x[:, :, :], A["x"]).then_inc(x_in, 16)
            sp.dma_start(con[:, 0:early], A["con"][:, 0:early]).then_inc(con_in, 16)
            sp.dma_start(vec[:, :], A["vec"]).then_inc(vec_in, 16)
            for s, (kind, name, i, w, _) in s_slots:
                if s == SLOTS:
                    sp.dma_start(con[:, early:], A["con"][:, early:]).then_inc(con2_in, 16)
                    sp.dma_start(pages[:, :], A["pages"]).then_inc(pages_in, 16)
                    sp.wait_ge(pages_in, 16)
                if kind == "page":
                    if name == "pk":
                        i = 2 * (4 * (i // 8) + i % 4) + i // 4 % 2
                    else:
                        i = 2 * (2 * (i // 4) + i % 2) + i // 2 % 2
                    numbers = [sp.value_load(pages[0:1, at:at + 1], min_val=0, max_val=POOL_PAGES - 1)
                               for at in range(4 * i, 4 * i + 4)]
                if s >= SLOTS:
                    last = slots[s - SLOTS][4]
                    if last[0] == "used":
                        sp.wait_ge(pages_used, last[1])
                    else:
                        full(sp, last)
                dst = ring[:, s % SLOTS, 0:w]
                if kind == "w":
                    sp.dma_start(dst, A[name][i]).then_inc(ring_full[s % SLOTS], 16)
                    continue
                pool = A["pool_k"] if name == "pk" else A["pool_v"]
                for j, page in enumerate(numbers):
                    sp.dma_start(dst[:, 512 * j:512 * (j + 1)].unsqueeze(1),
                                 pool[bass.ds(page, 1)].rearrange("a p n -> p a n")).then_inc(ring_full[s % SLOTS], 16)

        @block.gpsimd
        def _(pool):
            step = Steps(pool, pool_step)
            stores = [0]

            def store(dst, src, done=None):
                pool.dma_start(dst, src).then_inc(done or stored, 16)
                if not done:
                    stores[0] += 1

            step(nc.gpsimd.memset(rmask, 1.0))
            nc.gpsimd.memset(rmask.rearrange("p (k c) -> p k c", c=HCK)[:, :, 0:1], 0.0).then_inc(pads_ready, 1)
            nc.gpsimd.memset(zqkv[:, :, 0:3], 0.0).then_inc(pads_ready, 1)
            pool.dma_start(ch[:, :, :], A["gconv"]).then_inc(hist_in, 16)

            pool.wait_ge(hist_in, 16)
            drained(pool, ("lin", "ev_in_a", 11))
            nc.gpsimd.tensor_copy(cvo[:, :, 0:3], zqkv[:, :, 256:259])
            nc.gpsimd.tensor_copy(cvo[:, :, 3:19], ch[:, :, 8:24])
            nc.gpsimd.tensor_copy(cvo[:, :, 19:27], zqkv[:, :, 259:267]).then_inc(cvo_ready, 1)
            pool.wait_ge(cvo_ready, 1)
            store(A["o_gconv"], cvo[:, :, :])
            pool.wait_ge(xt_ready, 4)
            pool.wait_ge(con2_in, 16)
            for l in range(1, LEV):
                for gi, g in enumerate(G4):
                    n = (l - 1) * 4 + gi
                    if n >= 2:
                        pn = n - 2
                        full(pool, ("T1", pn // 4 + 1, G4[pn % 4]))
                    nc.gpsimd.tensor_tensor(ml[:, n % 2, :].rearrange("p (n k) -> p n k", n=4),
                                            mt[:, gi, :].rearrange("p (n k) -> p n k", n=4),
                                            four(cst("lev", i=l)), ALU.mult).then_inc(ml_ready, 1)
            full(pool, ("T1", LEV - 1, G4[3]))
            pool.dma_start(sgs, A["sgs"]).then_inc(sgs_in, 16)
            drained(pool, ("S", "gdn", NCH - 1))
            store(A["o_gdn"], sg[:, :, :])
            pool.wait_ge(sgs_in, 16)
            pool.wait_ge(w_ready, 1)
            nc.gpsimd.tensor_tensor(sgs, sgs, egc[:, :, 1:9].unsqueeze(3).broadcast_to([128, HC, NS, HD]),
                                    ALU.mult).then_inc(sdec_ready, 1)
            pool.wait_ge(sst_ready, 4)
            pool.dma_start(A["o_sgs"], sgs).then_inc(sgs_out, 16)
            pool.wait_ge(sgs_out, 16)
            full(pool, ("sO", "gdn"))
            pool.dma_start(shs, A["shs"]).then_inc(shs_in, 16)
            nc.gpsimd.memset(attb, 0.0).then_inc(att_zero, 1)
            for m in range(4, 8):
                drained(pool, ("lin", "ev_in_b", m))
            pool.wait_ge(exp_ready, 4)
            pool.wait_ge(fk_ready, HC)
            nc.gpsimd.tensor_copy(fl, qin[:, :, HCK - 1::HCK]).then_inc(hg_pool, 1)
            pool.wait_ge(hg_pool, 1)
            nc.gpsimd.tensor_tensor(ko, ko, zk[:, :, 0:L], ALU.mult).then_inc(hg_pool, 1)
            nc.gpsimd.tensor_tensor(qin, qin, zq[:, :, 0:L], ALU.mult).then_inc(hg_pool, 1)
            pool.wait_ge(shs_in, 16)
            nc.gpsimd.tensor_tensor(shs, shs, zf[:, :, L:T].unsqueeze(3).broadcast_to([128, HC, NS, HD]),
                                    ALU.mult).then_inc(sdec_ready, 1)
            full(pool, ("ho", G4[3]))
            drained(pool, ("lin", "ev_in_b", 11))
            nc.gpsimd.tensor_tensor(hws2, cst("i2", 64).unsqueeze(1).unsqueeze(1).broadcast_to([128, HC, NS, HD]),
                                    zi[:, :, L:T].unsqueeze(3).broadcast_to([128, HC, NS, HD]),
                                    ALU.mult).then_inc(w_ready, 1)
            drained(pool, ("kv", 7))
            store(A["o_hgrn"], SH[0], hg_stored)
            pool.wait_ge(sst_ready, 8)
            store(A["o_shs"], shs, hg_stored)

            def memory_io(l):
                full(pool, ("lin", "ev_in_b", 15) if l == 0 else ("sx", "moba"))
                pool.dma_start(h[:, :, 0:NM], A["memx"]).then_inc(memx_in, 16)
                pool.wait_ge(hn_done, hn_no[(f"memk{l}", MH - 1)] + 1)
                store(A["o_memk"][l], mk, mem_stored)
                drained(pool, ("lin", f"memv{l}", MH - 1))
                store(A["o_memv"][l], mv, mem_stored)

            def ffn_rows(l):
                full(pool, ("ss", "ffn", l))
                nc.gpsimd.memset(gb[:, :, 0:2], 0.0).then_inc(fpads, 1)
                pool.dma_start(fh, A["fh"][l]).then_inc(fh_in, 16)
                pool.wait_ge(fh_in, 16 * (l + 1))
                for i in range(FT + 2):
                    if i < FT:
                        drained(pool, ("lin", f"gu{l}", 2 * i))
                        nc.gpsimd.tensor_copy(fo[:, i, 0:2], gb[:, i % 3, 2 + L - 2:2 + L])
                        nc.gpsimd.tensor_copy(fo[:, i, 10:18], gb[:, i % 3, 2 + L:2 + T]).then_inc(fcopy_done, 1)
                    if i >= 2:
                        pool.wait_ge(ah_ready, l * FT + i - 1)
                        nc.gpsimd.tensor_tensor(act_lo[:, i - 2, :], act_[:, i - 2, :],
                                                act_hi[:, i - 2, :].bitcast(F32), ALU.subtract).then_inc(al_ready, 1)
                nc.gpsimd.tensor_copy(fo[:, :, 2:10], fh[:, :, 8:16]).then_inc(fcopy_done, 1)
                pool.wait_ge(fcopy_done, (FT + 1) * (l + 1))
                store(A["o_ffn"][l], fo, ffn_stored)

            memory_io(0)
            ffn_rows(0)
            full(pool, ("ss", "mix", 1))
            pool.dma_start(s5b, A["s5b"]).then_inc(s5_in, 16)
            pool.dma_start(s5c, A["s5c"]).then_inc(s5_in, 16)
            drained(pool, ("bx",))
            pool.dma_start(A["bias_x"], bxs).then_inc(bx_stored, 16)
            full(pool, ("lin", "od_in", 15))
            pool.dma_start(s5h, A["s5h"]).then_inc(s5_in, 16)
            pool.wait_ge(hn_done, hn_no[("moba", 7)] + 1)
            store(A["o_k"], zo[:, 4:8, :], kv_stored)
            drained(pool, ("lin", "od_in", 11))
            store(A["o_v"], zo[:, 8:12, :], kv_stored)
            for n in range(NT):
                pool.wait_ge(s5_g, 2 * (n + 1))
                b = n % 2
                if n == 4:
                    full(pool, ("pt", "moba", 3))
                if n >= NHB:
                    full(pool, ("s5y", (n - NHB) // 4))
                H_ = HH[n % NHB]
                step(nc.gpsimd.tensor_tensor(pt_[:, b, 0, :], gg[:, b, 0, :], sinT[:, n, :], ALU.mult))
                step(nc.gpsimd.tensor_tensor(pt_[:, b, 1, :], gg[:, b, 1, :], cosT[:, n, :], ALU.mult))
                nc.gpsimd.tensor_tensor(H_[:, 1, :], pt_[:, b, 0, :], pt_[:, b, 1, :], ALU.add).then_inc(s5_hi, 1)
                pool.wait_ge(s5_hi, 2 * n + 1)
                nc.gpsimd.tensor_copy(hl[:, 1, n:n + 1], H_[:, 1, L - 1:L]).then_inc(s5_hi, 1)
            pool.wait_ge(s5_hs, 3)
            store(A["o_s5"], s5o[:, :, :, :])
            memory_io(1)
            ffn_rows(1)
            drained(pool, ("lin", "down1", KC - 1))
            store(A["y"], x[:, :, :])
            for s_, n in ((stored, stores[0]), (hg_stored, 2), (mem_stored, 4), (ffn_stored, 2), (kv_stored, 2)):
                pool.wait_ge(s_, 16 * n)

        @block.scalar
        def _(act):
            step = Steps(act, act_step)

            table = [""]

            def log_exp_tables():
                if table[0] != "log_exp":
                    nc.scalar.preload_act_table_set("natural_log_exp_and_others")
                    table[0] = "log_exp"

            def f(out, in_, func, **k):
                if func in (ACT.Ln, ACT.Exp):
                    log_exp_tables()
                elif func not in (ACT.Copy, ACT.Square):
                    table[0] = ""
                return nc.scalar.activation(out, in_, func, **k)

            def norm(i):
                kind, l = norms[i]
                w = NM if kind == "memkv" else T
                key = ("ss", kind, l)
                log_exp_tables()
                full(act, key)
                if seen["hn"]:
                    act.wait_ge(hr_ready, seen["hn"])
                seen["norm"] += 1
                f(lnb[:, 0, 0:w], bank(key)[:, 0:w], ACT.Ln, scale=1.0 / D, bias=epsc).then_inc(
                    psum_free[no[key] % NBANK], 1)
                drained(act, key)
                f(rs[:, 0:w], lnb[:, 0, 0:w], ACT.Exp, scale=-0.5).then_inc(r_ready, 1)

            seen = {"hn": 0, "norm": 0}

            def squares(name, chunks=range(KC)):
                for m in chunks:
                    drained(act, ("lin", name, m))
                    f(sq[:, m, :], x[:, m, :], ACT.Square).then_inc(sq_ready, 1)

            def hn_square(name, i, w, src):
                if i >= 2:
                    full(act, ("hn", name, i - 2))
                f(hsq[:, (hn_no[(name, 0)] + i) % 2, 0:w], src, ACT.Square).then_inc(hsq_ready, 1)

            def hn_roots(name, i, w, mean):
                first = hn_no[(name, 0)] + i
                log_exp_tables()
                full(act, ("hn", name, i + 1))
                act.wait_ge(r_ready, seen["norm"])
                if first:
                    act.wait_ge(hr_ready, first)
                for m in range(2):
                    key = ("hn", name, i + m)
                    drain(f(lnb[:, m, 0:w], bank(key)[:, 0:w], ACT.Ln, scale=mean, bias=epsc), key)
                for m in range(2):
                    j = first + m
                    drained(act, ("hn", name, i + m))
                    if j >= 2:
                        act.wait_ge(hn_done, j - 1)
                    f(hr[:, j % 2, 0:w], lnb[:, m, 0:w], ACT.Exp, scale=-0.5).then_inc(hr_ready, 1)
                seen["hn"] = first + 2

            def headnorm(name, n, w, mean, src, meanwhile=None):
                hn_square(name, 0, w, src(0))
                for i in range(n + 1):
                    if i < n and meanwhile:
                        meanwhile(i)
                    if i + 1 < n:
                        hn_square(name, i + 1, w, src(i + 1))
                    if i >= 2 and i % 2 == 0:
                        hn_roots(name, i - 2, w, mean)

            def copy_out(key, dst, src):
                full(act, key)
                drain(f(dst, src, ACT.Copy), key)

            def samples_out(name, dst, nh):
                n = 2 if nh == MH else 4
                act.wait_ge(qz_ready, ["mem0", "moba", "mem1"].index(name) * 2 + 2)
                for i in range(n):
                    key = ("so", name, i)
                    full(act, key)
                    for s_ in range(NS // n * i, NS // n * (i + 1)):
                        r = 32 * (s_ % 4)
                        ins = f(dst[r:r + nh, s_ // 4, :], bank(key)[r:r + nh, :], ACT.Copy)
                    drain(ins, key)

            def attend(name, n, hd, after=None):
                pbuf, ptb = att_buf[name]
                for i in range(n + 2):
                    if i < n:
                        j = at_no[(name, i)]
                        act.wait_ge(smax_ready, j + 1)
                        b = j % 2
                        for qt in range(2):
                            v = pbuf[:, i % 2, qt * L:(qt + 1) * L]
                            ins = f(v, v, ACT.Exp, bias=smx[:, b, 0, qt:qt + 1], scale=1.0,
                                    accum_out=smx[:, b, 1, qt:qt + 1])
                        ins.then_inc(p_exp, 1)
                    if 0 <= i - 1 < n:
                        key = ("PT", name, i - 1)
                        full(act, key)
                        drain(f(ptb[:, (i - 1) % 2, :], bank(key)[:, :], ACT.Copy), key)
                    if 0 <= i - 2 < n:
                        k = i - 2
                        key = ("O", name, k)
                        p0 = 0 if hd == 128 else 64 * (k % 2)
                        c = k if hd == 128 else k // 2
                        copy_out(key, mix[p0:p0 + hd, c, 0:L], bank(key)[p0:p0 + hd, 0:L])
                    if after:
                        after(i)

            epsc = epst[:, 0:1]
            act.wait_ge(eps_ready, 1)
            act.wait_ge(x_in, 16)
            for m in range(KC):
                f(sq[:, m, :], x[:, m, :], ACT.Square).then_inc(sq_ready, 1)
            act.wait_ge(vec_in, 16)
            act.wait_ge(lb_step, 1)
            f(lbt[:, 0:3, :], lbt[:, 0:3, :], ACT.Exp).then_inc(lb_step, 1)
            f(par[:, 0, :], cols("s5_dt", NT), ACT.Exp).then_inc(s5_par, 1)
            norm(0)
            act.wait_ge(s5_par, 2)
            f(par[:, 1, :], par[:, 1, :], ACT.Exp)
            f(par[:, 4, :], par[:, 4, :], ACT.Sin)
            f(par[:, 5, :], par[:, 5, :], ACT.Sin).then_inc(s5_par, 1)
            full(act, ("ab",))
            f(gs[0:8, 0, :], bank(("ab",))[0:8, 0:T], ACT.Exp, scale=-1.0).then_inc(gate_rows, 1)
            f(aexp[0:8, :], col("small", 1, 0, 8), ACT.Exp).then_inc(gate_rows, 1)
            act.wait_ge(gate_rows, 3)
            step(f(gs[0:8, 4, :], gs[0:8, 4, :], ACT.Exp))
            f(gs[0:8, 4, :], gs[0:8, 4, :], ACT.Ln, bias=onec[0:8, 0:1]).then_inc(gate_rows, 1)
            act.wait_ge(gate_rows, 5)
            f(gs[0:8, 2, :], gs[0:8, 4, :], ACT.Exp)
            f(gs[0:8, 3, 0:L], gs[0:8, 3, 0:L], ACT.Exp).then_inc(gate_rows, 1)
            def in_a(m):
                key = ("lin", "ev_in_a", m)
                full(act, key)
                if m < 12:
                    drain(f(zqkv[:, m, 3:3 + T], bank(key)[:, 0:T], ACT.Copy), key)
                else:
                    drain(f(zg[:, m - 12, :], bank(key)[:, 0:T], ACT.Silu), key)
                if 2 <= m < 14:
                    act.wait_ge(conv_done, m - 1)
                    f(qkv[:, m - 2, :], qkv[:, m - 2, :], ACT.Silu).then_inc(silu_done, 1)

            def silued(i):
                act.wait_ge(silu_done, i + 1)
                return qkv[:, i, :]
            for m in range(8):
                in_a(m)
            headnorm("l2", 8, T, 1.0, silued, lambda i: in_a(8 + i))
            for t in range(NCH):
                copy_out(("trk", t), ketok[:, t, :], bank(("trk", t))[:, :])
                copy_out(("trv", t), vbtok[:, t, :], bank(("trv", t))[:, :])
            for gi, g in enumerate(G4):
                if gi >= 2:
                    drained(act, ("KK", G4[gi - 2]))
                full(act, ("DT", g))
                drain(f(dt_[:, gi % 2, :], bank(("DT", g))[:, :], ACT.Exp), ("DT", g))
            for gi, g in enumerate(G4):
                copy_out(("X1", g), xx[:, gi, :], bank(("X1", g))[:, :])
            for l in range(1, LEV):
                for gi, g in enumerate(G4):
                    copy_out(("T1", l, g), t1[:, gi, :], bank(("T1", l, g))[:, :])

            def o_copy(key, p, at, t):
                full(act, key)
                drain(f(oT[64 * p:64 * p + 64, :, t * 128:(t + 1) * 128],
                        blocks(key, 4, 64 * p, 64 * p + 64), ACT.Copy), key)

            def so_copy(name):
                copy_out(("sO", name), oT[:, :, L:T], bank(("sO", name))[:, 0:32].rearrange("p (c s) -> p c s", c=HC))

            for t in range(NCH):
                copy_out(("u", t), utok, bank(("u", t))[:, :])
                for p in range(2):
                    o_copy(("o", t, p), p, 0, t)

            def in_b(m):
                key = ("lin", "ev_in_b", m)
                b = bank(key)[:, 0:T]
                full(act, key)
                if m < 4:
                    f(zf[:, m, :], b, ACT.Sigmoid)
                    drain(f(zk[:, m, :], b, ACT.Sigmoid, scale=-1.0), key)
                elif m < 8:
                    drain(f(zq[:, m - 4, :], b, ACT.Silu), key)
                elif m < 12:
                    drain(f(zi[:, m - 8, :], b, ACT.Copy), key)
                else:
                    drain(f(zh[:, m - 12, :], b, ACT.Silu), key)
            for m in range(8):
                in_b(m)
            act.wait_ge(w_ready, 2)
            act.wait_ge(fk_ready, HC)
            f(lf, zf[:, :, 0:L], ACT.Ln).then_inc(lf_ready, 1)
            so_copy("gdn")
            for m in range(8, 12):
                in_b(m)
            act.wait_ge(dec_ready, 2)
            f(qx, d1, ACT.Exp).then_inc(exp_ready, 1)
            act.wait_ge(exp_ready, 1)
            f(kx, d1, ACT.Exp, scale=-1.0).then_inc(exp_ready, 1)
            f(qin, bcs, ACT.Exp).then_inc(exp_ready, 1)
            f(ko, d2, ACT.Exp).then_inc(exp_ready, 1)

            def out_rows(name):
                def src(i):
                    drained(act, ("sO", name))
                    return oT[:, i, :]
                return src
            headnorm("gdn", HC, T, 1.0 / HD, out_rows("gdn"), lambda i: in_b(12 + i))
            for t in range(NCH):
                copy_out(("htk", t), hkt[:, t, :], bank(("htk", t))[:, :])
                copy_out(("htv", t), hvt[:, t, :], bank(("htv", t))[:, :])
            act.wait_ge(mix_ready, HC)
            for t, p in G4:
                o_copy(("ho", (t, p)), p, 0, t)
            so_copy("hgrn")
            headnorm("hgrn", HC, T, 1.0 / HD, out_rows("hgrn"))

            def memory_norm(l):
                act.wait_ge(memx_in, 16 * (l + 1))
                act.wait_ge(hg_stored if l == 0 else kv_stored, 32)
                for m in range(KC):
                    f(mh[:, m, :], h[:, m, 0:NM], ACT.Square).then_inc(msq_ready, 1)
                norm(norms.index(("memkv", l)))
            memory_norm(0)
            squares("ev_out")

            def memory(l):
                for m in range(MH):
                    copy_out(("lin", f"memk{l}", m), mk[:, m, :], bank(("lin", f"memk{l}", m))[:, 0:NM])
                norm(norms.index(("mem", l)))

                def key_rows(i):
                    drained(act, ("lin", f"memk{l}", i))
                    return mk[:, i, :]
                headnorm(f"memk{l}", MH, NM, 1.0 / 128, key_rows,
                         lambda m: copy_out(("lin", f"memv{l}", m), mv[:, m, :],
                                            bank(("lin", f"memv{l}", m))[:, 0:NM]))
                for t in range(2):
                    copy_out(("mvt", l, t), mvt[:, t, :], bank(("mvt", l, t))[:, :])

                def query(m):
                    copy_out(("lin", f"wq{l}", m), mq[:, m, :], bank(("lin", f"wq{l}", m))[:, 0:T])
                    drained(act, ("lin", f"wq{l}", m))
                    hn_square(f"memq{l}", m, T, mq[:, m, :])
                for m in range(MH):
                    query(m)
                for m in (0, 2):
                    hn_roots(f"memq{l}", m, T, 1.0 / 128)
                name = f"mem{l}"

                def probs(i):
                    if i in (2, 4):
                        g = i // 2 - 1
                        key = ("sc", name, g)
                        act.wait_ge(mx_ready, MXN[name] + g + 1)
                        drain(f(mpm[:, g, :], bank(key)[:, 0:NM], ACT.Exp, bias=msm[:, g, 1:2], scale=128 ** -0.5,
                                accum_out=msm[:, g, 2:3]), key)
                attend(name, MH, 128, probs)
                copy_out(("pt", name, 0), mps, bank(("pt", name, 0))[:, :].rearrange(
                    "p (n j h) -> p n j h", n=4, j=4)[:, :, :, 0:MH])
                samples_out(name, mos, MH)
                weights_high(l, 0)
                weights_high(l, 1)
                squares(f"wo{l}")

            def weights_high(l, n):
                k = FFN_SLOTS * l + n
                s_ = split_slots[k]
                act.wait_ge(ring_full[s_ % SLOTS], slot_value[s_])
                if k >= 2:
                    full(act, slots[split_slots[k - 2]][4])
                w = slots[s_][3]
                f(w_hi[:, k % 2, 0:w], ring[:, s_ % SLOTS, 0:w], ACT.Copy).then_inc(wh_ready, 1)

            def ffn(l):
                n_ = norms.index(("ffn", l))
                norm(n_)
                for k in range(KC):
                    act.wait_ge(h_ready, KC * n_ + k + 1)
                    f(mix_r[:, k, :], h[:, k, :], ACT.Copy).then_inc(xh_ready, 1)
                act.wait_ge(fpads, l + 1)
                for i in range(FT + 2):
                    if 1 <= i < FT:
                        weights_high(l, i + 1)
                    if i < FT:
                        key = ("lin", f"gu{l}", 2 * i)
                        full(act, key)
                        n = l * FT + i
                        if i >= 3:
                            act.wait_ge(fconv_done, n - 2)
                            act.wait_ge(fcopy_done, l * (FT + 1) + i - 2)
                        drain(f(gb[:, i % 3, 2:2 + T], bank(key)[:, 0:T], ACT.Copy), key)
                    if 1 <= i <= FT:
                        n = l * FT + i - 1
                        act.wait_ge(fconv_done, n + 1)
                        if i >= 3:
                            drained(act, ("lin", f"gu{l}", 2 * (i - 3) + 1))
                        f(csil[:, (i - 1) % 2, :], cacc[:, (i - 1) % 2, :], ACT.Silu).then_inc(fsilu_done, 1)
                    if i >= 2:
                        drained(act, ("lin", f"gu{l}", 2 * (i - 2) + 1))
                        f(act_hi[:, i - 2, :], act_[:, i - 2, :], ACT.Copy).then_inc(ah_ready, 1)
                for m in range(KC):
                    if m < KC - 1:
                        weights_high(l, FT + m + 1)
                    if l == 0 and m:
                        squares("down0", (m - 1,))
                if l == 0:
                    squares("down0", (KC - 1,))

            memory(0)
            ffn(0)
            norm(norms.index(("mix", 1)))
            act.wait_ge(mem_stored, 32)
            def od_in(m):
                key = ("lin", "od_in", m)
                copy_out(key, zo[:, m, :], bank(key)[:, 0:T])

            def head_rows(i):
                drained(act, ("lin", "od_in", i))
                return zo[:, i, :]
            for m in range(8):
                od_in(m)
            copy_out(("bx",), bxs, bank(("bx",))[0:8, 0:512])

            def meanwhile(i):
                od_in(8 + i)
                if i == 3:
                    bx = A["bias_x"]
                    act.wait_ge(bx_stored, 16)
                    act.wait_ge(hn_done, hn_no[("moba", 0)] + 1)
                    act.dma_start(hank, bass.AP(tensor=bx.tensor, offset=bx.offset,
                                                ap=[[1, 128], [512, H], [1, 384]])).then_inc(bias_in, 16)
            headnorm("moba", 8, T, 1.0 / HD, head_rows, meanwhile)
            for t in range(2):
                copy_out(("vt", t), ovt[:, t, :], bank(("vt", t))[:, :])
            for i in range(2):
                copy_out(("bs", i), bsp[:, i, :], bank(("bs", i))[:, :])
            attend("moba", H, 64)
            act.wait_ge(mx_ready, MXN["moba"] + 1)
            for g in range(2):
                for b in range(4):
                    v = ssc[:, g, 256 * b:256 * (b + 1)]
                    ins = f(v, v, ACT.Exp, bias=gsm[:, 5, 4 * g + b:4 * g + b + 1], scale=1.0,
                            accum_out=gsm[:, 6, 4 * g + b:4 * g + b + 1])
                    if b % 2:
                        ins.then_inc(pp_ready, 1)
                f(gs2[:, 4, g:g + 1], gs2[:, 2, g:g + 1], ACT.Exp, bias=gs2[:, 3, g:g + 1], scale=1.0)
            ins = f(gs2[:, 9, 0:1], gs2[:, 2, 0:1], ACT.Copy)
            ins.then_inc(pp_ready, 1)
            for i in range(4):
                key = ("pt", "moba", i)
                copy_out(key, spt[:, i], bank(key)[:, :].rearrange("p (n j h) -> p n j h", n=4, j=4)[:, :, :, 0:H])
            samples_out("moba", osm, H)
            act.wait_ge(kv_stored, 32)
            for c in range(HC):
                drained(act, ("s5y", c))
                f(ygl[:, c, :], tmpy[:, c, :], ACT.Gelu_apprx_tanh).then_inc(s5_gl2, 1)
            drained(act, ("sx", "moba"))
            for c in range(HC):
                key = ("lin", "glu", 2 * c + 1)
                full(act, key)
                if c >= 2:
                    drained(act, ("lin", "glu", 2 * (c - 2)))
                drain(f(tmp[:, c % 2, :], bank(key)[:, 0:T], ACT.Sigmoid), key)
            memory_norm(1)
            squares("od_out")
            memory(1)
            ffn(1)

        @block.tensor
        def _(pe):
            at = [0]

            def begin(key):
                assert order[at[0]] == key, (order[at[0]], key)
                if at[0] >= NBANK:
                    pe.wait_ge(psum_free[at[0] % NBANK], at[0] // NBANK)
                return bank(key)

            def end(ins):
                ins.then_inc(psum_full, 1)
                at[0] += 1

            def mm(out, lhsT, rhs, start=True, stop=True):
                return nc.tensor.matmul(out, lhsT, rhs, start=start, stop=stop, skip_group_check=True)

            def tr(out, in_):
                return nc.tensor.transpose(out, in_, ident)

            def norm(i):
                kind, l = norms[i]
                w = NM if kind == "memkv" else T
                b = begin(("ss", kind, l))
                src = mh if kind == "memkv" else sq
                for k in range(KC):
                    if kind == "memkv":
                        pe.wait_ge(msq_ready, KC * l + k + 1)
                    else:
                        pe.wait_ge(sq_ready, KC * xnorms.index((kind, l)) + k + 1)
                    ins = mm(b[:, 0:w], ones, src[:, k, 0:w], k == 0, k == KC - 1)
                end(ins)

            def hready(i):
                return lambda k: pe.wait_ge(h_ready, KC * i + k + 1)

            def open_(key):
                assert at[0] <= no[key] < at[0] + NBANK
                if no[key] >= NBANK:
                    pe.wait_ge(psum_free[no[key] % NBANK], no[key] // NBANK)
                return bank(key)

            def close(ins, key):
                assert order[at[0]] == key
                end(ins)

            def slot(name, i):
                n = slot_of[(name, i)]
                pe.wait_ge(ring_full[n % SLOTS], slot_value[n])
                return ring[:, n % SLOTS, :]

            def slot_done(ins, name, i):
                last = slots[slot_of[(name, i)]][4]
                if last[0] == "used":
                    ins.then_inc(pages_used, 1)
                else:
                    close(ins, last)

            def lin(name, m, kc, per_slot, src, w, ready=None):
                b = begin(("lin", name, m))
                s = slot_of[(name, m)]
                if m % per_slot == 0:
                    pe.wait_ge(ring_full[s % SLOTS], slot_value[s])
                for k in range(kc):
                    if ready and m == 0:
                        ready(k)
                    o = ((m % per_slot) * kc + k) * 128
                    ins = mm(b[:, 0:w], ring[:, s % SLOTS, o:o + 128], src[:, k, 0:w], k == 0, k == kc - 1)
                end(ins)

            def lin3(name, m, kc, per_slot, hi, lo, ready):
                b = begin(("lin", name, m))
                s = slot_of[(name, m)]
                n = split_no[s]
                if m % per_slot == 0:
                    pe.wait_ge(wl_ready, n + 1)
                for k in range(kc):
                    if m == 0:
                        ready(k)
                    o = ((m % per_slot) * kc + k) * 128
                    wh, wl = w_hi[:, n % 2, o:o + 128], ring_r[:, s % SLOTS, o:o + 128]
                    mm(b[:, 0:T], wh, hi[:, k, :], k == 0, False)
                    mm(b[:, 0:T], wh, lo[:, k, :], False, False)
                    ins = mm(b[:, 0:T], wl, hi[:, k, :], False, k == kc - 1)
                end(ins)

            def hn(name, i, w, lhsT):
                j = hn_no[(name, i)]
                b = begin(("hn", name, i))
                pe.wait_ge(hsq_ready, j + 1)
                end(mm(b[:, 0:w], lhsT, hsq[:, j % 2, 0:w]))

            def transposes(key, srcs):
                b = begin(key)
                for j, v in enumerate(srcs):
                    ins = tr(b[:, 128 * j:128 * (j + 1)], v)
                end(ins)

            def attend(name, n, hd, q, k, vt, between):
                pbuf, ptb = att_buf[name]
                for i in range(n + 2):
                    if i < n:
                        b = begin(("S", name, i))
                        p0, c = (0, i) if hd == 128 else (64 * (i % 2), i // 2)
                        for qt in range(2):
                            ins = mm(b[:, qt * L:(qt + 1) * L], q[p0:p0 + hd, c, qt * 128:(qt + 1) * 128],
                                     k[p0:p0 + hd, c, 0:L])
                        end(ins)
                    between(i, 0)
                    if 0 <= i - 1 < n:
                        b = begin(("PT", name, i - 1))
                        pe.wait_ge(p_ready, at_no[(name, i - 1)] + 1)
                        for kt in range(2):
                            for qt in range(2):
                                ins = tr(b[:, kt * L + qt * 128:kt * L + (qt + 1) * 128],
                                         pbuf[:, (i - 1) % 2, qt * L + kt * 128:qt * L + (kt + 1) * 128])
                        end(ins)
                    between(i, 1)
                    if 0 <= i - 2 < n:
                        j = i - 2
                        b = begin(("O", name, j))
                        drained(pe, ("PT", name, j))
                        p0 = 0 if hd == 128 else 64 * (j % 2)
                        for kt in range(2):
                            ins = mm(b[p0:p0 + hd, 0:L], vt[:, kt, j * hd:(j + 1) * hd],
                                     ptb[:, j % 2, kt * L:(kt + 1) * L], kt == 0, kt == 1)
                        end(ins)

            def state_update(name, w2, n):
                pe.wait_ge(w_ready, n)
                for c in range(HC):
                    b = begin(("su", name, c))
                    end(mm(b[:, :], bd, w2[:, c, :, :].rearrange("p s v -> p (s v)")))

            def state_out(name, st, q, n):
                pe.wait_ge(sst_ready, 4 * n)
                b = begin(("sO", name))
                for c in range(HC):
                    for s in range(NS):
                        for p in range(2):
                            ps = slice(64 * p, 64 * p + 64)
                            ins = mm(b[ps, c * NS + s:c * NS + s + 1], st[ps, c, s, :], q[ps, c, L + s:L + s + 1])
                end(ins)

            pe.wait_ge(con_in, 16)
            norm(0)
            b = begin(("ab",))
            pe.wait_ge(vec_in, 16)
            for k in range(KC):
                hready(0)(k)
                ins = mm(b[0:40, 0:T], cols("w_ab", 40, 40 * k), h[:, k, :], k == 0, k == KC - 1)
            end(ins)
            for m in range(16):
                lin("ev_in_a", m, KC, 2, h, T)
                if m >= 8:
                    hn("l2", m - 8, T, bd)
            pe.wait_ge(gate_rows, 6)
            pe.wait_ge(con2_in, 16)
            for c in range(HC):
                for name, r, w in (("bcB", 0, T), ("bcG", 2, T), ("bcL", 3, L)):
                    b = begin((name, c))
                    end(mm(b[:, 0:w], cst("selc", i=c, p=8), gs[0:8, r, 0:w]))
            for t in range(NCH):
                drained(pe, ("bcL", HC - 1))
                transposes(("trk", t), [ke[:, c, t * 128:(t + 1) * 128] for c in range(HC)])
                transposes(("trv", t), [vb[:, c, t * 128:(t + 1) * 128] for c in range(HC)])
            kn = qkv[:, 4:8, :]
            for gi, (t, p) in enumerate(G4):
                ts, ps = slice(t * 128, (t + 1) * 128), slice(64 * p, 64 * p + 64)
                b = begin(("DT", (t, p)))
                for c in range(HC):
                    hh_, o = 2 * c + p, b[:, c * 128:(c + 1) * 128]
                    mm(o, cst("selh", i=hh_, p=8), gs[0:8, 4, ts], True, False)
                    mm(o, gs[0:8, 4, ts], cst("nselh", i=hh_, p=8), False, False)
                    ins = mm(o, ident, cst("neg"), False, True)
                end(ins)
                b = begin(("QK", (t, p)))
                for c in range(HC):
                    ins = mm(b[:, c * 128:(c + 1) * 128], kn[ps, c, ts], qkv[ps, c, ts])
                end(ins)
                b = begin(("KK", (t, p)))
                for c in range(HC):
                    ins = mm(b[:, c * 128:(c + 1) * 128], kn[ps, c, ts], kb[ps, c, ts])
                end(ins)

            def blk(v, gi, c):
                return v[:, gi, c * 128:(c + 1) * 128]

            for gi, g in enumerate(G4):
                pe.wait_ge(xt_ready, gi + 1)
                transposes(("X1", g), [blk(xt, gi, c) for c in range(HC)])
            for l in range(1, LEV):
                for gi, g in enumerate(G4):
                    n = (l - 1) * 4 + gi
                    b = begin(("T1", l, g))
                    pe.wait_ge(ml_ready, n + 1)
                    drained(pe, ("X1", g) if l == 1 else ("Z", l - 1, g))
                    for c in range(HC):
                        ins = mm(b[:, c * 128:(c + 1) * 128], blk(ml, n % 2, c), blk(xx, gi, c))
                    end(ins)
                for gi, g in enumerate(G4):
                    b = begin(("ZT", l, g))
                    drained(pe, ("T1", l, g))
                    if l > 1:
                        drained(pe, ("ZT", l - 1, g))
                    for c in range(HC):
                        ins = mm(b[:, c * 128:(c + 1) * 128], blk(t1, gi, c), blk(xt, gi, c))
                    end(ins)
                    if l < LEV - 1:
                        b = begin(("Z", l, g))
                        for c in range(HC):
                            ins = mm(b[:, c * 128:(c + 1) * 128], blk(xt, gi, c), blk(t1, gi, c))
                        end(ins)
            for g in G4:
                drained(pe, ("ZT", LEV - 1, g))
            for t in range(NCH):
                ts = slice(t * 128, (t + 1) * 128)
                if t:
                    drained(pe, ("S", "gdn", t - 1))
                    for p in range(2):
                        ps = slice(64 * p, 64 * p + 64)
                        b = begin(("ks", p))
                        for c in range(HC):
                            ins = mm(b[:, c * 64:(c + 1) * 64], bk[ps, c, ts], sg[ps, c, :])
                        end(ins)
                    drained(pe, ("ks", 1))
                b = begin(("u", t))
                for hh_ in range(H):
                    cs = slice(hh_ * 64, (hh_ + 1) * 64)
                    ins = mm(b[:, cs], blk(xt, 2 * t + hh_ % 2, hh_ // 2), (rhst if t else vbtok[:, 0, :])[:, cs])
                end(ins)
                drained(pe, ("u", t))
                for p in range(2):
                    ps = slice(64 * p, 64 * p + 64)
                    b = begin(("o", t, p))
                    for c in range(HC):
                        hh_, o = 2 * c + p, b[ps, c * 128:(c + 1) * 128]
                        if t:
                            mm(o, sg[ps, c, :], qe[ps, c, ts], True, False)
                        ins = mm(o, utok[:, hh_ * 64:(hh_ + 1) * 64], blk(qkd, 2 * t + p, c), t == 0, True)
                    end(ins)
                b = begin(("S", "gdn", t))
                for hh_ in range(H):
                    ps, cs = slice(64 * (hh_ % 2), 64 * (hh_ % 2) + 64), slice(hh_ * 64, (hh_ + 1) * 64)
                    ins = mm(b[ps, (hh_ // 2) * 64:(hh_ // 2 + 1) * 64], ketok[:, t, cs], utok[:, cs])
                end(ins)
            for m in range(4):
                lin("ev_in_b", m, KC, 2, h, T)
            state_update("gdn", ws2, 2)
            for m in range(4, 8):
                lin("ev_in_b", m, KC, 2, h, T)
            state_out("gdn", sgs, qkv, 1)
            for m in range(8, 16):
                lin("ev_in_b", m, KC, 2, h, T)
                if m >= 12:
                    hn("gdn", m - 12, T, bd)
            pe.wait_ge(hg_dve, 2)
            pe.wait_ge(hg_pool, 3)
            for t in range(NCH):
                ts = slice(t * 128, (t + 1) * 128)
                transposes(("htk", t), [ko[:, c, ts] for c in range(HC)])
                drained(pe, ("lin", "ev_in_b", 11))
                transposes(("htv", t), [zi[:, c, ts] for c in range(HC)])
            for t, p in G4:
                ts, ps = slice(t * 128, (t + 1) * 128), slice(64 * p, 64 * p + 64)
                b = begin(("att", (t, p)))
                for c in range(HC):
                    ins = mm(b[:, c * 128:(c + 1) * 128], kx[ps, c, ts], qx[ps, c, ts])
                end(ins)
            for t in range(NCH):
                drained(pe, ("htk", t))
                drained(pe, ("htv", t))
            for k in range(L // HCK):
                t, r = k // 4, k % 4
                rs_ = slice(32 * r, 32 * r + 32)
                b = begin(("kv", k))
                for hh_ in range(H):
                    ps, cs = slice(64 * (hh_ % 2), 64 * (hh_ % 2) + 64), slice(hh_ * 64, (hh_ + 1) * 64)
                    ins = mm(b[ps, (hh_ // 2) * 64:(hh_ // 2 + 1) * 64], hkt[rs_, t, cs], hvt[rs_, t, cs])
                end(ins)
            for gi, (t, p) in enumerate(G4):
                drained(pe, ("kv", 4 * t + 2))
                ps = slice(64 * p, 64 * p + 64)
                b = begin(("ho", (t, p)))
                drained(pe, ("att", (t, p)))
                for c in range(HC):
                    hh_ = 2 * c + p
                    ins = mm(b[ps, c * 128:(c + 1) * 128], hvt[:, t, hh_ * 64:(hh_ + 1) * 64],
                             blk(attb, gi, c), True, False)
                    for r in range(4):
                        k = 4 * t + r
                        if k:
                            ins = mm(b[ps, c * 128 + 32 * r:c * 128 + 32 * r + 32], SH[k][ps, c, :],
                                     qin[ps, c, 32 * k:32 * k + 32], False, r == 3)
                end(ins)
            state_update("hgrn", hws2, 3)
            state_out("hgrn", shs, zq, 2)
            for c in range(HC):
                hn("hgrn", c, T, bd)
            for m in range(KC):
                if m == 4:
                    norm(norms.index(("memkv", 0)))
                lin("ev_out", m, KC, 2, mix, T, lambda k: pe.wait_ge(mix_ready, k + 1))

            def memory(l):
                i = norms.index(("memkv", l))
                for m in range(MH):
                    lin(f"memk{l}", m, KC, 2, mh, NM, hready(i))
                norm(i + 1)
                for m in range(MH):
                    lin(f"memv{l}", m, KC, 2, mh, NM)
                    hn(f"memk{l}", m, NM, ones)
                for t in range(2):
                    drained(pe, ("lin", f"memv{l}", MH - 1))
                    transposes(("mvt", l, t), [mv[:, hh_, t * 128:(t + 1) * 128] for hh_ in range(MH)])
                for m in range(MH):
                    lin(f"wq{l}", m, KC, 2, h, T, hready(i + 1))
                    if m:
                        hn(f"memq{l}", m - 1, T, ones)
                hn(f"memq{l}", MH - 1, T, ones)
                pe.wait_ge(hn_done, hn_no[(f"memq{l}", MH - 1)] + 1)
                for t in range(2):
                    drained(pe, ("mvt", l, t))
                name = f"mem{l}"

                def keys(i, part):
                    if part or i >= 4:
                        return
                    key = ("sc", name, i // 2)
                    b = open_(key) if i % 2 == 0 else bank(key)
                    if i == 0:
                        pe.wait_ge(qz_ready, QZN[name] + 1)
                    r = slot(f"ck{l}", i)
                    for s in (2 * i, 2 * i + 1):
                        j = s % 4
                        for hh_ in range(MH):
                            o = (s % 2) * 1024 + hh_ * 256
                            ins = mm(b[32 * j:32 * j + 32, 0:NM], mqz[:, hh_, s, :], r[:, o:o + NM],
                                     hh_ == 0, hh_ == MH - 1)
                    slot_done(ins, f"ck{l}", i)
                attend(name, MH, 128, mq, mk, mvt, keys)
                b = begin(("pt", name, 0))
                for g in range(2):
                    drained(pe, ("sc", name, g))
                    for t in range(2):
                        ins = tr(b[:, (2 * g + t) * 128:(2 * g + t + 1) * 128], mpm[:, g, 128 * t:128 * t + 128])
                end(ins)
                drained(pe, ("pt", name, 0))
                for i in range(4):
                    key = ("so", name, i // 2)
                    b = open_(key) if i % 2 == 0 else bank(key)
                    r = slot(f"cv{l}", i)
                    for s in (2 * i, 2 * i + 1):
                        j = s % 4
                        for t in range(2):
                            o = (s % 2) * 1024 + t * 512
                            ins = mm(b[32 * j:32 * j + MH, :], mps[:, 2 * (s // 4) + t, j, :], r[:, o:o + 512],
                                     t == 0, t == 1)
                    slot_done(ins, f"cv{l}", i)
                b = begin(("sx", name))
                for g in range(2):
                    drained(pe, ("so", name, g))
                pe.wait_ge(sel_ready, SELN[name])
                for c in range(MH):
                    for g in range(2):
                        ins = mm(b[:, 8 * c + 4 * g:8 * c + 4 * g + 4], mos[:, g, 128 * c:128 * c + 128],
                                 msel[:, g, 4 * c:4 * c + 4])
                end(ins)
                for hh_ in range(MH):
                    drained(pe, ("O", f"mem{l}", hh_))
                drained(pe, ("sx", name))
                for m in range(KC):
                    lin(f"wo{l}", m, MH, 4, mix, T)

            def ffn(l):
                i = norms.index(("ffn", l))
                norm(i)
                for m in range(2 * FT):
                    lin3(f"gu{l}", m, KC, 2, mix_r, h_r, lambda k: pe.wait_ge(xl_ready, KC * l + k + 1))
                for m in range(KC):
                    lin3(f"down{l}", m, FT, 1, act_hi, act_lo, lambda k: pe.wait_ge(al_ready, FT * l + k + 1))

            memory(0)
            ffn(0)
            norm(norms.index(("mix", 1)))
            for m in range(16):
                if m == 8:
                    b = begin(("bx",))
                    pe.wait_ge(relb_ready, 2)
                    end(mm(b[0:8, :], relb[0:33, :], cst("hotx", 512, p=33)))
                lin("od_in", m, KC, 2, h, T, hready(norms.index(("mix", 1))))
                if m >= 8:
                    hn("moba", m - 8, T, bd)
            for m in range(8, 12):
                drained(pe, ("lin", "od_in", m))
            for t in range(2):
                transposes(("vt", t), [zo[:, 8 + c, t * 128:(t + 1) * 128] for c in range(HC)])
            for i in range(2):
                b = begin(("bs", i))
                o = CON["hots"] + 512 * i
                end(mm(b[:, :], relr, con[0:32, o:o + 512]))
            pe.wait_ge(hn_done, hn_no[("moba", 7)] + 1)
            for t in range(2):
                drained(pe, ("vt", t))

            def pages(i, part):
                if (i, part) == (2, 0):
                    b = begin(("self",))
                    pe.wait_ge(qk_ready, 1)
                    for g in range(2):
                        for c in range(HC):
                            ins = mm(b[:, g:g + 1], kz[:, c, 4 * g:4 * g + 4, :].rearrange("p s h -> p (s h)"),
                                     ones[:, 0:1], c == 0, c == HC - 1)
                    end(ins)
                if i >= H or part:
                    return
                if i == 0:
                    pe.wait_ge(qz_ready, QZN["moba"] + 1)
                pair = (2 * i, 2 * i + 1)
                key = ("sc", "moba", i // 2)
                b = open_(key) if i % 2 == 0 else bank(key)
                r = [slot("pk", n)[:, 0:2048].rearrange("p (g c t) -> p g c t", g=4, c=HC) for n in pair]
                for c in range(HC):
                    for n in pair:
                        s_, j = 4 * (n // 8) + n % 4, n % 4
                        ins = mm(b[32 * j:32 * j + 32, :], qz[:, c, s_, :], r[n % 2][:, :, c, :],
                                 c == 0, c == HC - 1)
                        if c == HC - 1:
                            slot_done(ins, "pk", n)
            attend("moba", H, 64, zo[:, 0:4, :], zo[:, 4:8, :], ovt, pages)
            pe.wait_ge(s5_in, 48)
            for c in range(HC):
                drained(pe, ("lin", "od_in", 12 + c))

            def y_tile(c):
                b = begin(("s5y", c))
                if c == 0:
                    pe.wait_ge(s5_hs, 2)
                for j in range(4):
                    n = 4 * c + j
                    o = b[32 * j:32 * j + 32, 0:L]
                    pe.wait_ge(s5_hr, n + 1)
                    pe.wait_ge(s5_hi, 2 * n + 1)
                    mm(o, s5cp[:, 0, n, :], HH[n % NHB][:, 0, :], True, False)
                    mm(o, s5cp[:, 1, n, :], HH[n % NHB][:, 1, :], False, True)
                    o = b[32 * j:32 * j + 32, L:T]
                    mm(o, s5c[:, 0, n, :], hsS[:, 0, n, :], True, False)
                    ins = mm(o, s5cp[:, 2, n, :], hsS[:, 1, n, :], False, True)
                end(ins)

            def x_tile(n):
                c, js = n // 4, slice(32 * (n % 4), 32 * (n % 4) + 32)
                b = begin(("s5x", n))
                for q in range(2):
                    ins = mm(b[:, q * L:(q + 1) * L], s5b[js, q, c, :], zo[js, 12 + c, 0:L])
                end(ins)

            x_tile(0)
            x_tile(1)
            for i in range(4):
                b = begin(("pt", "moba", i))
                pe.wait_ge(pp_ready, i + 1)
                for n in range(4):
                    ins = tr(b[:, 128 * n:128 * n + 128],
                             ssc[:, i // 2, 512 * (i % 2) + 128 * n:512 * (i % 2) + 128 * n + 128])
                end(ins)
            for i in range(4):
                drained(pe, ("pt", "moba", i))
            for n in range(0, NT, 2):
                key = ("so", "moba", n // 4)
                b = open_(key) if n % 4 == 0 else bank(key)
                half = n // 2 % 2
                r = [slot("pv", n + m) for m in range(2)]
                for g in range(4):
                    for m in range(2):
                        s_ = 2 * (n // 4) + m
                        j = s_ % 4
                        ins = mm(b[32 * j:32 * j + H, :], spt[:, 2 * (s_ // 4) + half, g, j, :],
                                 r[m][:, 512 * g:512 * g + 512], half == 0 and g == 0, half == 1 and g == 3)
                        if g == 3:
                            slot_done(ins, "pv", n + m)
                if n + 2 < NT:
                    x_tile(n + 2)
                    x_tile(n + 3)
                if n < 4:
                    for j in (n, n + 1):
                        b5, js = begin(("s5s", j)), slice(32 * j, 32 * j + 32)
                        for c in range(HC):
                            for q in range(2):
                                o = (c * 2 + q) * NS
                                ins = mm(b5[:, o:o + NS], s5b[js, q, c, :], zo[js, 12 + c, L:T])
                        end(ins)
                if n % 4 == 0 and n:
                    y_tile(n // 4 - 1)
            y_tile(3)
            b = begin(("sx", "moba"))
            for i in range(4):
                drained(pe, ("so", "moba", i))
            pe.wait_ge(sel_ready, SELN["moba"])
            for p in range(2):
                ps = slice(64 * p, 64 * p + 64)
                for c in range(HC):
                    for g in range(2):
                        hh_ = 2 * c + p
                        mm(b[ps, 8 * c + 4 * g:8 * c + 4 * g + 4], osm[:, g, 64 * hh_:64 * hh_ + 64],
                           sel2[:, 0, g, 4 * hh_:4 * hh_ + 4])
                ins = mm(b[ps, 32:64], ones[:, 0:64],
                         sel2[:, 1].rearrange("p g (c b j) -> p b c g j", c=HC, b=2)[:, p])
            end(ins)
            for m in range(8):
                lin("glu", m, HC, 4, ygl, T, lambda k: pe.wait_ge(s5_gl2, k + 1))
            for j in range(H):
                drained(pe, ("O", "moba", j))
            for c in range(HC):
                drained(pe, ("lin", "glu", 2 * c))
            drained(pe, ("sx", "moba"))
            for m in range(KC):
                if m == 4:
                    norm(norms.index(("memkv", 1)))
                lin("od_out", m, KC, 2, mix, T)
            memory(1)
            ffn(1)
            assert at[0] == len(order)

        @block.vector
        def _(dve):
            step = Steps(dve, dve_step)
            V = nc.vector

            def tt(out, a, b, op):
                return V.tensor_tensor(out, a, b, op)

            def stt(out, a, s, b, op0, op1):
                return V.scalar_tensor_tensor(out, a, s, b, op0, op1)

            def norm(i):
                kind, l = norms[i]
                w = NM if kind == "memkv" else T
                dst = mh if kind == "memkv" else h
                src = h if kind == "memkv" else x
                dve.wait_ge(r_ready, i + 1)
                for k in range(KC):
                    stt(dst[:, k, 0:w], src[:, k, 0:w], col(NORM_G[kind], KC * l + k), rs[:, 0:w],
                        ALU.mult, ALU.mult).then_inc(h_ready, 1)

            def residual(name, chunks=range(KC)):
                for m in chunks:
                    key = ("lin", name, m)
                    full(dve, key)
                    drain(tt(x[:, m, :], x[:, m, :], bank(key)[:, 0:T], ALU.add), key)

            def headnorm(name, n, w, src, gain, dst, after=None):
                base = hn_no[(name, 0)]
                for i in (range(n) if isinstance(n, int) else n):
                    dve.wait_ge(hr_ready, base + i + 1)
                    stt(dst(i), src(i), gain(i), hr[:, (base + i) % 2, 0:w], ALU.mult, ALU.mult).then_inc(hn_done, 1)
                    if after:
                        dve.wait_ge(hn_done, base + i + 1)
                        after(i)

            def attend(name, n, hd, scale, after):
                pbuf, _ = att_buf[name]

                def scores(i):
                    j = at_no[(name, i)]
                    key = ("S", name, i)
                    full(dve, key)
                    v = pbuf[:, i % 2, :].rearrange("p (q k) -> p q k", q=2)
                    sv = bank(key)[:, :].rearrange("p (q k) -> p q k", q=2)
                    if i >= 2:
                        full(dve, ("PT", name, i - 2))
                    if hd == 128:
                        drain(V.tensor_scalar(v, sv, scale, None, ALU.mult), key)
                    else:
                        bv = hank[:, i, 255:256]
                        bv = bass.AP(tensor=bv.tensor, offset=bv.offset, ap=[list(bv.ap[0]), [128, 2], [-1, L]])
                        drain(stt(v, sv, scale, bv, ALU.mult, ALU.add), key)
                    drained(dve, key)
                    step(V.tensor_reduce(smx[:, j % 2, 2, 0:2], v, AX, ALU.max))
                    V.tensor_scalar(smx[:, j % 2, 0, 0:2], smx[:, j % 2, 2, 0:2], -1.0, None,
                                    ALU.mult).then_inc(smax_ready, 1)

                def normalise(i):
                    j = at_no[(name, i)]
                    dve.wait_ge(p_exp, j + 1)
                    step(V.reciprocal(smx[:, j % 2, 3, 0:2], smx[:, j % 2, 1, 0:2]))
                    for qt in range(2):
                        v = pbuf[:, i % 2, qt * L:(qt + 1) * L]
                        ins = V.tensor_scalar(v, v, smx[:, j % 2, 3, qt:qt + 1], None, ALU.mult)
                    ins.then_inc(p_ready, 1)

                for i in range(n + 1):
                    if i < n:
                        scores(i)
                    if i >= 1:
                        normalise(i - 1)
                    after(i)

            dve.wait_ge(vec_in, 16)
            V.memset(epst[:, :], EPS).then_inc(eps_ready, 1)
            step(V.memset(onec[:, :], 1.0))
            step(V.tensor_copy(relb[0:32, :], cols("relb", H, 0, 0, 32)))
            V.memset(relb[32:33, :], BIG).then_inc(relb_ready, 1)
            lb = lambda i: cols("lb", 4, 4 * i)
            step(tt(lbt[:, 5, :], lb(0), lb(1), ALU.max))
            step(tt(lbt[:, 6, :], lbt[:, 5, :], lb(2), ALU.max))
            for i in range(3):
                ins = tt(lbt[:, i, :], lb(i), lbt[:, 6, :], ALU.subtract)
            ins.then_inc(lb_step, 1)
            dve.wait_ge(lb_step, 2)
            step(tt(lbt[:, 5, :], lbt[:, 0, :], lbt[:, 1, :], ALU.add))
            step(tt(lbt[:, 6, :], lbt[:, 5, :], lbt[:, 2, :], ALU.add))
            step(V.reciprocal(lbt[:, 7, :], lbt[:, 6, :]))
            step(tt(lbt[:, 3, :], lbt[:, 0, :], lbt[:, 7, :], ALU.mult))
            step(V.tensor_scalar(lbt[:, 4, :], lbt[:, 3, :], -1.0, 1.0, ALU.mult, ALU.add))
            dt0, lrd, th, k0, r_s, r_c = [par[:, i, :] for i in range(6)]
            lr, li = cols("s5_re", NT), cols("s5_im", NT)
            dve.wait_ge(s5_par, 1)
            step(tt(lrd, lr, dt0, ALU.mult))
            step(tt(th, li, dt0, ALU.mult))
            hi_, mid_ = 6.28125, 0.0019350051879882812
            lo_ = TWO_PI - hi_ - mid_
            for add, r in ((0.0, r_s), (0.25, r_c)):
                step(V.tensor_scalar(k0, th, 1.0 / TWO_PI, add, ALU.mult, ALU.add))
                step(V.tensor_scalar(k0, k0, MAGIC, None, ALU.add))
                step(V.tensor_scalar(k0, k0, -MAGIC, None, ALU.add))
                step(stt(r, k0, -hi_, th, ALU.mult, ALU.add))
                step(stt(r, k0, -mid_, r, ALU.mult, ALU.add))
                step(stt(r, k0, -lo_, r, ALU.mult, ALU.add))
                step(V.tensor_scalar(r, r, add * TWO_PI, 3.1415925, ALU.add, ALU.min))
                ins = V.tensor_scalar(r, r, -3.1415925, None, ALU.max)
                if add == 0.0:
                    step(ins)
            ins.then_inc(s5_par, 1)
            norm(0)
            dve.wait_ge(s5_par, 3)
            mag, sn, cs_ = par[:, 1, :], par[:, 4, :], par[:, 5, :]
            ar, ai, den, nr, cr, ci, q1, q2 = [par[:, i, :] for i in range(6, 14)]
            step(tt(ar, mag, cs_, ALU.mult))
            step(tt(ai, mag, sn, ALU.mult))
            step(tt(q1, lr, lr, ALU.mult))
            step(tt(q2, li, li, ALU.mult))
            step(tt(q1, q1, q2, ALU.add))
            step(V.reciprocal(den, q1))
            step(V.tensor_scalar(nr, ar, -1.0, None, ALU.add))
            for out, a, b, c, d, op in ((cr, nr, lr, ai, li, ALU.add), (ci, ai, lr, nr, li, ALU.subtract)):
                step(tt(q1, a, b, ALU.mult))
                step(tt(q2, c, d, ALU.mult))
                step(tt(q1, q1, q2, op))
                step(tt(out, q1, den, ALU.mult))
            full(dve, ("ab",))
            dve.wait_ge(gate_rows, 2)
            step(V.tensor_scalar(gs[0:8, 1, :], bank(("ab",))[32:40, 0:T], col("small", 0, 32, 40), None, ALU.add))
            step(V.tensor_scalar(gs[0:8, 2, :], gs[0:8, 1, :], -1.0, None, ALU.mult))
            step(tt(gs[0:8, 4, :], gs[0:8, 1, :], gs[0:8, 2, :], ALU.min))
            drain(V.tensor_scalar(gs[0:8, 0, :], gs[0:8, 0, :], 1.0, None, ALU.add), ("ab",))
            drained(dve, ("ab",))
            V.reciprocal(gs[0:8, 0, :], gs[0:8, 0, :]).then_inc(gate_rows, 1)
            dve.wait_ge(gate_rows, 4)
            step(stt(gs[0:8, 1, :], gs[0:8, 1, :], 0.0, gs[0:8, 4, :], ALU.max, ALU.add))
            step(V.tensor_scalar(gs[0:8, 1, :], gs[0:8, 1, :], aexp[0:8, 0:1], -1.0, ALU.mult, ALU.mult))
            for t in range(NCH):
                ts = slice(t * 128, (t + 1) * 128)
                step(V.tensor_tensor_scan(gs[0:8, 4, ts], cst("ones", p=8), gs[0:8, 1, ts], 0.0, ALU.mult, ALU.add))
                step(V.tensor_scalar(gs[0:8, 3, ts], gs[0:8, 4, ts], -1.0,
                                     gs[0:8, 4, (t + 1) * 128 - 1:(t + 1) * 128], ALU.mult, ALU.add))
            V.tensor_copy(gs[0:8, 4, L:T], gs[0:8, 1, L:T]).then_inc(gate_rows, 1)
            dve.wait_ge(pads_ready, 2)
            dve.wait_ge(hist_in, 16)
            cw = lambda k, m: col("conv_w", 12 * k + m)

            def l2norm(chunks):
                headnorm("l2", chunks, T, lambda i: qkv[:, i, :], lambda i: HD ** -0.5 if i < 4 else 1.0,
                         lambda i: qkv[:, i, :])
            for m in range(12):
                drained(dve, ("lin", "ev_in_a", m))
                o, os_ = qkv[:, m, 0:L], qkv[:, m, L:T]
                V.tensor_scalar(o, zqkv[:, m, 0:L], cw(0, m), None, ALU.mult)
                step(V.tensor_scalar(os_, ch[:, m, 0:8], cw(0, m), None, ALU.mult))
                for k in range(1, 4):
                    stt(o, zqkv[:, m, k:k + L], cw(k, m), o, ALU.mult, ALU.add)
                    v = ch[:, m, 8 * k:8 * k + 8] if k < 3 else zqkv[:, m, 3 + L:3 + T]
                    ins = stt(os_, v, cw(k, m), os_, ALU.mult, ALU.add)
                    if k < 3:
                        step(ins)
                ins.then_inc(conv_done, 1)
                if m >= 10:
                    l2norm((m - 10,))
            l2norm(range(2, 8))
            dve.wait_ge(silu_done, 12)
            dve.wait_ge(hn_done, 8)
            for c in range(HC):
                full(dve, ("bcL", c))
                B, G, E_ = bank(("bcB", c))[:, 0:T], bank(("bcG", c))[:, 0:T], bank(("bcL", c))[:, 0:L]
                tt(vb[:, c, :], qkv[:, 8 + c, :], B, ALU.mult)
                drain(tt(kb[:, c, :], qkv[:, 4 + c, :], B, ALU.mult), ("bcB", c))
                drained(dve, ("bcB", c))
                tt(bk[:, c, :], kb[:, c, :], G, ALU.mult)
                tt(qe[:, c, :], qkv[:, c, :], G, ALU.mult)
                drain(V.tensor_copy(egc[:, c, :], G[:, L - 1:T]), ("bcG", c))
                drain(tt(ke[:, c, :], qkv[:, 4 + c, 0:L], E_, ALU.mult), ("bcL", c))
            dve.wait_ge(con2_in, 16)
            dve.wait_ge(cvo_ready, 1)
            for gi, g in enumerate(G4):
                d = dt_[:, gi % 2, :]
                drained(dve, ("DT", g))
                full(dve, ("QK", g))
                drain(tt(qkd[:, gi, :], bank(("QK", g))[:, :], d, ALU.mult), ("QK", g))
                full(dve, ("KK", g))
                drain(tt(mt[:, gi, :], bank(("KK", g))[:, :], d, ALU.mult), ("KK", g))
                drained(dve, ("KK", g))
                m4 = mt[:, gi, :].rearrange("p (n k) -> p n k", n=4)
                x4 = xt[:, gi, :].rearrange("p (n k) -> p n k", n=4)
                step(stt(x4, m4, -1.0, four(cst("lev", i=0)), ALU.mult, ALU.mult))
                tt(x4, x4, four(ident), ALU.add).then_inc(xt_ready, 1)
            for l in range(1, LEV):
                for gi, g in enumerate(G4):
                    key = ("ZT", l, g)
                    last = l == LEV - 1
                    full(dve, key if last else ("Z", l, g))
                    drain(tt(xt[:, gi, :], xt[:, gi, :], bank(key)[:, :], ALU.subtract), key)
                    if not last:
                        key = ("Z", l, g)
                        drain(tt(xx[:, gi, :], xx[:, gi, :], bank(key)[:, :], ALU.subtract), key)
            full(dve, ("S", "gdn", 0))
            drain(V.tensor_copy(sg[:, :, :], bank(("S", "gdn", 0))[:, 0:256].rearrange("p (c v) -> p c v", c=HC)),
                  ("S", "gdn", 0))
            for p in range(2):
                full(dve, ("ks", p))
                ap = lambda v: v.rearrange("p (c b v) -> p c b v", c=HC, b=2)[:, :, p, :]
                drain(tt(ap(rhst), ap(vbtok[:, 1, :]), bank(("ks", p))[:, 0:256].rearrange("p (c v) -> p c v", c=HC),
                         ALU.subtract), ("ks", p))
            full(dve, ("S", "gdn", 1))
            for c in range(HC):
                ins = stt(sg[:, c, :], sg[:, c, :], egc[:, c, 0:1], bank(("S", "gdn", 1))[:, c * 64:(c + 1) * 64],
                          ALU.mult, ALU.add)
            drain(ins, ("S", "gdn", 1))

            bc4 = lambda v: v.unsqueeze(3).broadcast_to([128, HC, NS, HD])
            bc3 = lambda v: v.unsqueeze(2).broadcast_to([128, NS, HD])

            def state_update(name, w1, st, k, n):
                for c in range(HC):
                    key = ("su", name, c)
                    full(dve, key)
                    drain(tt(w1[:, c], bank(key)[:, :].rearrange("p (s v) -> p s v", s=NS), bc3(k[:, c, L:T]),
                             ALU.mult), key)
                dve.wait_ge(sdec_ready, n)
                for c in range(HC):
                    drained(dve, ("su", name, c))
                    tt(st[:, c], st[:, c], w1[:, c], ALU.add).then_inc(sst_ready, 1)

            dve.wait_ge(sgs_in, 16)
            tt(ws1, sgs, bc4(bk[:, :, L:T]), ALU.mult).then_inc(w_ready, 1)
            dve.wait_ge(w_ready, 1)
            step(tt(ws2, cst("i2", 64).unsqueeze(1).unsqueeze(1).broadcast_to([128, HC, NS, HD]),
                    bc4(vb[:, :, L:T]), ALU.mult))
            tt(ws2, ws2, ws1, ALU.subtract).then_inc(w_ready, 1)

            def gated(gate, at):
                def after(i):
                    tt(mix[:, at + i, :], tmp[:, i % 2, :], gate[:, i, :], ALU.mult).then_inc(mix_ready, 1)
                return after

            for c in range(HC):
                drained(dve, ("lin", "ev_in_b", c))
                V.tensor_scalar(zk[:, c, :], zk[:, c, :], lbt[:, 4, c:c + 1], None, ALU.mult)
                V.tensor_scalar(zf[:, c, :], zf[:, c, :], lbt[:, 4, c:c + 1], lbt[:, 3, c:c + 1],
                                ALU.mult, ALU.add).then_inc(fk_ready, 1)
            state_update("gdn", ws1, sgs, qkv[:, 4:8, :], 1)
            dve.wait_ge(lf_ready, 1)
            for c in range(HC):
                ins = V.tensor_tensor_scan(bcs[:, c, :], rmask, lf[:, c, :], 0.0, ALU.mult, ALU.add)
            step(ins)
            ch4 = lambda v: v.rearrange("p c (k i) -> p (c k) i", i=HCK)
            mid, end_ = (HCK - 1) // 2, HCK - 1
            b4 = ch4(bcs)
            tt(ch4(d1), b4, b4[:, :, mid:mid + 1].broadcast_to([128, 32, HCK]), ALU.subtract).then_inc(dec_ready, 1)
            tt(ch4(d2), b4[:, :, end_:end_ + 1].broadcast_to([128, 32, HCK]), b4, ALU.subtract).then_inc(dec_ready, 1)
            dve.wait_ge(exp_ready, 2)
            for m in range(HC, 2 * HC):
                drained(dve, ("lin", "ev_in_b", m))
            tt(qx, qx, zq[:, :, 0:L], ALU.mult).then_inc(hg_dve, 1)
            dve.wait_ge(fk_ready, HC)
            tt(kx, kx, zk[:, :, 0:L], ALU.mult).then_inc(hg_dve, 1)
            for m in range(12, 16):
                drained(dve, ("lin", "ev_in_a", m))
            headnorm("gdn", HC, T, lambda i: oT[:, i, :], lambda i: col("gdn_norm"), lambda i: tmp[:, i % 2, :],
                     gated(zg, 0))
            dve.wait_ge(att_zero, 1)
            for gi, g in enumerate(G4):
                full(dve, ("att", g))
                drain(V.copy_predicated(attb[:, gi, :].rearrange("p (n k) -> p n k", n=4),
                                        four(cst("cmask").bitcast(I32)),
                                        blocks(("att", g))), ("att", g))
            dve.wait_ge(hg_pool, 1)
            for k in range(8):
                key = ("kv", k)
                full(dve, key)
                kv = bank(key)[:, 0:256].rearrange("p (c v) -> p c v", c=HC)
                nxt = SH[(k + 1) % 8]
                if k:
                    drained(dve, ("kv", k - 1))
                    step(tt(nxt, SH[k], fl[:, :, k:k + 1].broadcast_to([128, HC, HD]), ALU.mult))
                    drain(tt(nxt, nxt, kv, ALU.add), key)
                else:
                    drain(V.tensor_copy(nxt, kv), key)
            state_update("hgrn", hws1, shs, zk, 2)
            headnorm("hgrn", HC, T, lambda i: oT[:, i, :], lambda i: col("hgrn_norm"), lambda i: tmp[:, i % 2, :],
                     gated(zh, 4))
            residual("ev_out", range(4))
            norm(norms.index(("memkv", 0)))
            residual("ev_out", range(4, KC))

            def memory(l):
                norm(norms.index(("mem", l)))
                headnorm(f"memk{l}", MH, NM, lambda i: mk[:, i, :], lambda i: col("mem_gk", l),
                         lambda i: mk[:, i, :])
                headnorm(f"memq{l}", MH, T, lambda i: mq[:, i, :], lambda i: col("mem_gq", l),
                         lambda i: mq[:, i, :])
                step(V.memset(mqz, 0.0))
                for hh_ in range(MH):
                    ins = V.tensor_copy(mqz[:, hh_, :, hh_], mq[:, hh_, L:T])
                ins.then_inc(qz_ready, 1)
                V.memset(mos, 0.0).then_inc(qz_ready, 1)
                name = f"mem{l}"

                def maxima(i):
                    if i in (2, 4):
                        g = i // 2 - 1
                        key = ("sc", name, g)
                        full(dve, key)
                        step(V.tensor_reduce(msm[:, g, 0:1], bank(key)[:, 0:NM], AX, ALU.max))
                        V.tensor_scalar(msm[:, g, 1:2], msm[:, g, 0:1], -128 ** -0.5, None,
                                        ALU.mult).then_inc(mx_ready, 1)
                attend(name, MH, 128, 128 ** -0.5, maxima)
                for g in range(2):
                    drained(dve, ("sc", name, g))
                step(V.reciprocal(msm[:, :, 3], msm[:, :, 2]))
                for g in range(2):
                    ins = V.tensor_scalar(msel[:, g, :], cst("sel", 4 * MH), msm[:, g, 3:4], None, ALU.mult)
                ins.then_inc(sel_ready, 1)
                full(dve, ("sx", name))
                drain(V.tensor_copy(mix[:, 0:4, L:T], bank(("sx", name))[:, 0:32].rearrange("p (h s) -> p h s", h=MH)),
                      ("sx", name))
                weights_low(l, 0)
                weights_low(l, 1)
                residual(f"wo{l}")

            def weights_low(l, n):
                k = FFN_SLOTS * l + n
                s_ = split_slots[k]
                w = slots[s_][3]
                dve.wait_ge(wh_ready, k + 1)
                tt(ring_r[:, s_ % SLOTS, 0:w], ring[:, s_ % SLOTS, 0:w], w_hi[:, k % 2, 0:w].bitcast(F32),
                   ALU.subtract).then_inc(wl_ready, 1)

            def ffn(l):
                norm(norms.index(("ffn", l)))
                for k in range(KC):
                    dve.wait_ge(xh_ready, KC * l + k + 1)
                    tt(h_r[:, k, :], h[:, k, :], mix_r[:, k, :].bitcast(F32), ALU.subtract).then_inc(xl_ready, 1)
                dve.wait_ge(mem_stored, 32 * (l + 1))
                dve.wait_ge(fh_in, 16 * (l + 1))
                fw = lambda k, i: col("ffn_w", (l * 3 + k) * FT + i)
                for i in range(FT + 1):
                    if 1 <= i < FT:
                        weights_low(l, i + 1)
                    if i < FT:
                        g, c = gb[:, i % 3, :], cacc[:, i % 2, :]
                        drained(dve, ("lin", f"gu{l}", 2 * i))
                        if i >= 2:
                            dve.wait_ge(fsilu_done, l * FT + i - 1)
                        fb = col("ffn_b", l * FT + i)
                        V.tensor_scalar(c[:, 0:L], g[:, 0:L], fw(0, i), fb, ALU.mult, ALU.add)
                        step(V.tensor_scalar(c[:, L:T], fh[:, i, 0:8], fw(0, i), fb, ALU.mult, ALU.add))
                        stt(c[:, 0:L], g[:, 1:1 + L], fw(1, i), c[:, 0:L], ALU.mult, ALU.add)
                        step(stt(c[:, L:T], fh[:, i, 8:16], fw(1, i), c[:, L:T], ALU.mult, ALU.add))
                        stt(c[:, 0:L], g[:, 2:2 + L], fw(2, i), c[:, 0:L], ALU.mult, ALU.add)
                        stt(c[:, L:T], g[:, 2 + L:2 + T], fw(2, i), c[:, L:T], ALU.mult,
                            ALU.add).then_inc(fconv_done, 1)
                    if 1 <= i <= FT:
                        j = i - 1
                        key = ("lin", f"gu{l}", 2 * j + 1)
                        full(dve, key)
                        dve.wait_ge(fsilu_done, l * FT + j + 1)
                        drain(tt(act_[:, j, :], csil[:, j % 2, :], bank(key)[:, 0:T], ALU.mult), key)
                for m in range(KC):
                    if m < KC - 1:
                        weights_low(l, FT + m + 1)
                    residual(f"down{l}", (m,))

            memory(0)
            ffn(0)
            norm(norms.index(("mix", 1)))
            step(V.memset(relr, 0.0))
            V.tensor_copy(relr.rearrange("p (j h) -> p j h", j=4)[:, :, 0:H],
                          relb[0:32, :].unsqueeze(1).broadcast_to([32, 4, H])).then_inc(relb_ready, 1)
            ms = lambda v, c_: V.memset(v, c_)
            dve.wait_ge(ffn_stored, 16)
            ms(cosT[:, :, 0:1], 1.0)
            step(ms(sinT[:, :, 0:1], 0.0))
            c0, s0_, c1, s1_ = [t16[:, i, :] for i in range(4)]
            step(V.tensor_copy(c0, cs_))
            step(V.tensor_copy(s0_, sn))
            wt = lambda i, n: place(TABTMP + i * 2048, NT, n)[0]
            n = 1
            while n < L:
                bb = lambda v: v.unsqueeze(2).broadcast_to([128, NT, n])
                wa, wb, wc, wd = [wt(i, n) for i in range(4)]
                C_, S_ = cosT[:, :, 0:n], sinT[:, :, 0:n]
                tt(wa, C_, bb(c0), ALU.mult)
                tt(wb, S_, bb(s0_), ALU.mult)
                tt(wc, C_, bb(s0_), ALU.mult)
                step(tt(wd, S_, bb(c0), ALU.mult))
                tt(cosT[:, :, n:2 * n], wa, wb, ALU.subtract)
                step(tt(sinT[:, :, n:2 * n], wc, wd, ALU.add))
                n *= 2
                if n < L:
                    step(tt(c1, c0, c0, ALU.mult))
                    step(tt(q1, s0_, s0_, ALU.mult))
                    step(tt(s1_, c0, s0_, ALU.mult))
                    step(tt(c0, c1, q1, ALU.subtract))
                    step(V.tensor_scalar(s0_, s1_, 2.0, None, ALU.mult))
            headnorm("moba", 8, T, lambda i: zo[:, i, :],
                     lambda i: col("moba_gq") if i < 4 else col("moba_gk"), lambda i: zo[:, i, :])
            full(dve, ("lin", "od_in", 15))
            step(ms(qz, 0.0))
            dve.wait_ge(hn_done, hn_no[("moba", 7)] + 1)
            for c in range(HC):
                for p in range(2):
                    ps = slice(64 * p, 64 * p + 64)
                    ins = V.tensor_copy(qz[ps, c, :, 2 * c + p], zo[ps, c, L:T])
            ins.then_inc(qz_ready, 1)
            dve.wait_ge(qz_ready, QZN["moba"] + 1)
            for c in range(HC):
                ins = tt(kz[:, c], qz[:, c], zo[:, 4 + c, L:T].unsqueeze(2).broadcast_to([128, NS, 32]), ALU.mult)
            ins.then_inc(qk_ready, 1)
            vs = tmpf[:, 400:432].rearrange("p (c s) -> p c s", c=HC)
            V.tensor_copy(vs, zo[:, 8:12, L:T])
            for i in range(2):
                drained(dve, ("bs", i))
            dve.wait_ge(bias_in, 16)

            def s5_output_matrices():
                dve.wait_ge(s5_in, 48)
                full(dve, ("lin", "od_in", 15))
                cb = lambda v: v.unsqueeze(2).broadcast_to([128, NT, 32])
                w1_, w2_ = place(WTMP, NT, 32)[0], place(WTMP + 512, NT, 32)[0]
                step(tt(w1_, s5c[:, 0], cb(cr), ALU.mult))
                step(tt(w2_, s5c[:, 1], cb(ci), ALU.mult))
                step(tt(s5cp[:, 0], w1_, w2_, ALU.subtract))
                step(tt(w1_, s5c[:, 0], cb(ci), ALU.mult))
                step(tt(w2_, s5c[:, 1], cb(cr), ALU.mult))
                step(stt(s5cp[:, 1].rearrange("p a b -> p (a b)"), w1_.rearrange("p a b -> p (a b)"), -1.0,
                         w2_.rearrange("p a b -> p (a b)"), ALU.mult, ALU.subtract))
                step(V.tensor_scalar(s5cp[:, 2].rearrange("p a b -> p (a b)"), s5c[:, 1].rearrange("p a b -> p (a b)"),
                                     -1.0, None, ALU.mult))

            def own_score():
                full(dve, ("self",))
                drain(V.tensor_scalar(gs2[:, 2, :], bank(("self",))[:, 0:2], HD ** -0.5, col("relb0"), ALU.mult, ALU.add),
                      ("self",))

            def score_rows(i):
                if i == 3:
                    s5_output_matrices()
                if i == 2:
                    own_score()
                if i < 2 or i % 2:
                    return
                k = i // 2 - 1
                g, half = k // 2, k % 2
                key = ("sc", "moba", k)
                full(dve, key)
                dst = ssc[:, g, 512 * half:512 * half + 512]
                V.tensor_reduce(gsm[:, 0, 4 * g + 2 * half:4 * g + 2 * half + 2],
                                bank(key)[:, :].rearrange("p (b t) -> p b t", b=2), AX, ALU.add)
                drain(stt(dst, bank(key)[:, :], HD ** -0.5, bsp[:, half, :], ALU.mult, ALU.add), key)
                drained(dve, key)
                step(V.tensor_reduce(gsm[:, 1, 4 * g + 2 * half:4 * g + 2 * half + 2],
                                     dst.rearrange("p (b t) -> p b t", b=2), AX, ALU.max))
            attend("moba", H, 64, HD ** -0.5, score_rows)
            gv = gsm[:, 0, :].rearrange("p (g b) -> p g b", g=2)
            cnt = gsm[:, 2, :].rearrange("p (g b) -> p g b", g=2)
            cmp_ = gs2[:, 0, :]
            for b in range(4):
                first = True
                for b2 in range(4):
                    if b2 == b:
                        continue
                    op = ALU.is_ge if b2 < b else ALU.is_gt
                    if first:
                        step(tt(cnt[:, :, b], gv[:, :, b2], gv[:, :, b], op))
                    else:
                        step(tt(cmp_, gv[:, :, b2], gv[:, :, b], op))
                        step(tt(cnt[:, :, b], cnt[:, :, b], cmp_, ALU.add))
                    first = False
            step(V.tensor_scalar(gsm[:, 3, :], gsm[:, 2, :], 3.0, BIG, ALU.is_ge, ALU.mult))
            step(tt(gsm[:, 4, :], gsm[:, 1, :], gsm[:, 3, :], ALU.add))
            step(V.tensor_reduce(gs2[:, 1, :], gsm[:, 4, :].rearrange("p (g b) -> p g b", g=2), AX, ALU.max))
            step(tt(gs2[:, 5, :], gs2[:, 1, :], gs2[:, 2, :], ALU.max))
            step(V.tensor_scalar(gs2[:, 3, :], gs2[:, 5, :], -1.0, None, ALU.mult))
            for g in range(2):
                ins = V.tensor_scalar(gsm[:, 5, 4 * g:4 * g + 4], gsm[:, 3, 4 * g:4 * g + 4], gs2[:, 3, g:g + 1], None,
                                      ALU.add)
            ins.then_inc(mx_ready, 1)
            V.memset(osm, 0.0).then_inc(qz_ready, 1)
            dve.wait_ge(pp_ready, 5)
            step(V.tensor_reduce(gs2[:, 6, :], gsm[:, 6, :].rearrange("p (g b) -> p g b", g=2), AX, ALU.add))
            step(tt(gs2[:, 7, :], gs2[:, 6, :], gs2[:, 4, :], ALU.add))
            step(V.reciprocal(gs2[:, 8, :], gs2[:, 7, :]))
            for g in range(2):
                ins = V.tensor_scalar(sel2[:, 0, g, :], cst("sel", 4 * H), gs2[:, 8, g:g + 1], None, ALU.mult)
                ins = V.tensor_scalar(sel2[:, 1, g, :], cst("sel", 4 * H), gs2[:, 8, g:g + 1], gs2[:, 4, g:g + 1],
                                      ALU.mult, ALU.mult)
            ins.then_inc(sel_ready, 1)
            def sample_states():
                for j in range(4):
                    full(dve, ("s5s", j))
                    src = bank(("s5s", j))[:, 0:64].rearrange("p (c q s) -> p q c s", c=HC, q=2)
                    for q in range(2):
                        ins = V.tensor_copy(hsS[:, q].rearrange("p (c j) s -> p c j s", j=4)[:, :, j, :], src[:, q])
                    drain(ins, ("s5s", j))
                for j in range(4):
                    drained(dve, ("s5s", j))
                sb8 = lambda v: v.unsqueeze(2).broadcast_to([128, NT, NS])
                for q, (a, b, c, d, op) in enumerate(((ar, ai, cr, ci, ALU.subtract), (ai, ar, ci, cr, ALU.add))):
                    out = s5o[:, q, :, 1:9]
                    step(tt(w3, s5h[:, 0], sb8(a), ALU.mult))
                    step(tt(w4, s5h[:, 1], sb8(b), ALU.mult))
                    step(tt(w3, w3, w4, op))
                    step(tt(w4, hsS[:, 0], sb8(c), ALU.mult))
                    step(tt(w3, w3, w4, ALU.add))
                    step(tt(w4, hsS[:, 1], sb8(d), ALU.mult))
                    step(tt(out, w3, w4, op))
                for q in range(2):
                    V.tensor_copy(hsS[:, q], s5o[:, q, :, 1:9]).then_inc(s5_hs, 1)

            def y_out(c):
                key = ("s5y", c)
                full(dve, key)
                drain(stt(tmpy[:, c, :], zo[:, 12 + c, :], col("s5_d", c), bank(key)[:, 0:T], ALU.mult, ALU.add), key)

            for n in range(NT):
                key = ("s5x", n)
                b = n % 2
                full(dve, key)
                xv = bank(key)[:, :].rearrange("p (q t) -> p q t", q=2)
                tab = lambda v: v[:, n, :].unsqueeze(1).broadcast_to([128, 2, L])
                tt(ta[:, b], xv, tab(cosT), ALU.mult)
                drain(tt(tb[:, b], xv, tab(sinT), ALU.mult), key)
                drained(dve, key)
                tt(ta[:, b, 0, :], ta[:, b, 0, :], tb[:, b, 1, :], ALU.add)
                step(tt(ta[:, b, 1, :], ta[:, b, 1, :], tb[:, b, 0, :], ALU.subtract))
                if n >= 2:
                    dve.wait_ge(s5_hi, 2 * (n - 1))
                for q in range(2):
                    V.tensor_tensor_scan(gg[:, b, q, :], par[:, 1, n:n + 1].broadcast_to([128, L]), ta[:, b, q, :],
                                         0.0, ALU.mult, ALU.add).then_inc(s5_g, 1)
                dve.wait_ge(s5_g, 2 * (n + 1))
                tt(ta[:, b, 0, :], gg[:, b, 0, :], cosT[:, n, :], ALU.mult)
                step(tt(ta[:, b, 1, :], gg[:, b, 1, :], sinT[:, n, :], ALU.mult))
                if n == 4:
                    full(dve, ("pt", "moba", 3))
                if n >= NHB:
                    full(dve, ("s5y", (n - NHB) // 4))
                tt(HH[n % NHB][:, 0, :], ta[:, b, 0, :], ta[:, b, 1, :], ALU.subtract).then_inc(s5_hr, 1)
                dve.wait_ge(s5_hr, n + 1)
                ins = V.tensor_copy(hl[:, 0, n:n + 1], HH[n % NHB][:, 0, L - 1:L])
                if n == NT - 1:
                    step(ins)
                if n == 3:
                    sample_states()
                if n >= 6 and n % 4 == 2:
                    y_out((n - 6) // 4)
            y_out(3)
            full(dve, ("sx", "moba"))
            w = tmpf[:, 360:392].rearrange("p (c s) -> p c s", c=HC)
            b = bank(("sx", "moba"))
            ob, pb = [b[:, 32 * i:32 * i + 32].rearrange("p (c s) -> p c s", c=HC) for i in range(2)]
            step(tt(w, vs, pb, ALU.mult))
            drain(tt(mix[:, 0:4, L:T], w, ob, ALU.add), ("sx", "moba"))
            drained(dve, ("sx", "moba"))
            dve.wait_ge(s5_hi, 2 * NT)
            for q, (a, b, op) in enumerate(((cr, ci, ALU.subtract), (ci, cr, ALU.add))):
                step(tt(t16[:, 0, :], hl[:, 0, :], a, ALU.mult))
                step(tt(t16[:, 1, :], hl[:, 1, :], b, ALU.mult))
                ins = tt(s5o[:, q, :, 0], t16[:, 0, :], t16[:, 1, :], op)
                if q == 0:
                    step(ins)
            ins.then_inc(s5_hs, 1)
            for c in range(HC):
                key = ("lin", "glu", 2 * c)
                full(dve, key)
                drained(dve, ("lin", "glu", 2 * c + 1))
                drain(tt(mix[:, 4 + c, :], bank(key)[:, 0:T], tmp[:, c % 2, :], ALU.mult), key)
            residual("od_out", range(4))
            norm(norms.index(("memkv", 1)))
            residual("od_out", range(4, KC))
            memory(1)
            ffn(1)


_OUT = {"y": (128, KC, T), "o_gconv": (128, 12, 27), "o_gdn": (128, HC, HD), "o_sgs": (128, HC, NS, HD),
        "o_hgrn": (128, HC, HD), "o_shs": (128, HC, NS, HD), "o_k": (128, HC, T), "o_v": (128, HC, T),
        "o_s5": (128, 2, NT, 9), "o_memk": (2, 128, MH, NM), "o_memv": (2, 128, MH, NM), "o_ffn": (2, 128, FT, 18)}


def feats(a):
    n, f = a.shape
    return a.T.reshape(f // 128, 128, n).transpose(1, 0, 2)


def stream(w, per):
    k, m = w.shape
    a = w.reshape(k // 128, 128, m // 128, 128).transpose(2, 1, 0, 3)
    a = a.reshape(m // 128 // per, per, 128, k // 128, 128).transpose(0, 2, 1, 3, 4)
    return np.ascontiguousarray(a.reshape(m // 128 // per, 128, -1))


def layout(i):
    g = {k: np.asarray(v) for k, v in i.items()}
    a = {"con": constants()}
    a["x"] = feats(np.concatenate([g["x_prompt"][0], g["x_sample"][:, 0]], 0))
    a["memx"] = feats(g["mem_prompt"][0])
    vec = np.zeros((128, VECW), np.float32)

    def put(name, v, at=0):
        v = np.asarray(v)
        vec[:v.shape[0], VEC[name] + at:VEC[name] + at + v.shape[1]] = v

    for n in ("norm_mix", "norm_mem", "norm_memkv", "norm_ffn"):
        put(n, g[n].reshape(16, 128).T)
    put("mem_gq", g["mem_gq"].T)
    put("mem_gk", g["mem_gk"].T)
    put("ffn_w", g["ffn_conv_w"].reshape(6 * FT, 128).T)
    put("ffn_b", g["ffn_conv_b"].reshape(2 * FT, 128).T)
    put("conv_w", g["gdn_conv_w"][0].reshape(48, 128).T)
    for n in ("gdn_norm", "hgrn_norm", "moba_gq", "moba_gk"):
        put(n, np.concatenate([g[n][0], g[n][0]])[:, None])
    put("lb", g["hgrn_lb_raw"].reshape(12, 128).T)
    put("s5_re", g["s5_A_re"][0].reshape(NT, 128).T)
    put("s5_im", g["s5_A_im"][0].reshape(NT, 128).T)
    put("s5_dt", np.repeat(g["s5_log_dt"][0], 64).reshape(NT, 128).T)
    put("s5_d", g["s5_D"][0].reshape(4, 128).T)
    vec[32:40, VEC["small"]] = g["gdn_dt_bias"][0]
    vec[0:8, VEC["small"] + 1] = g["gdn_A_log"][0]
    put("relb", g["rel_bias"])
    for j in range(4):
        vec[32 * j:32 * j + H, VEC["relb0"]] = g["rel_bias"][0]
    w = g["ev_w_in"][0]
    z = 4 * 512
    for k in range(KC):
        vec[:, VEC["w_ab"] + 40 * k:VEC["w_ab"] + 40 * k + 8] = w[128 * k:128 * k + 128, z:z + 8]
        vec[:, VEC["w_ab"] + 40 * k + 32:VEC["w_ab"] + 40 * k + 40] = w[128 * k:128 * k + 128, z + 8:z + 16]
    a["vec"] = vec
    a["pages"] = g["page_table"].reshape(1, NS * PAGES)
    a["ev_in_a"] = stream(w[:, :z], 2)
    hq = w[:, z + 16:z + 528]
    a["ev_in_b"] = stream(np.concatenate([w[:, z + 528:z + 1040], hq, w[:, z + 1040:]], 1), 2)
    a["ev_out"] = stream(g["ev_w_out"][0], 2)
    a["od_in"] = stream(g["od_w_in"][0], 2)
    a["od_out"] = stream(g["od_w_out"][0], 2)
    glu = g["s5_glu_w"][0].reshape(512, 2, 4, 128).transpose(0, 2, 1, 3).reshape(512, 1024)
    a["glu"] = stream(glu, 4)
    for l in range(2):
        a[f"memk{l}"] = stream(g["mem_wkv"][l][:, :512], 2)
        a[f"memv{l}"] = stream(g["mem_wkv"][l][:, 512:], 2)
        a[f"wq{l}"] = stream(g["mem_wq"][l], 2)
        a[f"wo{l}"] = stream(g["mem_wo"][l], 4)
        gu = g["ffn_w_gu"][l].reshape(D, 2, FT, 128).transpose(0, 2, 1, 3).reshape(D, 2 * DFF)
        a[f"gu{l}"] = stream(gu, 2)
        a[f"down{l}"] = stream(g["ffn_w_down"][l], 1)
        k = g["cache_mem_k"][l]
        a[f"ck{l}"] = k.reshape(4, 2, NM, MH, 128).transpose(0, 4, 1, 3, 2).reshape(4, 128, 2048)
        v = g["cache_mem_v"][l]
        a[f"cv{l}"] = v.reshape(4, 2, 2, 128, 512).transpose(0, 3, 1, 2, 4).reshape(4, 128, 2048)
    a["gconv"] = g["state_gdn_conv"][0].reshape(NS, 3, 12, 128).transpose(3, 2, 1, 0).reshape(128, 12, 24)
    for n, k in (("sgs", "state_gdn"), ("shs", "state_hgrn")):
        a[n] = g[k][0].reshape(NS, HC, 2, 64, 64).transpose(2, 3, 1, 0, 4).reshape(128, HC, NS, HD)
    a["fh"] = g["state_ffn_conv"].reshape(2, NS, 2, FT, 128).transpose(0, 4, 3, 2, 1).reshape(2, 128, FT, 16)
    a["s5h"] = np.stack([g[k][0].reshape(NS, NT, 128).transpose(2, 1, 0) for k in ("state_s5_re", "state_s5_im")], 1)
    b = np.zeros((4, 2, 16, 2, 4, 2, 64), np.float32)
    c = np.zeros((2, 64, 2, NT, 2, 16), np.float32)
    for q in range(2):
        bq = g[("s5_B_re", "s5_B_im")[q]][0].reshape(4, 4, 2, 64, 16)
        cq = g[("s5_C_re", "s5_C_im")[q]][0].reshape(NT, 2, 16, 64)
        for e in range(2):
            b[:, e, :, q, :, e, :] = bq[:, :, e].transpose(1, 3, 0, 2)
            c[e, :, q, :, e, :] = cq[:, e].transpose(2, 0, 1)
    a["s5b"] = b.reshape(128, 2, 4, 128)
    a["s5c"] = c.reshape(128, 2, NT, 32)
    a["pool_k"] = g["cache_moba_k"][0].reshape(POOL_PAGES, 128, HC, 128).transpose(0, 3, 2, 1).reshape(
        POOL_PAGES, 128, 512)
    a["pool_v"] = g["cache_moba_v"][0].reshape(POOL_PAGES, 128, 512)
    return {k: np.ascontiguousarray(v) for k, v in a.items()}


def kernel(**inputs):
    import concourse.bacc as bacc
    from concourse.bass_utils import run_bass_kernel_spmd

    nc = bacc.Bacc("TRN2", target_bir_lowering=False, num_devices=1)
    arrays, A = {}, {}
    for name, a in layout(inputs).items():
        arrays[f"in_{name}"] = a
        A[name] = nc.dram_tensor(f"in_{name}", a.shape, mybir.dt.from_np(a.dtype), kind="ExternalInput").ap()
    for name, shape in _OUT.items():
        A[name] = nc.dram_tensor(f"out_{name}", shape, F32, kind="ExternalOutput").ap()
    A["bias_x"] = nc.dram_tensor("bias_x", (8, 512), F32, kind="Internal").ap()
    build(nc, A)
    r = run_bass_kernel_spmd(nc, [arrays], core_ids=[0]).results[0]
    o = {name: np.asarray(r[f"out_{name}"]) for name in _OUT}

    def rows(a):
        return a.transpose(2, 1, 0).reshape(a.shape[2], -1)

    y = rows(o["y"])
    gc = o["o_gconv"]
    k, v = rows(o["o_k"]), rows(o["o_v"])
    pst = lambda a: a.reshape(2, 64, HC, 64).transpose(2, 0, 1, 3).reshape(1, 1, H, 64, 64)
    sst = lambda a: a.reshape(2, 64, HC, NS, 64).transpose(3, 2, 0, 1, 4).reshape(1, NS, H, 64, 64)
    s5 = o["o_s5"].transpose(1, 3, 2, 0).reshape(2, 9, 32, 64)
    memo = lambda a: np.stack([rows(a[l]) for l in range(2)]).reshape(2, 1, NM, MH, 128)
    ff = o["o_ffn"]
    ffp = ff[..., 0:2].transpose(0, 3, 2, 1).reshape(2, 1, 2, DFF)
    ffs = ff[..., 2:18].reshape(2, 128, FT, 2, NS).transpose(0, 4, 3, 2, 1).reshape(2, NS, 2, DFF)
    out = (y[None, :L], y[L:, None], rows(gc[:, :, 0:3]).reshape(1, 1, 3, 1536), pst(o["o_gdn"]), pst(o["o_hgrn"]),
           k[:L].reshape(1, 1, L, H, HD), v[:L].reshape(1, 1, L, H, HD), s5[0:1, 0:1], s5[1:2, 0:1],
           memo(o["o_memk"]), memo(o["o_memv"]), ffp,
           gc[:, :, 3:].reshape(128, 12, 3, NS).transpose(3, 2, 1, 0).reshape(1, NS, 3, 1536),
           sst(o["o_sgs"]), sst(o["o_shs"]), k[L:].reshape(1, NS, 1, H, HD), v[L:].reshape(1, NS, 1, H, HD),
           s5[0:1, 1:], s5[1:2, 1:], ffs)
    return tuple(np.ascontiguousarray(a) for a in out)
```
